# Optimizing a Trainium2 kernel written in Bass

```python
import math
import jax, jax.numpy as jnp
from jax import lax
import numpy as np

D_MODEL = 1024
BATCH = 1
SEQ = 512
DEPTH = 2

GRID_W = 64
CTX_LEN = 256
HEAD_DIM = 64
BRANCH_WIDTH = D_MODEL // 2
N_BRANCH = 4
NA_HEADS = BRANCH_WIDTH // HEAD_DIM
NA_KR = 8
NA_KC = 16
SW_HEADS = BRANCH_WIDTH // HEAD_DIM
SW_KV_HEADS = 2
SW_WINDOW = 128
SW_BLOCK = 128
GLA_HEADS = 4
GLA_DK = BRANCH_WIDTH // 2
GLA_DV = BRANCH_WIDTH
GLA_RANK = 16
GLA_TAU = 16.0
GLA_CHUNK = 64
HY_WIDTH = BRANCH_WIDTH
HY_CONV = 3
HY_EMB = 33
HY_FFN = 64
HY_TARGET = 1e-2
HY_FAST_PCT = 0.3
HY_SLOW_PCT = 1.5
ROPE_BASE = 10000.0
EPS = 1e-6
NEG_INF = -1e30
F32 = jnp.float32

IN_WIDTHS = (
    BRANCH_WIDTH, BRANCH_WIDTH, BRANCH_WIDTH, BRANCH_WIDTH,
    BRANCH_WIDTH, SW_KV_HEADS * HEAD_DIM, SW_KV_HEADS * HEAD_DIM, BRANCH_WIDTH,
    GLA_DK, GLA_DK, GLA_DV, GLA_RANK, GLA_RANK, BRANCH_WIDTH,
    3 * HY_WIDTH, BRANCH_WIDTH,
    N_BRANCH * D_MODEL,
)
IN_TOTAL = sum(IN_WIDTHS)

kernel_name = "hybrid_dit_parallel_mixers"

def rmsnorm(x, w):
    xf = x.astype(F32)
    y = xf * lax.rsqrt(jnp.mean(xf * xf, axis=-1, keepdims=True) + EPS)
    return (y * w.astype(F32)).astype(x.dtype)

def split_cols(p):
    idx = [int(i) for i in np.cumsum(IN_WIDTHS)[:-1]]
    return jnp.split(p, idx, axis=-1)

def heads(x, n):
    b, t, _ = x.shape
    return x.reshape(b, t, n, -1).transpose(0, 2, 1, 3)

def merge_heads(x):
    b, h, t, d = x.shape
    return x.transpose(0, 2, 1, 3).reshape(b, t, h * d)

def softmax_f32(s):
    return jax.nn.softmax(s.astype(F32), axis=-1)

def axial_rope(length):
    t = jnp.arange(length, dtype=jnp.int32)
    row = (t // GRID_W).astype(F32)
    col = (t % GRID_W).astype(F32)
    n_freq = HEAD_DIM // 4
    inv = ROPE_BASE ** (-jnp.arange(n_freq, dtype=F32) / n_freq)
    ang = jnp.concatenate([row[:, None] * inv, col[:, None] * inv], axis=-1)
    return jnp.cos(ang), jnp.sin(ang)

def rope_2d(x, cos, sin):
    half = x.shape[-1] // 2
    x1, x2 = x[..., :half], x[..., half:]
    return jnp.concatenate([x1 * cos - x2 * sin, x1 * sin + x2 * cos], axis=-1).astype(x.dtype)

def ctx_attention(q, k, v, sink):
    b, hq, t, d = q.shape
    hkv = k.shape[1]
    g = hq // hkv
    qg = q.reshape(b, hkv, g, t, d)
    s = jnp.einsum('bkgqd,bkcd->bkgqc', qg, k).astype(F32) * (d ** -0.5)
    if sink is not None:
        s_sink = jnp.broadcast_to(sink.astype(F32).reshape(1, hkv, g, 1, 1), (b, hkv, g, t, 1))
        s = jnp.concatenate([s, s_sink], axis=-1)
    p = softmax_f32(s)[..., :k.shape[2]].astype(v.dtype)
    return jnp.einsum('bkgqc,bkcd->bkgqd', p, v).reshape(b, hq, t, d)

def natten_mixer(q_l, k_l, v_l, q_c, k_c, v_c, rpb, with_ctx_out):
    b, h, length, d = q_l.shape
    rows = length // GRID_W
    kr = min(NA_KR, rows)
    ncb = GRID_W // NA_KC
    kw = 2 * NA_KC
    scale = d ** -0.5
    qcol = np.arange(GRID_W).reshape(ncb, NA_KC)
    kc0 = np.clip(np.arange(ncb) * NA_KC - NA_KC // 2, 0, GRID_W - kw)
    kcol = kc0[:, None] + np.arange(kw)[None, :]
    cs = np.clip(qcol - NA_KC // 2, 0, GRID_W - NA_KC)
    colmask = (kcol[:, None, :] >= cs[..., None]) & (kcol[:, None, :] < cs[..., None] + NA_KC)
    dc_idx = np.clip(kcol[:, None, :] - qcol[..., None] + (NA_KC - 1), 0, 2 * NA_KC - 2)
    mask = jnp.asarray(np.broadcast_to(colmask[:, :, None, :], (ncb, NA_KC, kr, kw)).reshape(ncb, NA_KC, kr * kw))
    qg = q_l.reshape(b, h, rows, GRID_W, d)
    kg = k_l.reshape(b, h, rows, GRID_W, d)
    vg = v_l.reshape(b, h, rows, GRID_W, d)
    n_nb = kr * kw

    def row_block(r):
        rs = jnp.clip(r - kr // 2, 0, rows - kr)
        q_r = lax.dynamic_index_in_dim(qg, r, axis=2, keepdims=False).reshape(b, h, ncb, NA_KC, d)

        def gather(t):
            t_r = lax.dynamic_slice_in_dim(t, rs, kr, axis=2)
            t_b = t_r[:, :, :, kcol]
            return t_b.transpose(0, 1, 3, 2, 4, 5).reshape(b, h, ncb, n_nb, d)

        k_b, v_b = gather(kg), gather(vg)
        dr_idx = rs + jnp.arange(kr) - r + (NA_KR - 1)
        bias = rpb[:, dr_idx[None, None, :, None], dc_idx[:, :, None, :]].reshape(h, ncb, NA_KC, n_nb)
        s_nb = jnp.einsum('bhjqd,bhjkd->bhjqk', q_r, k_b).astype(F32) * scale + bias.astype(F32)
        s_nb = jnp.where(mask, s_nb, NEG_INF)
        s_cx = jnp.einsum('bhjqd,bhkd->bhjqk', q_r, k_c).astype(F32) * scale
        p = softmax_f32(jnp.concatenate([s_nb, s_cx], axis=-1)).astype(v_l.dtype)
        o = (jnp.einsum('bhjqk,bhjkd->bhjqd', p[..., :n_nb], v_b)
             + jnp.einsum('bhjqk,bhkd->bhjqd', p[..., n_nb:], v_c))
        return o.reshape(b, h, GRID_W, d)

    o = lax.map(row_block, jnp.arange(rows))
    o_l = o.transpose(1, 2, 0, 3, 4).reshape(b, h, length, d)
    o_c = ctx_attention(q_c, k_c, v_c, None) if with_ctx_out else None
    return o_c, o_l

def swa_mixer(q_l, k_l, v_l, q_c, k_c, v_c, sink, with_ctx_out):
    b, hq, length, d = q_l.shape
    hkv = k_l.shape[1]
    g = hq // hkv
    nb = length // SW_BLOCK
    kw = 3 * SW_BLOCK
    lc = k_c.shape[2]
    scale = d ** -0.5
    qb = q_l.reshape(b, hkv, g, nb, SW_BLOCK, d)

    def band(t):
        tp = jnp.pad(t, ((0, 0), (0, 0), (SW_BLOCK, SW_BLOCK), (0, 0))).reshape(b, hkv, nb + 2, SW_BLOCK, d)
        return jnp.concatenate([tp[:, :, :-2], tp[:, :, 1:-1], tp[:, :, 2:]], axis=3)

    k_w, v_w = band(k_l), band(v_l)
    qpos = jnp.arange(length).reshape(nb, SW_BLOCK)
    kpos = (jnp.arange(nb)[:, None] - 1) * SW_BLOCK + jnp.arange(kw)[None, :]
    mask = ((jnp.abs(qpos[:, :, None] - kpos[:, None, :]) <= SW_WINDOW)
            & (kpos[:, None, :] >= 0) & (kpos[:, None, :] < length))
    s_w = jnp.einsum('bkgnqd,bknwd->bkgnqw', qb, k_w).astype(F32) * scale
    s_w = jnp.where(mask, s_w, NEG_INF)
    s_c = jnp.einsum('bkgnqd,bkcd->bkgnqc', qb, k_c).astype(F32) * scale
    s_sink = jnp.broadcast_to(sink.astype(F32).reshape(1, hkv, g, 1, 1, 1), (b, hkv, g, nb, SW_BLOCK, 1))
    p = softmax_f32(jnp.concatenate([s_w, s_c, s_sink], axis=-1)).astype(v_l.dtype)
    o = (jnp.einsum('bkgnqw,bknwd->bkgnqd', p[..., :kw], v_w)
         + jnp.einsum('bkgnqc,bkcd->bkgnqd', p[..., kw:kw + lc], v_c))
    o_l = o.reshape(b, hq, length, d)
    o_c = ctx_attention(q_c, k_c, v_c, sink) if with_ctx_out else None
    return o_c, o_l

def gla_direction(q, k, v, log_a, s0, with_out):
    b, h, t, dk = k.shape
    dv = v.shape[-1]
    n = t // GLA_CHUNK
    kc = k.reshape(b, h, n, GLA_CHUNK, dk)
    vc = v.reshape(b, h, n, GLA_CHUNK, dv)
    cum = jnp.cumsum(log_a.reshape(b, h, n, GLA_CHUNK, dk), axis=3)
    cum_end = cum[:, :, :, -1:]
    kv = jnp.einsum('bhncd,bhnce->bhnde', kc * jnp.exp(cum_end - cum), vc)
    g = jnp.exp(cum_end[:, :, :, 0])

    def step(s, inp):
        g_n, kv_n = inp
        return g_n[..., None] * s + kv_n, s

    s_fin, s_prev = lax.scan(step, s0, (jnp.moveaxis(g, 2, 0), jnp.moveaxis(kv, 2, 0)))
    if not with_out:
        return None, s_fin
    qc = q.reshape(b, h, n, GLA_CHUNK, dk)
    qd = qc * jnp.exp(cum)
    kd = kc * jnp.exp(-cum)
    tril = jnp.tril(jnp.ones((GLA_CHUNK, GLA_CHUNK), dtype=bool))
    a = jnp.where(tril, jnp.einsum('bhnid,bhnjd->bhnij', qd, kd), 0.0)
    o = jnp.einsum('bhnij,bhnje->bhnie', a, vc) + jnp.einsum('bhnid,nbhde->bhnie', qd, s_prev)
    return o.reshape(b, h, t, dv), s_fin

def gla_mixer(q_l, k_l, v_l, laf_l, lab_l, q_c, k_c, v_c, laf_c, lab_c, norm_w, with_ctx_out):
    b, h, _, dk = k_l.shape
    dv = v_l.shape[-1]
    s0 = jnp.zeros((b, h, dk, dv), F32)
    flip = lambda t: t[:, :, ::-1]
    o_cf, s_cf = gla_direction(q_c, k_c, v_c, laf_c, s0, with_ctx_out)
    o_cb, s_cb = gla_direction(flip(q_c), flip(k_c), flip(v_c), flip(lab_c), s0, with_ctx_out)
    o_lf, _ = gla_direction(q_l, k_l, v_l, laf_l, s_cf, True)
    o_lb, _ = gla_direction(flip(q_l), flip(k_l), flip(v_l), flip(lab_l), s_cb, True)
    o_l = rmsnorm(o_lf + flip(o_lb), norm_w)
    o_c = rmsnorm(o_cf + flip(o_cb), norm_w) if with_ctx_out else None
    return o_c, o_l

def short_conv(u, w, bias):
    t = u.shape[1]
    pad = HY_CONV // 2
    up = jnp.pad(u, ((0, 0), (pad, HY_CONV - 1 - pad), (0, 0)))
    out = up[:, 0:t] * w[0]
    for i in range(1, HY_CONV):
        out = out + up[:, i:i + t] * w[i]
    return out + bias

def hyena_filter(t_len, w1, b1, w2, b2, w3, b3, freq, wout):
    t = jnp.linspace(0.0, 1.0, t_len, dtype=F32)[:, None]
    bands = (HY_EMB - 1) // 2
    w_ang = 2.0 * math.pi * jnp.arange(t_len, dtype=F32)[:, None] / t_len
    f = jnp.linspace(1e-4, bands - 1, bands, dtype=F32)[None, :]
    z = jnp.concatenate([t, jnp.cos(f * w_ang), -jnp.sin(f * w_ang)], axis=-1)
    fr = freq.astype(F32)
    hh = jnp.sin(fr * (z @ w1.astype(F32) + b1.astype(F32)))
    hh = jnp.sin(fr * (hh @ w2.astype(F32) + b2.astype(F32)))
    hh = jnp.sin(fr * (hh @ w3.astype(F32) + b3.astype(F32)))
    hh = hh @ wout.astype(F32)
    deltas = jnp.abs(jnp.linspace(math.log(HY_TARGET) / HY_SLOW_PCT, math.log(HY_TARGET) / HY_FAST_PCT,
                                  HY_WIDTH, dtype=F32))
    decay = jnp.exp(-t * deltas)
    h_f = hh[:, :HY_WIDTH] * decay
    h_b = hh[:, HY_WIDTH:] * decay
    l1 = jnp.sum(jnp.abs(h_f), axis=0) + jnp.sum(jnp.abs(h_b[1:]), axis=0)
    k2 = jnp.concatenate([h_f, jnp.zeros((1, HY_WIDTH), F32), h_b[:0:-1]], axis=0)
    return k2 / l1

def hyena_mixer(u_proj, conv_w, conv_b, w1, b1, w2, b2, w3, b3, freq, wout, filt_bias):
    t_len = u_proj.shape[1]
    u = short_conv(u_proj, conv_w, conv_b)
    x0, x1, v = jnp.split(u, 3, axis=-1)
    z = x1 * v
    k2 = hyena_filter(t_len, w1, b1, w2, b2, w3, b3, freq, wout)
    zf = jnp.fft.rfft(z.astype(F32), n=2 * t_len, axis=1)
    kf = jnp.fft.rfft(k2, axis=0)
    y = jnp.fft.irfft(zf * kf[None], n=2 * t_len, axis=1)[:, :t_len].astype(z.dtype)
    return x0 * (y + z * filt_bias)

def layer(xc, xl, c, c_ctx, cos, sin, norm_w, w_mod, b_mod, w_in, rpb, sink, w_alpha_up, b_alpha,
          gla_norm_w, conv_w, conv_b, filt_w1, filt_b1, filt_w2, filt_b2, filt_w3, filt_b3, filt_freq,
          filt_wout, filt_bias, w_branch, w_out, with_ctx_out):
    mod_l = jax.nn.silu(c) @ w_mod + b_mod
    mod_c = jax.nn.silu(c_ctx) @ w_mod + b_mod
    sh_l, sc_l, g_l = jnp.split(mod_l[:, None, :], 3, axis=-1)
    sh_c, sc_c, g_c = jnp.split(mod_c, 3, axis=-1)
    hl = rmsnorm(xl, norm_w) * (1.0 + sc_l) + sh_l
    hc = rmsnorm(xc, norm_w) * (1.0 + sc_c) + sh_c
    (qa_l, ka_l, va_l, ga_l, qb_l, kb_l, vb_l, gb_l, qg_l, kg_l, vg_l, lrf_l, lrb_l, gg_l,
     uh_l, gh_l, gm_l) = split_cols(hl @ w_in)
    (qa_c, ka_c, va_c, ga_c, qb_c, kb_c, vb_c, gb_c, qg_c, kg_c, vg_c, lrf_c, lrb_c, gg_c,
     uh_c, gh_c, gm_c) = split_cols(hc @ w_in)

    a_c, a_l = natten_mixer(heads(qa_l, NA_HEADS), heads(ka_l, NA_HEADS), heads(va_l, NA_HEADS),
                            heads(qa_c, NA_HEADS), heads(ka_c, NA_HEADS), heads(va_c, NA_HEADS),
                            rpb, with_ctx_out)
    b_c, b_l = swa_mixer(rope_2d(heads(qb_l, SW_HEADS), cos, sin), rope_2d(heads(kb_l, SW_KV_HEADS), cos, sin),
                         heads(vb_l, SW_KV_HEADS),
                         heads(qb_c, SW_HEADS), heads(kb_c, SW_KV_HEADS), heads(vb_c, SW_KV_HEADS),
                         sink, with_ctx_out)
    dk_h = GLA_DK // GLA_HEADS

    def log_decay(lr, direction):
        return heads(jax.nn.log_sigmoid((lr @ w_alpha_up[direction] + b_alpha[direction]).astype(F32)) / GLA_TAU,
                     GLA_HEADS)

    c_c, c_l = gla_mixer(heads(qg_l, GLA_HEADS) * dk_h ** -0.5, heads(kg_l, GLA_HEADS), heads(vg_l, GLA_HEADS),
                         log_decay(lrf_l, 0), log_decay(lrb_l, 1),
                         heads(qg_c, GLA_HEADS) * dk_h ** -0.5, heads(kg_c, GLA_HEADS), heads(vg_c, GLA_HEADS),
                         log_decay(lrf_c, 0), log_decay(lrb_c, 1), gla_norm_w, with_ctx_out)
    d_l = hyena_mixer(uh_l, conv_w, conv_b, filt_w1, filt_b1, filt_w2, filt_b2, filt_w3, filt_b3,
                      filt_freq, filt_wout, filt_bias)

    def merge(ys, gm):
        gates = jax.nn.sigmoid(gm.reshape(gm.shape[:-1] + (N_BRANCH, D_MODEL)))
        acc = gates[..., 0, :] * (ys[0] @ w_branch[0])
        for i in range(1, N_BRANCH):
            acc = acc + gates[..., i, :] * (ys[i] @ w_branch[i])
        return acc @ w_out

    ys_l = [merge_heads(a_l) * jax.nn.silu(ga_l), merge_heads(b_l) * jax.nn.silu(gb_l),
            merge_heads(c_l) * jax.nn.silu(gg_l), d_l * jax.nn.silu(gh_l)]
    xl_new = xl + g_l * merge(ys_l, gm_l)
    if with_ctx_out:
        d_c = hyena_mixer(uh_c, conv_w, conv_b, filt_w1, filt_b1, filt_w2, filt_b2, filt_w3, filt_b3,
                          filt_freq, filt_wout, filt_bias)
        ys_c = [merge_heads(a_c) * jax.nn.silu(ga_c), merge_heads(b_c) * jax.nn.silu(gb_c),
                merge_heads(c_c) * jax.nn.silu(gg_c), d_c * jax.nn.silu(gh_c)]
        xc = xc + g_c * merge(ys_c, gm_c)
    return xc, xl_new

def setup_inputs(seed: int = 0) -> dict:
    key = jax.random.key(seed)
    ks = jax.random.split(key, 28)
    nrm = lambda k, shape, scale: jax.random.normal(k, shape, jnp.float32) * scale
    d = D_MODEL
    return {
        "x": nrm(ks[0], (BATCH, SEQ, d), 1.0),
        "c": nrm(ks[1], (BATCH, d), 1.0),
        "ctx": nrm(ks[2], (BATCH, CTX_LEN, d), 1.0),
        "c_ctx": nrm(ks[3], (d,), 1.0),
        "norm_w": 1.0 + nrm(ks[4], (DEPTH, d), 0.02),
        "w_mod": nrm(ks[5], (DEPTH, d, 3 * d), d ** -0.5),
        "b_mod": nrm(ks[6], (DEPTH, 3 * d), 0.01),
        "w_in": nrm(ks[7], (DEPTH, d, IN_TOTAL), d ** -0.5),
        "rpb": nrm(ks[8], (DEPTH, NA_HEADS, 2 * NA_KR - 1, 2 * NA_KC - 1), 0.5),
        "sink": nrm(ks[9], (DEPTH, SW_HEADS), 0.5),
        "w_alpha_up": nrm(ks[10], (DEPTH, 2, GLA_RANK, GLA_DK), GLA_RANK ** -0.5),
        "b_alpha": nrm(ks[11], (DEPTH, 2, GLA_DK), 0.1),
        "gla_norm_w": 1.0 + nrm(ks[12], (DEPTH, GLA_DV // GLA_HEADS), 0.02),
        "conv_w": nrm(ks[13], (DEPTH, HY_CONV, 3 * HY_WIDTH), HY_CONV ** -0.5),
        "conv_b": nrm(ks[14], (DEPTH, 3 * HY_WIDTH), 0.01),
        "filt_w1": nrm(ks[15], (DEPTH, HY_EMB, HY_FFN), HY_EMB ** -0.5),
        "filt_b1": nrm(ks[16], (DEPTH, HY_FFN), 0.1),
        "filt_w2": nrm(ks[17], (DEPTH, HY_FFN, HY_FFN), HY_FFN ** -0.5),
        "filt_b2": nrm(ks[18], (DEPTH, HY_FFN), 0.1),
        "filt_w3": nrm(ks[19], (DEPTH, HY_FFN, HY_FFN), HY_FFN ** -0.5),
        "filt_b3": nrm(ks[20], (DEPTH, HY_FFN), 0.1),
        "filt_freq": 1.0 + nrm(ks[21], (DEPTH, HY_FFN), 0.02),
        "filt_wout": nrm(ks[22], (DEPTH, HY_FFN, 2 * HY_WIDTH), HY_FFN ** -0.5),
        "filt_bias": nrm(ks[23], (DEPTH, HY_WIDTH), 0.5),
        "w_branch": nrm(ks[24], (DEPTH, N_BRANCH, BRANCH_WIDTH, d), BRANCH_WIDTH ** -0.5),
        "w_out": nrm(ks[25], (DEPTH, d, d), d ** -0.5),
        "final_norm_w": 1.0 + nrm(ks[26], (d,), 0.02),
    }

def reference(x, c, ctx, c_ctx, norm_w, w_mod, b_mod, w_in, rpb, sink, w_alpha_up, b_alpha, gla_norm_w,
              conv_w, conv_b, filt_w1, filt_b1, filt_w2, filt_b2, filt_w3, filt_b3, filt_freq, filt_wout,
              filt_bias, w_branch, w_out, final_norm_w):
    cos, sin = axial_rope(x.shape[1])
    xc, xl = ctx, x
    for i in range(DEPTH):
        xc, xl = layer(xc, xl, c, c_ctx, cos, sin, norm_w[i], w_mod[i], b_mod[i], w_in[i], rpb[i], sink[i],
                       w_alpha_up[i], b_alpha[i], gla_norm_w[i], conv_w[i], conv_b[i], filt_w1[i], filt_b1[i],
                       filt_w2[i], filt_b2[i], filt_w3[i], filt_b3[i], filt_freq[i], filt_wout[i], filt_bias[i],
                       w_branch[i], w_out[i], with_ctx_out=(i < DEPTH - 1))
    return rmsnorm(xl, final_norm_w)


_drawn_inputs = setup_inputs


def setup_inputs(seed=0):
    import zlib

    import numpy as np

    out = dict(_drawn_inputs(seed))
    spreads = {}
    factors = {'b_mod': 2.842,
     'sink': 8.0,
     'b_alpha': 2.767,
     'gla_norm_w': 7.987,
     'conv_b': 22.799,
     'filt_freq': 8.0,
     'final_norm_w': 8.388,
     'rpb': 5.449}
    for name, (base, spread) in spreads.items():
        noise = np.random.default_rng([zlib.crc32(name.encode()), seed]).standard_normal(out[name].shape)
        drawn = base * np.exp(spread * noise) if base else spread * noise
        out[name] = __import__('jax').numpy.asarray(drawn.astype(out[name].dtype))
    for name, factor in factors.items():
        out[name] = (out[name] * factor).astype(out[name].dtype)
    return out
```

```python
import math
from contextlib import ExitStack

import numpy as np

import concourse.bass as bass
from concourse import mybir

F32 = mybir.dt.float32
BF16 = mybir.dt.bfloat16
I32 = mybir.dt.int32
ALU = mybir.AluOpType
ACT = mybir.ActivationFunctionType
AX = mybir.AxisListType.X

D_MODEL, SEQ, CTX, DEPTH = 1024, 512, 256, 2
T = SEQ + CTX
KT = D_MODEL // 128
HD = 64
HEADS = 8
GRID_W, NKR, NKC = 64, 8, 16
BW = 512
EPS = 1e-6
NEG = -1e30
SLOTS = 6
GROUP = 2048
ROUND = 1.5 * 2.0 ** 23
TWO_PI_HI = 6.28125
TWO_PI_LO = 2.0 * math.pi - TWO_PI_HI
PI_IN = 3.1415925

WIDTHS = (512, 512, 512, 512, 512, 128, 128, 512, 256, 256, 512, 16, 16, 512, 1536, 512, 4096)
STARTS = np.concatenate([[0], np.cumsum(WIDTHS)]).astype(int)
(QA, KA, VA, GA, QB, KB, VB, GB, QG, KG, VG, LRF, LRB, GG, UH, GH, GM) = STARTS[:-1]

TILES = {
    "D": [("u", i, UH + 128 * i, False) for i in range(12)] + [("gd", i, GH + 128 * i, False) for i in range(4)],
    "C": [("lr", 0, LRF, True)] + [("kg", i, KG + 128 * i, True) for i in range(2)]
         + [("qg", i, QG + 128 * i, False) for i in range(2)] + [("vg", i, VG + 128 * i, True) for i in range(4)]
         + [("gg", i, GG + 128 * i, False) for i in range(4)] + [None],
    "A": [("ka", i, KA + 128 * i, True) for i in range(4)] + [("va", i, VA + 128 * i, True) for i in range(4)]
         + [("qa", i, QA + 128 * i, False) for i in range(4)] + [("ga", i, GA + 128 * i, False) for i in range(4)],
    "B": [("kb", 0, KB, True), ("vb", 0, VB, True)] + [("qb", i, QB, False) for i in range(4)]
         + [("gb", i, GB + 128 * i, False) for i in range(4)],
}
MIXERS = ("D", "C", "A", "B")
BRANCH = {"A": 0, "B": 1, "C": 2, "D": 3}
MOD_TILES = 3 * KT
MOD_GROUPS = MOD_TILES // 2
PROJ_GROUPS = sum(len(t) for t in TILES.values()) // 2
MERGE_GROUPS = 3 * KT
OUT_GROUPS = KT // 2
LAYER_GROUPS = PROJ_GROUPS + MERGE_GROUPS + OUT_GROUPS
GROUPS = DEPTH * (MOD_GROUPS + LAYER_GROUPS)
NATTEN_COL0 = [min(max(j * NKC - NKC // 2, 0), GRID_W - 2 * NKC) for j in range(GRID_W // NKC)]

ARENA = 31744
Y_AT = {"D": 0, "C": 3072, "A": 6144, "B": 9216}
KSPEC, FWD, INV, FWD_C, INV_C = 3072, 7168, 11264, 15360, 16384
X_AT = 17408
HX0, HZ, HV = 17408, 20480, 23552
ZSPEC, HTMP = 26624, 30720
LR, GQ, GK, GV, GE, GS, GL, GAT, GO, GR = 6144, 6912, 8448, 9984, 13056, 17664, 20736, 23808, 26880, 28416
AQ, AK, AV, AVB, ABIAS, AP_, APT, AO = 9216, 12288, 15360, 18432, 22528, 26624, 27904, 29184
BQ, BK, BV, BROPE, BTMP = 12288, 15360, 16128, 16896, 17920
MACC, MGATE, MPROD = 23552, 12288, 13824
FZE, FH0, FH1, FT, FABS = INV, INV + 512, INV + 1024, INV + 1536, INV + 2048
FHF, FHB, FDEC = ZSPEC, ZSPEC + 2048, HV
FW, FWO = INV + 3072, HTMP

P_NORM, P_BMOD, P_CW, P_CB, P_FB, P_BA, P_GN, P_FREQ, P_B1, P_B2, P_B3, P_SINK, P_FIN, P_C, P_W = (
    0, 8, 32, 68, 80, 84, 88, 89, 90, 91, 92, 93, 101, 109, 125)


def build(nc, wstream, xT, params, zembT, filt_w, filt_wout, decay, dft, dft_c, idft, idft_c,
          bias, rope, rot, alpha_w, masks_f, masks_b, masks_u, x_mid, v_mid, out):
    with ExitStack() as ctx:
        def sb(name, shape, dt=F32):
            return ctx.enter_context(nc.sbuf_tensor(name, shape, dt))

        def sem(name):
            return ctx.enter_context(nc.semaphore(name))

        ar = sb("arena", [128, ARENA])
        h = sb("h", [128, KT, T])
        ring = sb("ring", [128, SLOTS, GROUP])
        const_f = sb("const_f", [128, 257])
        ones, ident = const_f[:, 0:128], const_f[:, 128:256]
        ident_b = sb("ident_b", [128, 128], BF16)
        bmask = sb("bmask", [128, 2, 128], BF16)
        cmask = sb("cmask", [128, 2, T], BF16)
        umask = sb("umask", [128, 2, 128], I32)
        alt = const_f[:, 256:257]
        rotm = sb("rotm", [128, 128])
        aw = sb("aw", [32, 512])
        par = sb("par", [128, P_W])
        csil = sb("csil", [128, 8, 2])
        mod = sb("mod", [128, DEPTH, MOD_TILES, 2])
        nscale = sb("nscale", [128, 8, 2])
        stat = sb("stat", [128, 2, 4, 8])
        rmx = sb("rmx", [128, 4])
        gend = sb("gend", [128, 2, 12])
        pf = ctx.enter_context(nc.psum_tensor("psum", [128, 8 * 512], F32))

        def at(off, *shape):
            n = int(np.prod(shape))
            v = ar[:, off:off + n]
            if len(shape) == 1:
                return v
            names = "abcd"[:len(shape)]
            return v.rearrange(f"p ({' '.join(names)}) -> p {' '.join(names)}",
                               **{k: s for k, s in zip(names, shape)})

        y = {b: at(Y_AT[b], 4, T) for b in MIXERS}
        slot_tile = ring[:, :, :].rearrange("p s (t k m) -> p s t k m", t=2, k=KT)
        slot_br = ring[:, :, :].rearrange("p s (b k m) -> p s b k m", b=4, k=4)

        ring_full = [sem(f"ring_full{s}") for s in range(SLOTS)]
        ring_turn = sem("ring_turn")
        const_in = sem("const_in")
        par_in = sem("par_in")
        par_free = sem("par_free")
        csil_ready = sem("csil_ready")
        mod_ready = sem("mod_ready")
        mod_done = sem("mod_done")
        x_in = sem("x_in")
        x_saved = sem("x_saved")
        tile_ready = sem("tile_ready")
        drained = [sem("drained0"), sem("drained1")]
        conv_ready = sem("conv_ready")
        dve_chain = sem("dve_chain")
        phase_done = sem("phase_done")
        filt_in = sem("filt_in")
        filt_pe = sem("filt_pe")
        filt_dve = sem("filt_dve")
        filt_act = sem("filt_act")
        norm_sq = sem("norm_sq")
        norm_ps = sem("norm_ps")
        norm_ms = sem("norm_ms")
        norm_rt = sem("norm_rt")
        h_ready = sem("h_ready")
        dft_in = sem("dft_in")
        hy_z = sem("hy_z")
        hy_tr = sem("hy_tr")
        hy_ztok = sem("hy_ztok")
        hy_spec = sem("hy_spec")
        hy_zs = sem("hy_zs")
        hy_prod = sem("hy_prod")
        hy_inv = sem("hy_inv")
        hy_out = sem("hy_out")
        gl_alpha = sem("gl_alpha")
        gl_z = sem("gl_z")
        gl_ln = sem("gl_ln")
        gl_cum = sem("gl_cum")
        gl_rest = sem("gl_rest")
        gl_exp = sem("gl_exp")
        gl_ke = sem("gl_ke")
        gl_tr = sem("gl_tr")
        gl_ket = sem("gl_ket")
        gl_kv = sem("gl_kv")
        gl_state = sem("gl_state")
        gl_qk = sem("gl_qk")
        gl_at = sem("gl_at")
        gl_atc = sem("gl_atc")
        gl_o = sem("gl_o")
        gl_sq = sem("gl_sq")
        gl_ss = sem("gl_ss")
        gl_ms = sem("gl_ms")
        gl_rt = sem("gl_rt")
        gl_fin = sem("gl_fin")
        vblk_in = sem("vblk_in")
        v_out = sem("v_out")
        bias_in = [sem("bias_in0"), sem("bias_in1")]
        rope_in = sem("rope_in")
        rope_rot = sem("rope_rot")
        rope_done = sem("rope_done")
        at_s = sem("at_s")
        at_max = sem("at_max")
        at_p = sem("at_p")
        at_pt = sem("at_pt")
        at_ptc = [sem("at_ptc0"), sem("at_ptc1")]
        at_o = sem("at_o")
        at_sum = sem("at_sum")
        at_sink = sem("at_sink")
        at_on = sem("at_on")
        at_ot = sem("at_ot")
        at_y = sem("at_y")
        mg_unit = sem("mg_unit")
        mg_gate = sem("mg_gate")
        mg_prod = sem("mg_prod")
        mg_sum = sem("mg_sum")
        res_done = sem("res_done")
        out_dma = sem("out_dma")
        fin_sq = sem("fin_sq")

        tile_no, n_tiles = {}, 0
        group_of, g = {}, 0
        mod_group, merge_group = [0] * DEPTH, [0] * DEPTH
        mod_group[0] = 0
        g = MOD_GROUPS
        for L in range(DEPTH):
            for b in MIXERS:
                for i, t in enumerate(TILES[b]):
                    if t is not None:
                        tile_no[L, t[0], t[1]] = n_tiles
                        group_of[L, t[0], t[1]] = (g + i // 2, i % 2)
                        n_tiles += 1
                g += len(TILES[b]) // 2
            if L + 1 < DEPTH:
                mod_group[L + 1] = g
                g += MOD_GROUPS
            merge_group[L] = g
            g += MERGE_GROUPS
            for m in range(KT):
                tile_no[L, "out", m] = n_tiles
                group_of[L, "out", m] = (g + m // 2, m % 2)
                n_tiles += 1
            g += OUT_GROUPS
        assert g == GROUPS

        def width(L, needed):
            return T if L < DEPTH - 1 or needed else SEQ

        def pair(t):
            return (t % 2) * 1024

        def wait_tile(eng, L, name, i):
            t = tile_no[L, name, i]
            eng.wait_ge(drained[t % 2], t // 2 + 1)

        phase_list = [(L, name) for L in range(DEPTH) for name in ("filter", "norm", "D", "Dc", "C", "A", "B", "merge")
                      if name != "Dc" or L < DEPTH - 1]

        def PH(L, name):
            return phase_list.index((L, name)) + 1

        def barrier(eng, n):
            eng.drain().then_inc(phase_done, 1)
            eng.wait_ge(phase_done, 4 * n)

        def units(mixer, L):
            nq = 4 + (2 if L < DEPTH - 1 else 0)
            return [(q, i, p) for q in range(nq) for i in range(4) for p in range(2)]

        def head(mixer, i, p):
            return 2 * i + p if mixer == "A" else i + 4 * p

        def key_blocks(mixer, q):
            if q >= 4:
                return [4, 5]
            if mixer == "A":
                return [-1, -1, 4, 5]
            return [n for n in (q - 1, q, q + 1) if 0 <= n < 4] + [4, 5]

        unit0, u = {}, 0
        qt0, qn = {}, 0
        for L in range(DEPTH):
            for b in ("A", "B"):
                unit0[L, b] = u
                qt0[L, b] = qn
                u += len(units(b, L))
                qn += len(units(b, L)) // 8

        hy_runs = [(0, False), (0, True), (1, False)]
        HYN = {False: dict(nt=4, t0=0, n=SEQ), True: dict(nt=2, t0=4, n=CTX)}
        HYT = [HYN[is_c]["nt"] for _, is_c in hy_runs]

        def FD(run):
            return sum(7 + 4 * nt for nt in HYT[:run])

        def FA(run):
            return sum(3 + 2 * nt for nt in HYT[:run])

        def FP(run):
            return sum(4 + 6 * nt for nt in HYT[:run])

        def HZS(run):
            return sum(2 * nt for nt in HYT[:run])

        def HPR(run):
            return sum(HYT[:run])

        def FIN(run):
            return 16 * (6, 10, 16)[run]

        def DIN(run):
            return 16 * (3, 3, 4)[run]

        def ZT(L):
            return 6 * L

        def QB(L):
            return 6 * L

        def MG(L):
            return 4 * KT * L

        def chunk_at(d, s):
            return 11 - s if d else (8 + s if s < 4 else s - 4)

        def state_slot(d, n):
            return 11 - n if d else (n + 4 if n < 8 else n - 8)

        block = ctx.enter_context(nc.Block())

        @block.sync
        def _(sp):
            for s in range(SLOTS):
                sp.dma_start(ring[:, s, :], wstream[s]).then_inc(ring_full[s], 16)
            with sp.Fori(1, GROUPS // SLOTS) as turn:
                for s in range(SLOTS):
                    sp.wait_ge(ring_turn, turn * SLOTS + (s + 2 - SLOTS))
                    sp.dma_start(ring[:, s, :], wstream[turn * SLOTS + s]).then_inc(ring_full[s], 16)
            for n in range(GROUPS - GROUPS % SLOTS, GROUPS):
                sp.wait_ge(ring_turn, n + 2 - SLOTS)
                sp.dma_start(ring[:, n % SLOTS, :], wstream[n]).then_inc(ring_full[n % SLOTS], 16)

        @block.gpsimd
        def _(pool):
            for dst, src in ((par[:, :], params[0]), (const_f[:, :], masks_f), (rotm[:, :], rot),
                             (ident_b[:, :], masks_b[:, 0:128]), (bmask[:, :, :], masks_b[:, 128:384].rearrange("p (a b) -> p a b", a=2)),
                             (cmask[:, :, :], masks_b[:, 384:384 + 2 * T].rearrange("p (a b) -> p a b", a=2)),
                             (umask[:, :, :], masks_u.rearrange("p (a b) -> p a b", a=2))):
                pool.dma_start(dst, src).then_inc(const_in, 16)
            for L in range(DEPTH):
                last = L == DEPTH - 1
                if L:
                    pool.dma_start(par[:, :], params[L]).then_inc(par_in, 16)
                pool.dma_start(at(FZE, 512)[0:33, :], zembT[:, 0:SEQ]).then_inc(filt_in, 16)
                pool.dma_start(at(FW, 192)[0:64, :], filt_w[L]).then_inc(filt_in, 16)
                pool.dma_start(at(FWO, 1024)[0:64, :], filt_wout[L]).then_inc(filt_in, 16)
                pool.dma_start(at(FDEC, 4, 512), decay[:, 0:4, :]).then_inc(filt_in, 16)
                pool.dma_start(at(FWD, 4, 1024), dft).then_inc(filt_in, 16)
                if L == 0:
                    pool.dma_start(at(X_AT, KT, T), xT).then_inc(x_in, 16)
                pool.dma_start(aw[:, :], alpha_w[L]).then_inc(filt_in, 16)
                if L:
                    pool.dma_start(x_mid, at(X_AT, KT, T)).then_inc(x_saved, 16)
                    pool.wait_ge(x_saved, 16)
                barrier(pool, PH(L, "filter"))
                pool.dma_start(at(INV, 8, 512), idft).then_inc(dft_in, 16)
                if not last:
                    pool.dma_start(at(FWD_C, 2, 512), dft_c).then_inc(dft_in, 16)
                    pool.dma_start(at(INV_C, 4, 256), idft_c).then_inc(dft_in, 16)
                barrier(pool, PH(L, "norm"))
                barrier(pool, PH(L, "D"))
                if not last:
                    pool.dma_start(at(FZE, 512)[0:33, 0:CTX], zembT[:, SEQ:T]).then_inc(filt_in, 16)
                    pool.dma_start(at(FW, 192)[0:64, :], filt_w[L]).then_inc(filt_in, 16)
                    pool.dma_start(at(FWO, 1024)[0:64, :], filt_wout[L]).then_inc(filt_in, 16)
                    pool.dma_start(at(FDEC, 4, 512)[:, 0:2, :], decay[:, 4:6, :]).then_inc(filt_in, 16)
                    barrier(pool, PH(L, "Dc"))
                barrier(pool, PH(L, "C"))
                for j in range(2):
                    pool.dma_start(at(ABIAS + 2048 * j, 8, 256), bias[L, j]).then_inc(bias_in[j], 16)
                for i in range(4):
                    wait_tile(pool, L, "va", i)
                pool.dma_start(v_mid[L].rearrange("(t p) c -> p t c", p=128), at(AV, 6, 512)[:, 0:4, :]).then_inc(v_out, 16)
                pool.wait_ge(v_out, 16 * (L + 1))
                rows = v_mid[L].rearrange("(r c) f -> r c f", c=GRID_W)
                for j, c0 in enumerate(NATTEN_COL0):
                    for k in range(2):
                        for r in range(4):
                            pool.dma_start(at(AVB, 4, 2, 512)[32 * r:32 * r + 32, j, k, :],
                                           rows[4 * k + r, c0:c0 + 32, :]).then_inc(vblk_in, 16)
                for j in range(2, 4):
                    pool.wait_ge(at_max, unit0[L, "A"] + 8 * (j - 1))
                    pool.dma_start(at(ABIAS + 2048 * (j % 2), 8, 256), bias[L, j]).then_inc(bias_in[j % 2], 16)
                barrier(pool, PH(L, "A"))
                pool.dma_start(at(BROPE, 2, 512), rope).then_inc(rope_in, 16)
                barrier(pool, PH(L, "B"))
                pool.dma_start(at(X_AT, KT, T), xT if L == 0 else x_mid).then_inc(x_in, 16)
                barrier(pool, PH(L, "merge"))
            for k in range(KT):
                pool.wait_ge(res_done, k + 1)
                pool.dma_start(out[128 * k:128 * k + 128, :], h[:, k, 0:SEQ]).then_inc(out_dma, 16)
            pool.wait_ge(out_dma, 16 * KT)

        @block.tensor
        def _(pe):
            def group_in(n):
                pe.wait_ge(ring_full[n % SLOTS], 16 * (n // SLOTS + 1))

            def modulation(L):
                if L == 0:
                    pe.wait_ge(csil_ready, 1)
                g0 = mod_group[L]
                with pe.Fori(0, MOD_GROUPS // SLOTS) as it:
                    for d in range(SLOTS):
                        s = (g0 + d) % SLOTS
                        pe.wait_ge(ring_full[s], 16 * it + 16 * ((g0 + d) // SLOTS + 1))
                        for t in range(2):
                            for k in range(KT):
                                mm = pe.matmul(pf[:, bass.ds(4 * SLOTS * it + (2048 + 4 * d + 2 * t), 2)], slot_tile[:, s, t, k, :], csil[:, k, :],
                                               start=(k == 0), stop=(k == KT - 1))
                                if t == 0 and k == 0:
                                    mm.then_inc(ring_turn, 1)
                        mm.then_inc(mod_ready, 1)

            def project(L, mixer):
                for ti in TILES[mixer]:
                    if ti is None:
                        continue
                    what, i, _, need = ti
                    t = tile_no[L, what, i]
                    n, half = group_of[L, what, i]
                    turn = half == 0 and (what, i) != ("gb", 2)
                    if half == 0:
                        group_in(n)
                    if t >= 2:
                        pe.wait_ge(drained[t % 2], t // 2)
                    w = slot_tile[:, n % SLOTS, half, :, :]
                    if what in ("va", "vb", "vg"):
                        for tt in range(6):
                            for k in range(KT):
                                mm = pe.matmul(pf[:, pair(t) + 128 * tt:pair(t) + 128 * tt + 128],
                                               h[:, k, 128 * tt:128 * tt + 128], w[:, k, :],
                                               start=(k == 0), stop=(k == KT - 1))
                                if turn and tt == 0 and k == 0:
                                    mm.then_inc(ring_turn, 1)
                    else:
                        m = 32 if what == "lr" else 128
                        for c0, c1 in ((0, SEQ), (SEQ, width(L, need))):
                            if c1 == c0:
                                continue
                            for k in range(KT):
                                mm = pe.matmul(pf[0:m, pair(t) + c0:pair(t) + c1], w[:, k, 0:m], h[:, k, c0:c1],
                                               start=(k == 0), stop=(k == KT - 1))
                                if turn and c0 == 0 and k == 0:
                                    mm.then_inc(ring_turn, 1)
                    mm.then_inc(tile_ready, 1)

            def filter_net(c, run):
                nt, n = c["nt"], c["n"]
                base_d, base_a = FD(run), FA(run)
                pe.wait_ge(filt_in, FIN(run))
                if nt == 2:
                    pe.wait_ge(dft_in, DIN(run))
                ze, w123 = at(FZE, 512), at(FW, 3, 64)
                for k in range(3):
                    src = (ze[0:33, 0:n], at(FH0, 512)[0:64, 0:n], at(FH1, 512)[0:64, 0:n])[k]
                    w = w123[0:33, 0, :] if k == 0 else w123[0:64, k, :]
                    if k:
                        pe.wait_ge(filt_act, base_a + k)
                    pe.matmul(pf[0:64, 0:n], w, src, start=True, stop=True).then_inc(filt_pe, 1)
                pe.wait_ge(filt_act, base_a + 3)
                h3, wo = at(FH0, 512)[0:64, :], at(FWO, 1024)[0:64, :]
                for j in range(2 * nt):
                    if j >= 2:
                        pe.wait_ge(filt_dve, base_d + 3 + j - 1)
                    pe.matmul(pf[:, 512 * (1 + j % 2):512 * (2 + j % 2)], h3[:, 128 * (j // 2):128 * (j // 2) + 128],
                              wo[:, 512 * (j % 2):512 * (j % 2) + 512], start=True, stop=True).then_inc(filt_pe, 1)
                for j in range(2 * nt):
                    pe.wait_ge(filt_act, base_a + 3 + j + 1)
                    mm = pe.matmul(pf[:, 1536:2048], ones[:, :], at(FABS + 512 * (j % 2), 512),
                                   start=(j == 0), stop=(j == 2 * nt - 1), skip_group_check=True)
                    mm.then_inc(filt_pe, 1)
                pe.wait_ge(filt_dve, base_d + 3 + 2 * nt + 2)
                fwd = at(FWD, 4, 1024) if nt == 4 else at(FWD_C, 2, 512)
                hs, hd = at(FDEC, 4, 512), at(FHB, 4, 512)
                for j in range(2 * nt):
                    if j >= 2:
                        pe.wait_ge(filt_dve, base_d + 3 + 2 * nt + 3 + j - 1)
                    src = hs if j < nt else hd
                    for t in range(nt):
                        mm = pe.matmul(pf[:, 512 * (4 + j % 2):512 * (5 + j % 2)], fwd[:, t, 128 * j:128 * j + 128],
                                       src[:, t, :], start=(t == 0), stop=(t == nt - 1))
                    mm.then_inc(filt_pe, 1)
                for t in range(nt):
                    mm = pe.matmul(pf[0:1, 0:512], alt[:, :], hs[:, t, :], start=(t == 0), stop=(t == nt - 1))
                mm.then_inc(filt_pe, 1)

            def norm(L):
                for k in range(KT):
                    pe.wait_ge(norm_sq, KT * L + k + 1)
                    mm = pe.matmul(pf[:, 0:SEQ], ones[:, :], h[:, k, 0:SEQ], start=(k == 0), stop=(k == KT - 1))
                    mm = pe.matmul(pf[:, SEQ:T], ones[:, :], h[:, k, SEQ:T], start=(k == 0), stop=(k == KT - 1))
                mm.then_inc(norm_ps, 1)

            def hyena(run):
                L, is_c = hy_runs[run]
                c = HYN[is_c]
                nt, n, t0 = c["nt"], c["n"], c["t0"]
                z, zt = at(HZ, 4, T), at(HV, 6, 512)
                zs = at(ZSPEC, 8, 512)
                fwd = at(FWD, 4, 1024) if nt == 4 else at(FWD_C, 2, 512)
                inv = at(INV, 8, 512) if nt == 4 else at(INV_C, 4, 256)
                if not is_c:
                    for j in range(6 if L < DEPTH - 1 else 4):
                        pe.wait_ge(hy_z, 4 * L + 4)
                        if j >= 2:
                            pe.wait_ge(hy_ztok, ZT(L) + j - 1)
                        for cc in range(4):
                            mm = pe.transpose(pf[:, 512 * (4 + j % 2) + 128 * cc:512 * (4 + j % 2) + 128 * cc + 128],
                                              z[:, cc, 128 * j:128 * j + 128], ident[:, :])
                        mm.then_inc(hy_tr, 1)
                    pe.wait_ge(hy_ztok, ZT(L) + (6 if L < DEPTH - 1 else 4))
                for j in range(2 * nt):
                    if j >= 2:
                        pe.wait_ge(hy_zs, HZS(run) + j - 1)
                    for t in range(nt):
                        mm = pe.matmul(pf[:, 512 * (6 + j % 2):512 * (7 + j % 2)], fwd[:, t, 128 * j:128 * j + 128],
                                       zt[:, t0 + t, :], start=(t == 0), stop=(t == nt - 1))
                    mm.then_inc(hy_spec, 1)
                pe.wait_ge(hy_prod, HPR(run) + nt)
                pe.wait_ge(dft_in, DIN(run))
                for cc in range(4):
                    if cc >= 2:
                        pe.wait_ge(hy_out, 4 * run + cc - 1)
                    for j in range(2 * nt):
                        mm = pe.matmul(pf[:, 512 * (4 + cc % 2):512 * (4 + cc % 2) + n], zs[:, j, 128 * cc:128 * cc + 128],
                                       inv[:, j, :], start=(j == 0), stop=(j == 2 * nt - 1))
                    mm.then_inc(hy_inv, 1)

            def gla(L):
                oc = width(L, False)
                nto = oc // 128
                q, k, v = at(GQ, 2, T), at(GK, 2, T), at(GV, 6, 512)
                lr = at(LR, T)
                E = at(GE, 2, 3, T)
                S = at(GS, 2, 12, 128)
                A = at(GAT, 2, 2, T)
                wait_tile(pe, L, "gg", 3)
                wait_tile(pe, L, "gg", 2)
                for hp in range(2):
                    N = 2 * L + hp
                    if N:
                        pe.wait_ge(gl_fin, 2 * N)
                    for d in range(2):
                        c0 = 128 * (2 * d + hp)
                        pe.matmul(pf[:, 1024 * d:1024 * d + SEQ], aw[:, c0:c0 + 128], lr[0:32, 0:SEQ], start=True, stop=True)
                        pe.matmul(pf[:, 1024 * d + SEQ:1024 * d + T], aw[:, c0:c0 + 128], lr[0:32, SEQ:T],
                                  start=True, stop=True).then_inc(gl_alpha, 1)
                    for d in range(2):
                        pe.wait_ge(gl_ke, 2 * N + d + 1)
                        for tt in range(6):
                            mm = pe.transpose(pf[:, 1024 * d + 128 * tt:1024 * d + 128 * tt + 128],
                                              E[:, d, 2, 128 * tt:128 * tt + 128], ident[:, :])
                        mm.then_inc(gl_tr, 1)
                    pe.wait_ge(gl_ket, 2 * N + 2)
                    for d in range(2):
                        ket = E[:, d, 2, :].rearrange("p (t f) -> p t f", t=6)
                        base = 2048 if d == 0 else 0
                        for p in range(2):
                            for tt in range(6):
                                for e in range(2):
                                    rows = slice(64 * p, 64 * p + 64)
                                    mm = pe.matmul(pf[64 * e:64 * e + 64, base + 1024 * p + 128 * tt:base + 1024 * p + 128 * tt + 128],
                                                   ket[rows, tt, 64 * e:64 * e + 64],
                                                   v[rows, tt, 128 * (2 * hp + e):128 * (2 * hp + e) + 128],
                                                   start=True, stop=True)
                        mm.then_inc(gl_kv, 1)
                    for e in range(2):
                        rows = slice(64 * e, 64 * e + 64)
                        for d in range(2):
                            pe.wait_ge(gl_state, 2 * N + e + 1)
                            pe.wait_ge(gl_qk, 2 * N + d + 1)
                            base = (2048 if e == 0 else 0) + 1024 * d
                            for tt in range(nto):
                                mm = pe.matmul(pf[:, base + 128 * tt:base + 128 * tt + 128],
                                               E[rows, d, 1, 128 * tt:128 * tt + 128], E[rows, d, 0, 128 * tt:128 * tt + 128],
                                               start=True, stop=True)
                            mm.then_inc(gl_at, 1)
                    for e in range(2):
                        rows = slice(64 * e, 64 * e + 64)
                        base = 2048 if e == 0 else 0
                        vc = slice(128 * (2 * hp + e), 128 * (2 * hp + e) + 128)
                        pe.wait_ge(gl_atc, 4 * N + 2 * e + 2)
                        pe.wait_ge(gl_state, 2 * N + 2)
                        for tt in range(nto):
                            o = pf[:, base + 128 * tt:base + 128 * tt + 128]
                            pe.matmul(o, v[:, tt, vc], A[:, e, 0, 128 * tt:128 * tt + 128], start=True, stop=False)
                            pe.matmul(o, v[:, tt, vc], A[:, e, 1, 128 * tt:128 * tt + 128], start=False, stop=False)
                            for p in range(2):
                                for d in range(2):
                                    mm = pe.matmul(o[:, 64 * p:64 * p + 64], S[rows, d, state_slot(d, 2 * tt + p), :],
                                                   E[rows, d, 0, 128 * tt + 64 * p:128 * tt + 64 * p + 64],
                                                   start=False, stop=(p == 1 and d == 1))
                        mm.then_inc(gl_o, 1)
                    for e in range(2):
                        base = (2048 if e == 0 else 0) + 1024
                        pe.wait_ge(gl_sq, 2 * N + e + 1)
                        sq = at(GL, 2, T)[:, e, :]
                        for c0, c1 in ((0, SEQ), (SEQ, oc)):
                            if c1 > c0:
                                mm = pe.matmul(pf[:, base + c0:base + c1], ones[:, :], sq[:, c0:c1], start=True, stop=True)
                        mm.then_inc(gl_ss, 1)

            def rotary(L):
                for i in range(5):
                    wait_tile(pe, L, *(("qb", i) if i < 4 else ("kb", 0)))
                    if i >= 2:
                        pe.wait_ge(rope_done, 5 * L + i - 1)
                    src = at(BQ, 4, T)[:, i, 0:SEQ] if i < 4 else at(BK, T)[:, 0:SEQ]
                    pe.matmul(pf[:, 512 * (4 + i % 2):512 * (5 + i % 2)], rotm[:, :], src, start=True, stop=True)\
                        .then_inc(rope_rot, 1)

            def attention(L, mixer):
                A = mixer == "A"
                q_, k_ = (at(AQ, 4, T), at(AK, 4, T)) if A else (at(BQ, 4, T), at(BK, 1, T))
                v_ = at(AV, 6, 512) if A else at(BV, 6, 128)
                pt_at = APT if A else BTMP + 1280
                us = units(mixer, L)
                u0 = unit0[L, mixer]
                wait_tile(pe, L, "ga" if A else "gb", 3)
                wait_tile(pe, L, "ga" if A else "gb", 2)
                if not A:
                    pe.wait_ge(rope_done, 5 * (L + 1))

                def scores(n):
                    q, i, p = us[n]
                    rows = slice(64 * p, 64 * p + 64)
                    base = 1024 * p
                    if n >= 2:
                        pe.wait_ge(at_p, u0 + n - 1)
                    lhs = q_[rows, i, 128 * q:128 * q + 128]
                    ki = i if A else 0
                    blocks = key_blocks(mixer, q)
                    if A and q < 4:
                        c0 = NATTEN_COL0[q]
                        pe.matmul(pf[:, base:base + 256].rearrange("p (r c) -> p r c", c=2 * NKC), lhs,
                                  k_[rows, ki, 0:SEQ].rearrange("p (r c) -> p r c", c=GRID_W)[:, :, c0:c0 + 32],
                                  start=True, stop=True)
                        mm = pe.matmul(pf[:, base + 256:base + 512], lhs, k_[rows, ki, SEQ:T], start=True, stop=True)
                    elif q >= 4:
                        mm = pe.matmul(pf[:, base:base + 256], lhs, k_[rows, ki, SEQ:T], start=True, stop=True)
                    else:
                        for c, b in enumerate(blocks):
                            edge = b < 4 and b != q
                            mm = pe.matmul(pf[:, base + 128 * c:base + 128 * c + 128], lhs,
                                           k_[rows, ki, 128 * b:128 * b + 128], start=True, stop=not edge)
                            if edge:
                                mm = pe.matmul(pf[:, base + 128 * c:base + 128 * c + 128], ident_b[:, :],
                                               bmask[:, 0 if b < q else 1, :], start=False, stop=True)
                    mm.then_inc(at_s, 1)

                def transposes(n):
                    q, i, p = us[n]
                    P = at((AP_ if A else BTMP) + 640 * p, 640)
                    pe.wait_ge(at_p, u0 + n + 1)
                    if n >= 2:
                        pe.wait_ge(at_ptc[p], (u0 + n) // 2)
                    nb = len(key_blocks(mixer, q))
                    for c in range(min(nb, 4)):
                        mm = pe.transpose(pf[:, 2048 + 512 * p + 128 * c:2048 + 512 * p + 128 * c + 128],
                                          P[:, 128 * c:128 * c + 128], ident[:, :])
                    if nb == 5:
                        pe.wait_ge(at_ptc[1 - p], (u0 + n + 1) // 2)
                        mm = pe.transpose(pf[:, 3072:3200], P[:, 512:640], ident[:, :])
                    mm.then_inc(at_pt, 1)

                def values(n):
                    q, i, p = us[n]
                    hh = head(mixer, i, p)
                    PT = at(pt_at + 640 * p, 5, 128)
                    pe.wait_ge(at_ptc[p], (u0 + n) // 2 + 1)
                    if n == 0 and A:
                        pe.wait_ge(vblk_in, 16 * 32 * (L + 1))
                    if i == 0 and p == 0 and (n or (L, mixer) != (0, "A")):
                        pe.wait_ge(at_on, qt0[L, mixer] + q)
                    blocks = key_blocks(mixer, q)
                    for c, b in enumerate(blocks):
                        if A:
                            rhs = at(AVB, 4, 2, 512)[:, q, c, 64 * hh:64 * hh + 64] if b < 0 else v_[:, b, 64 * hh:64 * hh + 64]
                        else:
                            rhs = v_[:, b, 64 * p:64 * p + 64]
                        mm = pe.matmul(pf[:, 3584 + 64 * hh:3584 + 64 * hh + 64], PT[:, c, :], rhs,
                                       start=(c == 0), stop=(c == len(blocks) - 1))
                    mm.then_inc(at_o, 1)

                def turn(q):
                    pe.wait_ge(at_on, qt0[L, mixer] + q + 1)
                    o = at(AO if A else BTMP + 2560, 512)
                    for f in range(4):
                        mm = pe.transpose(pf[:, 3072 + 128 * f:3072 + 128 * f + 128], o[:, 128 * f:128 * f + 128], ident[:, :])
                    mm.then_inc(at_ot, 1)

                scores(0)
                scores(1)
                for n in range(0, len(us), 2):
                    q = us[n][0]
                    transposes(n)
                    if n + 2 < len(us):
                        scores(n + 2)
                    transposes(n + 1)
                    if n + 3 < len(us):
                        scores(n + 3)
                    values(n)
                    values(n + 1)
                    if n % 8 == 6:
                        turn(q)
                        pe.wait_ge(at_y, qt0[L, mixer] + q + 1)

            def merge(L):
                g0 = merge_group[L]
                last = L == DEPTH - 1
                with pe.Fori(0, KT // 2) as it:
                    for mi in range(2):
                        for bi in range(4):
                            v = 4 * mi + bi
                            gg = g0 + 3 * mi
                            sg, sbr = (gg + 2 * (bi // 2)) % SLOTS, (gg + 1) % SLOTS
                            if bi % 2 == 0:
                                pe.wait_ge(ring_full[sg], 16 * it + 16 * ((gg + 2 * (bi // 2)) // SLOTS + 1))
                            pe.wait_ge(mg_prod, 8 * it + (MG(L) + v + 1))
                            for c0, c1 in ((0, SEQ), (SEQ, T)):
                                if last and c0:
                                    continue
                                for k in range(KT):
                                    mm = pe.matmul(pf[:, 2048 * (v % 2) + c0:2048 * (v % 2) + c1],
                                                   slot_tile[:, sg, bi % 2, k, :], h[:, k, c0:c1],
                                                   start=(k == 0), stop=(k == KT - 1))
                                    if c0 == 0 and ((bi == 0 and k < 2) or (bi == 2 and k == 0)):
                                        mm.then_inc(ring_turn, 1)
                            if bi == 0:
                                pe.wait_ge(ring_full[sbr], 16 * it + 16 * ((gg + 1) // SLOTS + 1))
                            src = y["ABCD"[bi]]
                            for c0, c1 in ((0, SEQ), (SEQ, T)):
                                if last and c0:
                                    continue
                                for k in range(4):
                                    mm = pe.matmul(pf[:, 2048 * (v % 2) + 1024 + c0:2048 * (v % 2) + 1024 + c1],
                                                   slot_br[:, sbr, bi, k, :], src[:, k, c0:c1],
                                                   start=(k == 0), stop=(k == 3))
                            mm.then_inc(mg_unit, 1)
                acc = at(MACC, KT, T)
                pe.wait_ge(mg_sum, 3 * KT * (L + 1))
                for m in range(KT):
                    t = tile_no[L, "out", m]
                    n, half = group_of[L, "out", m]
                    if half == 0:
                        group_in(n)
                    if m >= 2:
                        pe.wait_ge(drained[t % 2], t // 2)
                    for c0, c1 in ((0, SEQ), (SEQ, T)):
                        if last and c0:
                            continue
                        for k in range(KT):
                            mm = pe.matmul(pf[:, pair(t) + c0:pair(t) + c1], slot_tile[:, n % SLOTS, half, k, :],
                                           acc[:, k, c0:c1], start=(k == 0), stop=(k == KT - 1))
                            if c0 == 0 and ((half == 0 and k == 0) or (m == 0 and k == 1)):
                                mm.then_inc(ring_turn, 1)
                    mm.then_inc(tile_ready, 1)

            pe.wait_ge(const_in, 16 * 7)
            for L in range(DEPTH):
                filter_net(HYN[False], 2 * L)
                barrier(pe, PH(L, "filter"))
                if L == 0:
                    modulation(0)
                norm(L)
                barrier(pe, PH(L, "norm"))
                pe.wait_ge(h_ready, L + 1)
                project(L, "D")
                hyena(2 * L)
                barrier(pe, PH(L, "D"))
                if L < DEPTH - 1:
                    filter_net(HYN[True], 2 * L + 1)
                    hyena(2 * L + 1)
                    barrier(pe, PH(L, "Dc"))
                project(L, "C")
                gla(L)
                barrier(pe, PH(L, "C"))
                project(L, "A")
                attention(L, "A")
                barrier(pe, PH(L, "A"))
                project(L, "B")
                rotary(L)
                attention(L, "B")
                if L + 1 < DEPTH:
                    modulation(L + 1)
                barrier(pe, PH(L, "B"))
                merge(L)
                barrier(pe, PH(L, "merge"))
            for k in range(KT):
                pe.wait_ge(fin_sq, k + 1)
                mm = pe.matmul(pf[:, 0:SEQ], ones[:, :], h[:, k, 0:SEQ], start=(k == 0), stop=(k == KT - 1))
            mm.then_inc(norm_ps, 1)

        @block.scalar
        def _(act):
            def drain_tile(L, name, i, need, dst, func, scale=1.0, rows=128):
                t = tile_no[L, name, i]
                w = width(L, need)
                act.wait_ge(tile_ready, t + 1)
                src = pf[0:rows, pair(t):pair(t) + w]
                if name in ("va", "vb", "vg"):
                    src = src.rearrange("p (t f) -> p t f", f=128)
                act.activation(dst, src, func, scale=scale).then_inc(drained[t % 2], 1)

            def drain(L, mixer):
                for ti in TILES[mixer]:
                    if ti is None:
                        continue
                    what, i, _, need = ti
                    w = width(L, need)
                    if what == "u":
                        t = tile_no[L, what, i]
                        dst = (at(HX0, 4, T), at(HZ, 4, T), at(HV, 4, T))[i // 4][:, i % 4, 0:w]
                        act.wait_ge(tile_ready, t + 1)
                        act.activation(dst, pf[:, pair(t):pair(t) + w], ACT.Identity,
                                       scale=par[:, P_CW + 12 + i:P_CW + 13 + i],
                                       bias=par[:, P_CB + i:P_CB + i + 1]).then_inc(conv_ready, 1)
                    elif what in ("gd", "gg", "ga", "gb"):
                        drain_tile(L, what, i, need, y[mixer][:, i, 0:w], ACT.Silu)
                    elif what == "lr":
                        drain_tile(L, what, i, need, at(LR, T)[0:32, 0:w], ACT.Copy, rows=32)
                    elif what == "vg":
                        drain_tile(L, what, i, need, at(GV, 6, 512)[:, :, 128 * i:128 * i + 128], ACT.Copy)
                    elif what == "va":
                        drain_tile(L, what, i, need, at(AV, 6, 512)[:, :, 128 * i:128 * i + 128], ACT.Copy)
                    elif what == "vb":
                        drain_tile(L, what, i, need, at(BV, 6, 128), ACT.Copy)
                    elif what == "qa":
                        t = tile_no[L, what, i]
                        q = at(AQ + T * i, T)
                        act.wait_ge(tile_ready, t + 1)
                        ins = act.activation(q[:, 0:SEQ].rearrange("p (j r c) -> p r j c", r=8, c=NKC),
                                             pf[:, pair(t):pair(t) + SEQ].rearrange("p (r j c) -> p r j c", r=8, c=NKC),
                                             ACT.Copy, scale=HD ** -0.5)
                        if w > SEQ:
                            ins = act.activation(q[:, SEQ:T], pf[:, pair(t) + SEQ:pair(t) + T], ACT.Copy, scale=HD ** -0.5)
                        ins.then_inc(drained[t % 2], 1)
                    else:
                        off = {"ka": AK, "qb": BQ, "kb": BK, "qg": GQ, "kg": GK}[what]
                        drain_tile(L, what, i, need, at(off + T * i, T)[:, 0:w], ACT.Copy,
                                   scale=HD ** -0.5 if what[0] == "q" else 1.0)

            def filter_net(c, run):
                nt, n = c["nt"], c["n"]
                bd = FD(run)
                for k in range(3):
                    act.wait_ge(filt_dve, bd + k + 1)
                    dst = at((FH0, FH1, FH0)[k], 512)[0:64, 0:n]
                    act.activation(dst, at(FT, 512)[0:64, 0:n], ACT.Sin).then_inc(filt_act, 1)
                for j in range(2 * nt):
                    act.wait_ge(filt_dve, bd + 3 + 2 * nt)
                    if j >= 2:
                        act.wait_ge(filt_pe, FP(run) + 3 + 2 * nt + j - 1)
                    src = at(FHF if j % 2 == 0 else FHB, 4, 512)[:, j // 2, :]
                    act.activation(at(FABS + 512 * (j % 2), 512), src, ACT.Abs).then_inc(filt_act, 1)

            def norm(L, x):
                for k in range(KT):
                    act.activation(h[:, k, :], x[:, k, :], ACT.Square).then_inc(norm_sq, 1)
                act.wait_ge(norm_ms, L + 1)
                act.activation(rstd_all(), rstd_all(), ACT.Sqrt).then_inc(norm_rt, 1)

            def rstd_all():
                return at(ZSPEC, T)

            def hyena(run):
                L, is_c = hy_runs[run]
                c = HYN[is_c]
                if not is_c:
                    for j in range(6 if L < DEPTH - 1 else 4):
                        act.wait_ge(hy_tr, ZT(L) + j + 1)
                        act.activation(at(HV, 6, 512)[:, j, :], pf[:, 512 * (4 + j % 2):512 * (5 + j % 2)], ACT.Copy)\
                            .then_inc(hy_ztok, 1)
                if is_c:
                    act.wait_ge(filt_dve, FD(run + 1))
                for j in range(2 * c["nt"]):
                    act.wait_ge(hy_spec, HZS(run) + j + 1)
                    act.activation(at(ZSPEC, 8, 512)[:, j, :], pf[:, 512 * (6 + j % 2):512 * (7 + j % 2)], ACT.Copy)\
                        .then_inc(hy_zs, 1)

            def gla(L):
                oc = width(L, False)
                E = at(GE, 2, 3, T)
                for hp in range(2):
                    N = 2 * L + hp
                    for d in range(2):
                        zb, lb = at(GL + 1536 * d, T), at(GL + 1536 * d + T, T)
                        act.wait_ge(gl_z, 2 * N + d + 1)
                        act.activation(lb, zb, ACT.Abs).then_inc(gl_ln, 1)
                        act.wait_ge(gl_ln, 6 * N + 3 * d + 1)
                        act.activation(lb, lb, ACT.Exp, scale=-1.0).then_inc(gl_ln, 1)
                        act.wait_ge(gl_ln, 6 * N + 3 * d + 2)
                        act.activation(lb, lb, ACT.Ln, bias=1.0).then_inc(gl_ln, 1)
                    for d in range(2):
                        zb, lb = at(GL + 1536 * d, T), at(GL + 1536 * d + T, T)
                        act.wait_ge(gl_cum, 2 * N + d + 1)
                        act.activation(E[:, d, 0, :], lb, ACT.Exp, scale=1.0 / 16)
                        act.activation(E[:, d, 1, :], lb, ACT.Exp, scale=-1.0 / 16)
                        act.wait_ge(gl_rest, 2 * N + d + 1)
                        act.activation(E[:, d, 2, :], zb, ACT.Exp, scale=1.0 / 16).then_inc(gl_exp, 1)
                    for d in range(2):
                        act.wait_ge(gl_tr, 2 * N + d + 1)
                        act.activation(E[:, d, 2, :], pf[:, 1024 * d:1024 * d + T], ACT.Copy).then_inc(gl_ket, 1)
                    for e in range(2):
                        base = 2048 if e == 0 else 0
                        act.wait_ge(gl_o, 2 * N + e + 1)
                        act.activation(at(GO + T * e, T)[:, 0:oc], pf[:, base:base + oc], ACT.Copy)
                        act.activation(at(GL, 2, T)[:, e, 0:oc], pf[:, base:base + oc], ACT.Square).then_inc(gl_sq, 1)
                    for e in range(2):
                        act.wait_ge(gl_ms, 2 * N + e + 1)
                        r = at(GR, T)[:, 0:oc]
                        act.activation(r, r, ACT.Sqrt).then_inc(gl_rt, 1)

            def attention(L, mixer):
                A = mixer == "A"
                us = units(mixer, L)
                u0 = unit0[L, mixer]
                p_at = AP_ if A else BTMP
                pt_at = APT if A else BTMP + 1280

                def exps(n):
                    q, i, p = us[n]
                    w = 128 * len(key_blocks(mixer, q))
                    hh = head(mixer, i, p)
                    act.wait_ge(at_max, u0 + n + 1)
                    if n >= 2:
                        act.wait_ge(at_pt, u0 + n - 1)
                    if hh == 0 and q >= 2:
                        act.wait_ge(at_on, qt0[L, mixer] + q - 1)
                    act.activation(at(p_at + 640 * p, 640)[:, 0:w], pf[:, 1024 * p:1024 * p + w], ACT.Exp,
                                   bias=stat[:, q % 2, 0, hh:hh + 1],
                                   accum_out=stat[:, q % 2, 1, hh:hh + 1]).then_inc(at_p, 1)

                def copies(n):
                    q, i, p = us[n]
                    nb = len(key_blocks(mixer, q))
                    act.wait_ge(at_pt, u0 + n + 1)
                    if n >= 2:
                        act.wait_ge(at_o, u0 + n - 1)
                    PT = at(pt_at + 640 * p, 640)
                    w = 128 * min(nb, 4)
                    ins = act.activation(PT[:, 0:w], pf[:, 2048 + 512 * p:2048 + 512 * p + w], ACT.Copy)
                    if nb == 5:
                        ins = act.activation(PT[:, 512:640], pf[:, 3072:3200], ACT.Copy)
                    ins.then_inc(at_ptc[1], 1)

                exps(0)
                exps(1)
                for n in range(0, len(us), 2):
                    if n + 2 < len(us):
                        exps(n + 2)
                    copies(n + 1)
                    if n + 3 < len(us):
                        exps(n + 3)
                    if mixer == "B" and n % 8 == 6:
                        q = us[n][0]
                        act.wait_ge(at_sum, QB(L) + q + 1)
                        act.activation(stat[:, q % 2, 3, :], stat[:, q % 2, 3, :], ACT.Exp).then_inc(at_sink, 1)

            def merge(L):
                w = width(L, False)
                with act.Fori(0, KT // 2) as it:
                    for v in range(8):
                        act.wait_ge(mg_unit, 8 * it + (MG(L) + v + 1))
                        act.wait_ge(mg_prod, 8 * it + (MG(L) + v + 1))
                        act.activation(at(MGATE + T * (v % 2), T)[:, 0:w], pf[:, 2048 * (v % 2):2048 * (v % 2) + w],
                                       ACT.Sigmoid).then_inc(mg_gate, 1)

            act.wait_ge(const_in, 16 * 7)
            act.activation(csil[:, :, :], par[:, P_C:P_C + 16].rearrange("p (k c) -> p k c", c=2), ACT.Silu)\
                .then_inc(csil_ready, 1)
            for L in range(DEPTH):
                filter_net(HYN[False], 2 * L)
                barrier(act, PH(L, "filter"))
                if L == 0:
                    act.wait_ge(x_in, 16)
                norm(L, at(X_AT, KT, T))
                barrier(act, PH(L, "norm"))
                drain(L, "D")
                hyena(2 * L)
                barrier(act, PH(L, "D"))
                if L < DEPTH - 1:
                    filter_net(HYN[True], 2 * L + 1)
                    hyena(2 * L + 1)
                    barrier(act, PH(L, "Dc"))
                drain(L, "C")
                gla(L)
                barrier(act, PH(L, "C"))
                drain(L, "A")
                attention(L, "A")
                barrier(act, PH(L, "A"))
                drain(L, "B")
                attention(L, "B")
                barrier(act, PH(L, "B"))
                merge(L)
                barrier(act, PH(L, "merge"))
            for k in range(KT):
                act.activation(h[:, k, 0:SEQ], at(X_AT, KT, T)[:, k, 0:SEQ], ACT.Square).then_inc(fin_sq, 1)
            act.wait_ge(norm_ms, DEPTH + 1)
            act.activation(at(MGATE, SEQ), at(MGATE, SEQ), ACT.Sqrt).then_inc(norm_rt, 1)

        @block.vector
        def _(dve):
            chain = [0]

            def link(ins):
                chain[0] += 1
                ins.then_inc(dve_chain, 1)
                dve.wait_ge(dve_chain, chain[0])

            def filter_net(c, run):
                nt, n = c["nt"], c["n"]
                ba, bp = FA(run), FP(run)
                t, r = at(FT, 512)[0:64, 0:n], at(FABS, 512)[0:64, 0:n]
                dve.wait_ge(filt_in, FIN(run))
                for k in range(3):
                    dve.wait_ge(filt_pe, bp + k + 1)
                    if k:
                        dve.wait_ge(filt_act, ba + k)
                    link(dve.tensor_scalar(t, pf[0:64, 0:n], par[0:64, P_B1 + k:P_B1 + k + 1], par[0:64, P_FREQ:P_FREQ + 1],
                                           ALU.add, ALU.mult))
                    link(dve.tensor_scalar(r, t, 1.0 / (2.0 * math.pi), ROUND, ALU.mult, ALU.add))
                    link(dve.tensor_scalar(r, r, ROUND, None, ALU.subtract))
                    link(dve.scalar_tensor_tensor(t, r, -TWO_PI_HI, t, ALU.mult, ALU.add))
                    link(dve.scalar_tensor_tensor(t, r, -TWO_PI_LO, t, ALU.mult, ALU.add))
                    dve.tensor_scalar(t, t, PI_IN, -PI_IN, ALU.min, ALU.max).then_inc(filt_dve, 1)
                dec = at(FDEC, 4, 512)
                hf, hb = at(FHF, 4, 512), at(FHB, 4, 512)
                for j in range(2 * nt):
                    dve.wait_ge(filt_pe, bp + 3 + j + 1)
                    dst = (hf, hb)[j % 2][:, j // 2, :]
                    ins = dve.tensor_tensor(dst, pf[:, 512 * (1 + j % 2):512 * (2 + j % 2)], dec[:, j // 2, :], ALU.mult)
                    if j == 1:
                        link(ins)
                        ins = dve.memset(hb[0:1, 0, :], 0.0)
                    ins.then_inc(filt_dve, 1)
                dve.wait_ge(filt_act, ba + 3 + 2 * nt)
                dve.wait_ge(filt_dve, FD(run) + 3 + 2 * nt)
                dve.tensor_tensor(dec[:, 0:nt, :], hf[:, 0:nt, :], hb[:, 0:nt, :], ALU.add).then_inc(filt_dve, 1)
                dve.wait_ge(filt_dve, FD(run) + 3 + 2 * nt + 1)
                dve.tensor_tensor(hb[:, 0:nt, :], hf[:, 0:nt, :], hb[:, 0:nt, :], ALU.subtract).then_inc(filt_dve, 1)
                dve.wait_ge(filt_pe, bp + 3 + 4 * nt)
                rl = at(FHF, 512)
                dve.wait_ge(filt_dve, FD(run) + 3 + 2 * nt + 2)
                dve.reciprocal(rl, pf[:, 1536:2048]).then_inc(filt_dve, 1)
                dve.wait_ge(filt_dve, FD(run) + 3 + 2 * nt + 3)
                ks = at(KSPEC, 8, 512)
                for j in range(2 * nt):
                    dve.wait_ge(filt_pe, bp + 3 + 4 * nt + j + 1)
                    dve.tensor_tensor(ks[:, j, :], pf[:, 512 * (4 + j % 2):512 * (5 + j % 2)], rl, ALU.mult)\
                        .then_inc(filt_dve, 1)
                dve.wait_ge(filt_pe, bp + 3 + 6 * nt + 1)
                dve.wait_ge(filt_dve, FD(run) + 3 + 4 * nt + 3)
                dve.tensor_tensor(ks[0:1, nt, :], pf[0:1, 0:512], rl[0:1, :], ALU.mult).then_inc(filt_dve, 1)

            def modulation(L):
                dve.wait_ge(mod_ready, MOD_GROUPS * (L + 1))
                link(dve.tensor_copy(mod[:, L, :, :], pf[:, 2048:2048 + 2 * MOD_TILES].rearrange("p (m c) -> p m c", c=2)))

            def norm(L, x):
                rstd = at(ZSPEC, T)
                for c in range(2):
                    link(dve.tensor_tensor(mod[:, L, :, c], mod[:, L, :, c], par[:, P_BMOD:P_BMOD + MOD_TILES], ALU.add))
                for c in range(2):
                    link(dve.scalar_tensor_tensor(nscale[:, :, c], mod[:, L, KT:2 * KT, c], 1.0, par[:, P_NORM:P_NORM + KT],
                                                  ALU.add, ALU.mult))
                dve.wait_ge(norm_ps, L + 1)
                link(dve.tensor_scalar(rstd, pf[:, 0:T], 1.0 / D_MODEL, EPS, ALU.mult, ALU.add))
                dve.reciprocal(rstd, rstd).then_inc(norm_ms, 1)
                dve.wait_ge(norm_rt, L + 1)
                for k in range(KT):
                    for c, (c0, c1) in enumerate(((0, SEQ), (SEQ, T))):
                        ins = dve.scalar_tensor_tensor(h[:, k, c0:c1], x[:, k, c0:c1], nscale[:, k, c:c + 1], rstd[:, c0:c1],
                                                       ALU.mult, ALU.mult)
                link(ins)
                for k in range(KT):
                    for c, (c0, c1) in enumerate(((0, SEQ), (SEQ, T))):
                        ins = dve.tensor_scalar(h[:, k, c0:c1], h[:, k, c0:c1], mod[:, L, k, c:c + 1], None, ALU.add)
                ins.then_inc(h_ready, 1)

            def conv(L):
                x0, z, v = at(HX0, 4, T), at(HZ, 4, T), at(HV, 4, T)
                segs = ((0, SEQ), (SEQ, T))[:2 if L < DEPTH - 1 else 1]
                for i in range(12):
                    t = tile_no[L, "u", i]
                    dst = (x0, z, v)[i // 4][:, i % 4, :]
                    src = pf[:, pair(t):pair(t) + T]
                    dve.wait_ge(conv_ready, 12 * L + i + 1)
                    for c0, c1 in segs:
                        ins = dve.scalar_tensor_tensor(dst[:, c0 + 1:c1], src[:, c0:c1 - 1], par[:, P_CW + i:P_CW + i + 1],
                                                       dst[:, c0 + 1:c1], ALU.mult, ALU.add)
                    link(ins)
                    for c0, c1 in segs:
                        ins = dve.scalar_tensor_tensor(dst[:, c0:c1 - 1], src[:, c0 + 1:c1], par[:, P_CW + 24 + i:P_CW + 25 + i],
                                                       dst[:, c0:c1 - 1], ALU.mult, ALU.add)
                    ins.then_inc(drained[t % 2], 1)
                t = tile_no[L, "u", 11]
                dve.wait_ge(drained[t % 2], t // 2 + 1)
                w = width(L, False)
                for i in range(4):
                    dve.tensor_tensor(z[:, i, 0:w], z[:, i, 0:w], v[:, i, 0:w], ALU.mult).then_inc(hy_z, 1)

            def hyena(run):
                L, is_c = hy_runs[run]
                c = HYN[is_c]
                nt, n, c0 = c["nt"], c["n"], 128 * c["t0"]
                ks, zs = at(KSPEC, 8, 512), at(ZSPEC, 8, 512)
                t1, t2 = at(HTMP, 512), at(HTMP + 512, 512)
                for j in range(nt):
                    zc, zn, kc, kn = zs[:, j, :], zs[:, nt + j, :], ks[:, j, :], ks[:, nt + j, :]
                    dve.wait_ge(hy_zs, HZS(run) + nt + j + 1)
                    dve.tensor_tensor(t1, zn, kn, ALU.mult)
                    link(dve.tensor_tensor(t2, zn, kc, ALU.mult))
                    link(dve.tensor_tensor(zn, zc, kn, ALU.mult))
                    dve.tensor_tensor(zn, zn, t2, ALU.add)
                    link(dve.tensor_tensor(zc, zc, kc, ALU.mult))
                    if j == 0:
                        link(dve.tensor_copy(zn[0:1, :], t1[0:1, :]))
                        link(dve.memset(t1[0:1, :], 0.0))
                    dve.tensor_tensor(zc, zc, t1, ALU.subtract).then_inc(hy_prod, 1)
                    dve.wait_ge(hy_prod, HPR(run) + j + 1)
                if not is_c:
                    wait_tile(dve, L, "gd", 3)
                    wait_tile(dve, L, "gd", 2)
                x0, z = at(HX0, 4, T), at(HZ, 4, T)
                for cc in range(4):
                    dve.wait_ge(hy_inv, 4 * run + cc + 1)
                    zz, xx, yy = z[:, cc, c0:c0 + n], x0[:, cc, c0:c0 + n], y["D"][:, cc, c0:c0 + n]
                    dve.scalar_tensor_tensor(zz, zz, par[:, P_FB + cc:P_FB + cc + 1],
                                             pf[:, 512 * (4 + cc % 2):512 * (4 + cc % 2) + n], ALU.mult, ALU.add)\
                        .then_inc(hy_out, 1)
                    dve.wait_ge(hy_out, 4 * run + cc + 1)
                    link(dve.tensor_tensor(yy, yy, xx, ALU.mult))
                    link(dve.tensor_tensor(yy, yy, zz, ALU.mult))

            def gla(L):
                oc = width(L, False)
                q, k = at(GQ, 2, T), at(GK, 2, T)
                E = at(GE, 2, 3, T)
                S = at(GS, 2, 12, 128)
                A = at(GAT, 2, 2, T)
                link(dve.memset(A, 0.0))
                link(dve.memset(S[:, :, 0, :], 0.0))
                wait_tile(dve, L, "gg", 3)
                wait_tile(dve, L, "gg", 2)
                for hp in range(2):
                    N = 2 * L + hp
                    for d in range(2):
                        zb, lb = at(GL + 1536 * d, T), at(GL + 1536 * d + T, T)
                        dve.wait_ge(gl_alpha, 2 * N + d + 1)
                        dve.tensor_scalar(zb, pf[:, 1024 * d:1024 * d + T], par[:, P_BA + 2 * d + hp:P_BA + 2 * d + hp + 1], None,
                                          ALU.add).then_inc(gl_z, 1)
                    for d in range(2):
                        zb, lb = at(GL + 1536 * d, T), at(GL + 1536 * d + T, T)
                        dve.wait_ge(gl_ln, 6 * N + 3 * d + 3)
                        link(dve.scalar_tensor_tensor(zb, zb, 0.0, lb, ALU.min, ALU.subtract))
                        if d == 0:
                            dve.tensor_tensor_scan(lb, cmask[:, 0, :], zb, 0.0, ALU.mult, ALU.add).then_inc(gl_cum, 1)
                        else:
                            dve.tensor_tensor_scan(lb[:, ::-1], cmask[:, 1, ::-1], zb[:, ::-1], 0.0, ALU.mult, ALU.add)\
                                .then_inc(gl_cum, 1)
                        dve.wait_ge(gl_cum, 2 * N + d + 1)
                        l3 = lb.rearrange("p (n c) -> p n c", c=64)
                        end = l3[:, :, 63:64] if d == 0 else l3[:, :, 0:1]
                        dve.tensor_tensor(zb.rearrange("p (n c) -> p n c", c=64), end.to_broadcast([128, 12, 64]), l3,
                                          ALU.subtract).then_inc(gl_rest, 1)
                    for d in range(2):
                        dve.wait_ge(gl_exp, 2 * N + d + 1)
                        e3 = E[:, d, 0, :].rearrange("p (n c) -> p n c", c=64)
                        dve.tensor_tensor(E[:, d, 2, :], E[:, d, 2, :], k[:, hp, :], ALU.mult).then_inc(gl_ke, 1)
                        dve.tensor_tensor(E[:, d, 1, :], E[:, d, 1, :], k[:, hp, :], ALU.mult)
                        link(dve.tensor_copy(gend[:, d, :], e3[:, :, 63 if d == 0 else 0]))
                        dve.tensor_tensor(E[:, d, 0, 0:oc], E[:, d, 0, 0:oc], q[:, hp, 0:oc], ALU.mult).then_inc(gl_qk, 1)
                    for d in range(2):
                        dve.wait_ge(gl_kv, 2 * N + d + 1)
                        base = 2048 if d == 0 else 0
                        for s in range(11):
                            n = chunk_at(d, s)
                            kv = pf[:, base + 1024 * (n % 2) + 128 * (n // 2):base + 1024 * (n % 2) + 128 * (n // 2) + 128]
                            ins = dve.scalar_tensor_tensor(S[:, d, s + 1, :], S[:, d, s, :], gend[:, d, n:n + 1], kv,
                                                           ALU.mult, ALU.add)
                            if s < 10:
                                link(ins)
                        ins.then_inc(gl_state, 1)
                    for e in range(2):
                        for d in range(2):
                            dve.wait_ge(gl_at, 4 * N + 2 * e + d + 1)
                            base = (2048 if e == 0 else 0) + 1024 * d
                            dve.copy_predicated(A[:, e, d, 0:oc].rearrange("p (t i) -> p t i", i=128),
                                                umask[:, d:d + 1, :].to_broadcast([128, oc // 128, 128]),
                                                pf[:, base:base + oc].rearrange("p (t i) -> p t i", i=128)).then_inc(gl_atc, 1)
                    for e in range(2):
                        base = (2048 if e == 0 else 0) + 1024
                        r = at(GR, T)[:, 0:oc]
                        o = at(GO + T * e, T)[:, 0:oc]
                        yy = y["C"][:, 2 * hp + e, 0:oc]
                        dve.wait_ge(gl_ss, 2 * N + e + 1)
                        link(dve.tensor_scalar(r, pf[:, base:base + oc], 1.0 / 128, EPS, ALU.mult, ALU.add))
                        dve.reciprocal(r, r).then_inc(gl_ms, 1)
                        dve.wait_ge(gl_rt, 2 * N + e + 1)
                        link(dve.scalar_tensor_tensor(o, o, par[:, P_GN:P_GN + 1], r, ALU.mult, ALU.mult))
                        dve.tensor_tensor(yy, yy, o, ALU.mult).then_inc(gl_fin, 1)
                        dve.wait_ge(gl_fin, 2 * N + e + 1)

            def rotary(L):
                cs = at(BROPE, 2, 512)
                t = at(BTMP, 512)
                dve.wait_ge(rope_in, 16 * (L + 1))
                for i in range(5):
                    x = at(BQ, 4, T)[:, i, 0:SEQ] if i < 4 else at(BK, T)[:, 0:SEQ]
                    dve.wait_ge(rope_rot, 5 * L + i + 1)
                    dve.tensor_tensor(t, pf[:, 512 * (4 + i % 2):512 * (5 + i % 2)], cs[:, 1, :], ALU.mult)
                    link(dve.tensor_tensor(x, x, cs[:, 0, :], ALU.mult))
                    dve.tensor_tensor(x, x, t, ALU.add).then_inc(rope_done, 1)
                    dve.wait_ge(rope_done, 5 * L + i + 1)

            def attention(L, mixer):
                A = mixer == "A"
                us = units(mixer, L)
                u0 = unit0[L, mixer]
                pt_at = APT if A else BTMP + 1280
                o_at = AO if A else BTMP + 2560

                def maxima(n):
                    q, i, p = us[n]
                    hh = head(mixer, i, p)
                    w = 128 * len(key_blocks(mixer, q))
                    s = pf[:, 1024 * p:1024 * p + w]
                    dve.wait_ge(at_s, u0 + n + 1)
                    if A and q < 4:
                        if i == 0 and p == 0:
                            dve.wait_ge(bias_in[q % 2], 16 * (2 * L + q // 2 + 1))
                        dve.tensor_reduce(rmx[:, 0:1], s[:, 256:512], AX, ALU.max)
                        link(dve.tensor_tensor_reduce(s[:, 0:256], s[:, 0:256], at(ABIAS + 2048 * (q % 2), 8, 256)[:, hh, :],
                                                      1.0, -3e38, ALU.add, ALU.max, rmx[:, 1:2]))
                        m1 = rmx[:, 1:2]
                    else:
                        link(dve.tensor_reduce(rmx[:, 0:1], s, AX, ALU.max))
                        m1 = par[:, P_SINK + hh:P_SINK + hh + 1] if not A else rmx[:, 0:1]
                    dve.tensor_scalar(stat[:, q % 2, 0, hh:hh + 1], rmx[:, 0:1], m1, -1.0, ALU.max, ALU.mult).then_inc(at_max, 1)
                    dve.wait_ge(at_max, u0 + n + 1)

                def copies(n):
                    q, i, p = us[n]
                    nb = len(key_blocks(mixer, q))
                    dve.wait_ge(at_pt, u0 + n + 1)
                    if n >= 2:
                        dve.wait_ge(at_o, u0 + n - 1)
                    PT = at(pt_at + 640 * p, 640)
                    w = 128 * min(nb, 4)
                    ins = dve.tensor_copy(PT[:, 0:w], pf[:, 2048 + 512 * p:2048 + 512 * p + w])
                    if nb == 5:
                        ins = dve.tensor_copy(PT[:, 512:640], pf[:, 3072:3200])
                    ins.then_inc(at_ptc[0], 1)

                def finish(q, n):
                    st = stat[:, q % 2, :, :]
                    if not A:
                        dve.tensor_tensor(st[:, 3, :], par[:, P_SINK:P_SINK + 8], st[:, 0, :], ALU.add).then_inc(at_sum, 1)
                        dve.wait_ge(at_sink, QB(L) + q + 1)
                        dve.wait_ge(at_p, u0 + n + 2)
                        link(dve.tensor_tensor(st[:, 1, :], st[:, 1, :], st[:, 3, :], ALU.add))
                    dve.wait_ge(at_p, u0 + n + 2)
                    link(dve.reciprocal(st[:, 2, :], st[:, 1, :]))
                    dve.wait_ge(at_o, u0 + n + 2)
                    o = at(o_at, 8, 64)
                    dve.tensor_tensor(o, pf[:, 3584:4096].rearrange("p (h d) -> p h d", d=64),
                                      st[:, 2, :].unsqueeze(2).to_broadcast([128, 8, 64]), ALU.mult).then_inc(at_on, 1)

                def gate(q):
                    dve.wait_ge(at_ot, qt0[L, mixer] + q + 1)
                    turned = pf[:, 3072:3584].rearrange("p (f t) -> p f t", f=4)
                    if A and q < 4:
                        yy = y[mixer][:, :, 0:SEQ].rearrange("p f (r c) -> p f r c", c=GRID_W)[:, :, :, NKC * q:NKC * q + NKC]
                        turned = turned.rearrange("p f (r c) -> p f r c", c=NKC)
                        for f in range(4):
                            ins = dve.tensor_tensor(yy[:, f], yy[:, f], turned[:, f], ALU.mult)
                    else:
                        yy = y[mixer][:, :, 128 * q:128 * q + 128]
                        ins = dve.tensor_tensor(yy, yy, turned, ALU.mult)
                    ins.then_inc(at_y, 1)

                maxima(0)
                maxima(1)
                for n in range(0, len(us), 2):
                    q = us[n][0]
                    copies(n)
                    if n + 2 < len(us):
                        maxima(n + 2)
                        maxima(n + 3)
                    if n % 8 == 6:
                        finish(q, n)
                        gate(q)

            def merge(L):
                w = width(L, False)
                last = L == DEPTH - 1
                acc = at(MACC, KT, T)
                with dve.Fori(0, KT // 2) as it:
                    for v in range(8):
                        prod = at(MPROD + T * (v % 2), T)[:, 0:w]
                        dst = ar[:, bass.ds(it * (2 * T) + (MACC + T * (v // 4)), w)]
                        dve.wait_ge(mg_gate, 8 * it + (MG(L) + v + 1))
                        src = pf[:, 2048 * (v % 2) + 1024:2048 * (v % 2) + 1024 + w]
                        gate = at(MGATE + T * (v % 2), T)[:, 0:w]
                        if v % 4 == 0:
                            dve.tensor_tensor(dst, gate, src, ALU.mult).then_inc(mg_prod, 1)
                        else:
                            dve.tensor_tensor(prod, gate, src, ALU.mult).then_inc(mg_prod, 1)
                            dve.wait_ge(mg_prod, 8 * it + (MG(L) + v + 3))
                            dve.tensor_tensor(dst, dst, prod, ALU.add).then_inc(mg_sum, 1)
                            dve.wait_ge(mg_sum, 6 * it + (3 * KT * L + v - v // 4))
                x = at(X_AT, KT, T)
                dve.wait_ge(x_in, 16 * (L + 2))
                for m in range(KT):
                    t = tile_no[L, "out", m]
                    dve.wait_ge(tile_ready, t + 1)
                    for c, (c0, c1) in enumerate(((0, SEQ), (SEQ, w))):
                        if c1 > c0:
                            ins = dve.scalar_tensor_tensor(x[:, m, c0:c1], pf[:, pair(t) + c0:pair(t) + c1],
                                                           mod[:, L, 2 * KT + m, c:c + 1], x[:, m, c0:c1], ALU.mult, ALU.add)
                    ins.then_inc(drained[t % 2], 1)

            for i in range(2):
                dve.memset(rmx[:, 2 + i:3 + i], 0.0).then_inc(mg_prod, 1)
            dve.wait_ge(const_in, 16 * 7)
            for L in range(DEPTH):
                if L:
                    dve.wait_ge(par_in, 16 * L)
                filter_net(HYN[False], 2 * L)
                barrier(dve, PH(L, "filter"))
                if L == 0:
                    modulation(0)
                norm(L, at(X_AT, KT, T))
                barrier(dve, PH(L, "norm"))
                conv(L)
                hyena(2 * L)
                barrier(dve, PH(L, "D"))
                if L < DEPTH - 1:
                    filter_net(HYN[True], 2 * L + 1)
                    hyena(2 * L + 1)
                    barrier(dve, PH(L, "Dc"))
                gla(L)
                barrier(dve, PH(L, "C"))
                attention(L, "A")
                barrier(dve, PH(L, "A"))
                rotary(L)
                attention(L, "B")
                if L + 1 < DEPTH:
                    modulation(L + 1)
                barrier(dve, PH(L, "B"))
                merge(L)
                barrier(dve, PH(L, "merge"))
            r = at(MGATE, SEQ)
            dve.wait_ge(norm_ps, DEPTH + 1)
            link(dve.tensor_scalar(r, pf[:, 0:SEQ], 1.0 / D_MODEL, EPS, ALU.mult, ALU.add))
            dve.reciprocal(r, r).then_inc(norm_ms, 1)
            dve.wait_ge(norm_rt, DEPTH + 1)
            for k in range(KT):
                dve.scalar_tensor_tensor(h[:, k, 0:SEQ], at(X_AT, KT, T)[:, k, 0:SEQ], par[:, P_FIN + k:P_FIN + k + 1], r,
                                         ALU.mult, ALU.mult).then_inc(res_done, 1)


def weight_stream(w_mod, w_in, w_branch, w_out):
    def tile(w, c0, n=128):
        t = np.zeros((128, KT, 128), np.float32)
        t[:, :, :n] = w[:, c0:c0 + n].reshape(KT, 128, n).transpose(1, 0, 2)
        return t

    def in_tile(L, ti):
        if ti is None:
            return np.zeros((128, KT, 128), np.float32)
        what, i, c0, _ = ti
        if what == "lr":
            return tile(w_in[L], c0, 32)
        if what == "qb":
            t = tile(w_in[L], c0 + HD * i)
            t[:, :, HD:] = tile(w_in[L], c0 + HD * (i + 4))[:, :, :HD]
            return t
        return tile(w_in[L], c0)

    groups = []

    def add(tiles):
        for a, b in zip(tiles[::2], tiles[1::2]):
            groups.append(np.stack([a, b], 1).reshape(128, GROUP))

    add([tile(w_mod[0], 128 * m) for m in range(MOD_TILES)])
    for L in range(DEPTH):
        for b in MIXERS:
            add([in_tile(L, ti) for ti in TILES[b]])
        if L + 1 < DEPTH:
            add([tile(w_mod[L + 1], 128 * m) for m in range(MOD_TILES)])
        for m in range(KT):
            gates = [tile(w_in[L], GM + D_MODEL * i + 128 * m) for i in range(4)]
            add(gates[:2])
            br = w_branch[L][:, :, 128 * m:128 * m + 128].reshape(4, 4, 128, 128)
            groups.append(br.transpose(2, 0, 1, 3).reshape(128, GROUP))
            add(gates[2:])
        add([tile(w_out[L], 128 * m) for m in range(KT)])
    return np.stack(groups)


def columns(v):
    return np.asarray(v).reshape(-1, 128).T


def parameter_table(L, a):
    t = np.zeros((128, P_W), np.float32)
    t[:, P_NORM:P_NORM + 8] = columns(a["norm_w"][L])
    t[:, P_BMOD:P_BMOD + 24] = columns(a["b_mod"][L])
    t[:, P_CW:P_CW + 36] = columns(a["conv_w"][L])
    t[:, P_CB:P_CB + 12] = columns(a["conv_b"][L])
    t[:, P_FB:P_FB + 4] = columns(a["filt_bias"][L])
    t[:, P_BA:P_BA + 4] = columns(a["b_alpha"][L])
    t[:, P_GN] = a["gla_norm_w"][L]
    for col, name in ((P_FREQ, "filt_freq"), (P_B1, "filt_b1"), (P_B2, "filt_b2"), (P_B3, "filt_b3")):
        t[:64, col] = a[name][L]
    t[:, P_SINK:P_SINK + 8] = a["sink"][L]
    t[:, P_FIN:P_FIN + 8] = columns(a["final_norm_w"])
    t[:, P_C:P_C + 16:2] = columns(a["c"])
    t[:, P_C + 1:P_C + 16:2] = columns(a["c_ctx"])
    return t


def natten_bias(rpb):
    r, c, rk, ck = np.ogrid[0:8, 0:NKC, 0:8, 0:2 * NKC]
    out = np.empty((4, 128, HEADS, 256), np.float32)
    for j, c0 in enumerate(NATTEN_COL0):
        col, kcol = NKC * j + c, c0 + ck
        first = np.clip(col - NKC // 2, 0, GRID_W - NKC)
        seen = np.broadcast_to((kcol >= first) & (kcol < first + NKC), (8, NKC, 8, 2 * NKC))
        dr = np.broadcast_to(rk - r + NKR - 1, seen.shape)
        dc = np.broadcast_to(np.clip(kcol - col + NKC - 1, 0, 2 * NKC - 2), seen.shape)
        v = np.where(seen, rpb[:, dr, dc], np.float32(NEG))
        out[j] = v.reshape(HEADS, 128, 256).transpose(1, 0, 2)
    return out


def filter_constants(n):
    f32 = np.float32
    t = np.linspace(0.0, 1.0, n, dtype=f32)
    ang = (f32(2.0 * math.pi) * np.arange(n, dtype=f32) / f32(n)).astype(f32)
    f = np.linspace(1e-4, 15, 16, dtype=f32)
    fa = (f[:, None] * ang[None, :]).astype(f32).astype(np.float64)
    z = np.concatenate([t[None, :], np.cos(fa), -np.sin(fa)], 0).astype(f32)
    deltas = np.abs(np.linspace(math.log(1e-2) / 1.5, math.log(1e-2) / 0.3, 512, dtype=f32))
    decay = np.exp((-t[:, None] * deltas[None, :]).astype(np.float64)).astype(f32)
    return z, decay


def transforms(n):
    w, t = np.arange(n)[:, None], np.arange(n)[None, :]
    ang = 2.0 * np.pi * ((w * t) % (2 * n)) / (2 * n)
    c, s = np.cos(ang), np.sin(ang)
    s[0] = (-1.0) ** np.arange(n)
    back = np.concatenate([c, s], 0) / n
    back[0] /= 2
    back[n] /= 2
    def rows(m):
        return m.reshape(-1, 128, m.shape[1]).transpose(1, 0, 2).astype(np.float32)
    return rows(np.concatenate([c, s], 0).T), rows(back)


def kernel(**inputs):
    import concourse.bacc as bacc
    import ml_dtypes
    from concourse.bass_utils import run_bass_kernel_spmd

    a = {k: np.asarray(v) for k, v in inputs.items()}
    z_l, dec_l = filter_constants(SEQ)
    z_c, dec_c = filter_constants(CTX)
    dft, idft = transforms(SEQ)
    dft_c, idft_c = transforms(CTX)
    eye = np.eye(128, dtype=np.float32)
    sign = ((-1.0) ** np.arange(128)).astype(np.float32)
    i = np.arange(128)
    left = np.where(i[None, :] >= i[:, None], 0.0, NEG)
    right = np.where(i[None, :] <= i[:, None], 0.0, NEG)
    tt = np.arange(T)
    starts = np.broadcast_to((tt % 64 != 0).astype(np.float32), (128, T))
    ends = np.broadcast_to((tt % 64 != 63).astype(np.float32), (128, T))
    same = i[:, None] // 64 == i[None, :] // 64
    pos = np.arange(SEQ)
    inv = (np.float32(10000.0) ** (-np.arange(16, dtype=np.float32) / 16)).astype(np.float32)
    ang = np.concatenate([(pos // GRID_W)[:, None] * inv, (pos % GRID_W)[:, None] * inv], 1).astype(np.float32)
    ang = np.tile(ang.T.astype(np.float64), (4, 1))
    rot = np.zeros((128, 128), np.float32)
    for b in (0, 64):
        for d in range(32):
            rot[b + 32 + d, b + d] = -1.0
            rot[b + d, b + 32 + d] = 1.0
    fw = np.zeros((DEPTH, 64, 192), np.float32)
    fw[:, :33, 0:64], fw[:, :, 64:128], fw[:, :, 128:192] = a["filt_w1"], a["filt_w2"], a["filt_w3"]
    alpha = np.zeros((DEPTH, 32, 512), np.float32)
    alpha[:, 0:16, 0:256], alpha[:, 16:32, 256:512] = a["w_alpha_up"][:, 0], a["w_alpha_up"][:, 1]
    xT = np.concatenate([a["x"][0], a["ctx"][0]], 0).T.reshape(KT, 128, T).transpose(1, 0, 2)
    arrays = {
        "wstream": weight_stream(a["w_mod"], a["w_in"], a["w_branch"], a["w_out"]),
        "xT": xT,
        "params": np.stack([parameter_table(L, a) for L in range(DEPTH)]),
        "zembT": np.concatenate([z_l, z_c], 1),
        "filt_w": fw,
        "filt_wout": a["filt_wout"],
        "decay": np.concatenate([dec_l, dec_c], 0).reshape(6, 128, 512).transpose(1, 0, 2),
        "dft": dft, "dft_c": dft_c, "idft": idft, "idft_c": idft_c,
        "bias": np.stack([natten_bias(a["rpb"][L]) for L in range(DEPTH)]),
        "rope": np.stack([np.cos(ang), np.sin(ang)], 1).astype(np.float32),
        "rot": rot,
        "alpha_w": alpha,
        "masks_f": np.concatenate([np.ones((128, 128), np.float32), eye, sign[:, None]], 1),
        "masks_b": np.concatenate([eye, left, right, starts, ends], 1).astype(ml_dtypes.bfloat16),
        "masks_u": np.concatenate([same & (i[:, None] <= i[None, :]), same & (i[:, None] >= i[None, :])], 1).astype(np.int32),
    }
    nc = bacc.Bacc("TRN2", target_bir_lowering=False, num_devices=1)
    sent, args = {}, []
    for name, v in arrays.items():
        v = np.ascontiguousarray(v)
        sent[f"in_{name}"] = v
        args.append(nc.dram_tensor(f"in_{name}", v.shape, mybir.dt.from_np(v.dtype), kind="ExternalInput").ap())
    args.append(nc.dram_tensor("x_mid", [128, KT, T], F32, kind="Internal").ap())
    args.append(nc.dram_tensor("v_mid", [DEPTH, SEQ, 512], F32, kind="Internal").ap())
    args.append(nc.dram_tensor("outT", [D_MODEL, SEQ], F32, kind="ExternalOutput").ap())
    build(nc, *args)
    r = run_bass_kernel_spmd(nc, [sent], core_ids=[0])
    return np.ascontiguousarray(r.results[0]["outT"].T)[None]
```

```python
import math
from contextlib import ExitStack

import numpy as np

import concourse.bass as bass
from concourse import mybir

F32 = mybir.dt.float32
F32R = mybir.dt.float32r
BF16 = mybir.dt.bfloat16
I32 = mybir.dt.int32
ALU = mybir.AluOpType
ACT = mybir.ActivationFunctionType
AX = mybir.AxisListType.X

D_MODEL, SEQ, CTX, DEPTH = 1024, 512, 256, 2
T = SEQ + CTX
KT = D_MODEL // 128
HD = 64
HEADS = 8
GRID_W, NKR, NKC = 64, 8, 16
BW = 512
EPS = 1e-6
NEG = -1e30
SLOTS = 6
WTILE = KT * 128
ROUND = 1.5 * 2.0 ** 23
TWO_PI_HI = 6.28125
TWO_PI_LO = 2.0 * math.pi - TWO_PI_HI
PI_IN = 3.1415925

WIDTHS = (512, 512, 512, 512, 512, 128, 128, 512, 256, 256, 512, 16, 16, 512, 1536, 512, 4096)
STARTS = np.concatenate([[0], np.cumsum(WIDTHS)]).astype(int)
(QA, KA, VA, GA, QB, KB, VB, GB, QG, KG, VG, LRF, LRB, GG, UH, GH, GM) = STARTS[:-1]

TILES = {
    "D": [("u", i, UH + 128 * i, False) for i in range(12)] + [("gd", i, GH + 128 * i, False) for i in range(4)],
    "C": [("lr", 0, LRF, True)] + [("kg", i, KG + 128 * i, True) for i in range(2)]
         + [("qg", i, QG + 128 * i, False) for i in range(2)] + [("vg", i, VG + 128 * i, True) for i in range(4)]
         + [("gg", i, GG + 128 * i, False) for i in range(4)],
    "A": [("ka", i, KA + 128 * i, True) for i in range(4)] + [("va", i, VA + 128 * i, True) for i in range(4)]
         + [("qa", i, QA + 128 * i, False) for i in range(4)] + [("ga", i, GA + 128 * i, False) for i in range(4)],
    "B": [("kb", 0, KB, True), ("vb", 0, VB, True)] + [("qb", i, QB, False) for i in range(4)]
         + [("gb", i, GB + 128 * i, False) for i in range(4)],
}
MIXERS = ("D", "C", "A", "B")
BRANCH = {"A": 0, "B": 1, "C": 2, "D": 3}
MOD_TILES = 3 * KT
BRANCH_TILES = 6
MOD_AT = {"start": [(0, m) for m in range(2 * KT)],
          "D": [(0, m) for m in range(2 * KT, MOD_TILES)] + [(1, m) for m in range(8)],
          "C": [(1, m) for m in range(8, 21)],
          "A": [(1, m) for m in range(21, MOD_TILES)]}


def tile_order():
    order = [("mod",) + lm for lm in MOD_AT["start"]]
    for L in range(DEPTH):
        for b in MIXERS:
            extra = MOD_AT.get(b, []) if L == 0 else []
            for i, ti in enumerate(TILES[b]):
                order.append(("proj", L) + ti[:2])
                if i < len(extra):
                    order.append(("mod",) + extra[i])
        for m in range(KT):
            order += [("gate", L, m, 0), ("gate", L, m, 1), ("branch", L, m, 0),
                      ("gate", L, m, 2), ("gate", L, m, 3), ("branch", L, m, 1)]
        order += [("proj", L, "out", m) for m in range(KT)]
    return order


ORDER = tile_order()
POS = {key: n for n, key in enumerate(ORDER)}
SPLITS = [key for key in ORDER if key[0] in ("proj", "gate")]
SPLIT_NO = {key: n for n, key in enumerate(SPLITS)}
NATTEN_COL0 = [min(max(j * NKC - NKC // 2, 0), GRID_W - 2 * NKC) for j in range(GRID_W // NKC)]

ARENA = 27904
Y_AT = {"D": 0, "C": 3072, "A": 6144, "B": 9216}
KSPEC, FWD, FWD_C, INV_C = 3072, 7168, 11264, 12288
INV = FWD
X_AT = 13312
HX0, HZ, HV = 13312, 16384, 19456
ZSPEC, HTMP = 22528, 26624
LR, GQ, GK, GV, GE, GS, GL, GAT = 6144, 6912, 8448, 9984, 13056, 17664, 20736, 23808
GR, GO = GL + 1536, (GL + 2304, 26880)
AQ, AK, AV, AVB, ABIAS, AP_, APT, AO = 9216, 12288, 15360, (15360, 16384, 18432, 19456), 20480, 24576, 25856, 27136
BQ, BK, BV, BROPE, BTMP = 12288, 15360, 16128, 16896, 17920
VT_AT = {"C": GL, "A": AP_, "B": BTMP + 3072}
NSQ, NRS = 19456, 25600
MACC, MGATE, MPROD = 19456, 25600, (12288, 27136)
FZE, FH0, FH1, FT, FABS = KSPEC, KSPEC + 512, KSPEC + 1024, KSPEC + 1536, KSPEC + 2048
FHF, FHB, FDEC = ZSPEC, ZSPEC + 2048, HV
FW, FWO = KSPEC + 3072, HTMP

P_NORM, P_BMOD, P_CW, P_CB, P_FB, P_BA, P_GN, P_FREQ, P_B1, P_B2, P_B3, P_SINK, P_FIN, P_C, P_W = (
    0, 8, 32, 68, 80, 84, 88, 89, 90, 91, 92, 93, 101, 109, 125)


MOD_COL = 7 * 512
VALUES = ("va", "vb", "vg")


def gate_place(v):
    return BRANCH_TILES * (v // 4) + (0, 1, 3, 4)[v % 4]


def build(nc, wstream, xT, params, zembT, filt_w, filt_wout, decay, dft, dft_c, idft, idft_c,
          bias, rope, rot, alpha_w, masks_f, masks_b, masks_u, x_mid, v_mid, out):
    with ExitStack() as ctx:
        def sb(name, shape, dt=F32):
            return ctx.enter_context(nc.sbuf_tensor(name, shape, dt))

        def sem(name):
            return ctx.enter_context(nc.semaphore(name))

        ar = sb("arena", [128, ARENA])
        h_hi = sb("h_hi", [128, KT, T], F32R)
        h_lo = sb("h_lo", [128, KT, T], F32R)
        ring = sb("ring", [128, SLOTS, WTILE])
        w_hi = sb("w_hi", [128, 2, KT, 128], F32R)
        w_lo = sb("w_lo", [128, 2, KT, 128], F32R)
        const_f = sb("const_f", [128, 257])
        ones, ident = const_f[:, 0:128], const_f[:, 128:256]
        ident_b = sb("ident_b", [128, 128], BF16)
        bmask = sb("bmask", [128, 2, 128], BF16)
        cmask = sb("cmask", [128, 2, T], BF16)
        umask = sb("umask", [128, 2, 128], I32)
        alt = const_f[:, 256:257]
        rotm = sb("rotm", [128, 128])
        aw = sb("aw", [32, 512])
        par = sb("par", [128, P_W])
        csil = sb("csil", [128, 8, 2])
        mod = sb("mod", [128, DEPTH, MOD_TILES, 2])
        nscale = sb("nscale", [128, 8, 2])
        stat = sb("stat", [128, 2, 4, 8])
        rmx = sb("rmx", [128, 4])
        gend = sb("gend", [128, 2, 12])
        pf = ctx.enter_context(nc.psum_tensor("psum", [128, 8 * 512], F32))

        def at(off, *shape):
            n = int(np.prod(shape))
            v = ar[:, off:off + n]
            if len(shape) == 1:
                return v
            names = "abcd"[:len(shape)]
            return v.rearrange(f"p ({' '.join(names)}) -> p {' '.join(names)}",
                               **{k: s for k, s in zip(names, shape)})

        y = {b: at(Y_AT[b], 4, T) for b in MIXERS}
        slot_tile = ring[:, :, :].rearrange("p s (k m) -> p s k m", k=KT)
        slot_br = ring[:, :, :].rearrange("p s (b k m) -> p s b k m", b=2, k=4)

        ring_full = [sem(f"ring_full{s}") for s in range(SLOTS)]
        ring_read = [sem(f"ring_read{s}") for s in range(SLOTS)]
        split_hi = sem("split_hi")
        const_in = sem("const_in")
        mask_in = sem("mask_in")
        first_in = sem("first_in")
        par_first = sem("par_first")
        par_in = sem("par_in")
        csil_ready = sem("csil_ready")
        mod_done = sem("mod_done")
        norm_t = sem("norm_t")
        h_high = sem("h_high")
        h_ready = sem("h_ready")
        v_tr = sem("v_tr")
        v_done = sem("v_done")
        dec_in = sem("dec_in")
        fwd_in = sem("fwd_in")
        dftc_in = sem("dftc_in")
        aw_in = sem("aw_in")
        x_in = sem("x_in")
        x_saved = sem("x_saved")
        tile_ready = sem("tile_ready")
        drained = [sem("drained0"), sem("drained1")]
        conv_ready = sem("conv_ready")
        dve_chain = sem("dve_chain")
        phase_done = sem("phase_done")
        filt_in = sem("filt_in")
        filt_pe = sem("filt_pe")
        filt_dve = sem("filt_dve")
        filt_act = sem("filt_act")
        norm_sq = sem("norm_sq")
        norm_ps = sem("norm_ps")
        norm_ms = sem("norm_ms")
        norm_rt = sem("norm_rt")
        dft_in = sem("dft_in")
        hy_z = sem("hy_z")
        hy_tr = sem("hy_tr")
        hy_ztok = sem("hy_ztok")
        hy_spec = sem("hy_spec")
        hy_zs = sem("hy_zs")
        hy_prod = sem("hy_prod")
        hy_inv = sem("hy_inv")
        hy_out = sem("hy_out")
        gl_alpha = sem("gl_alpha")
        gl_z = sem("gl_z")
        gl_ln = sem("gl_ln")
        gl_cum = sem("gl_cum")
        gl_rest = sem("gl_rest")
        gl_exp = sem("gl_exp")
        gl_ke = sem("gl_ke")
        gl_tr = sem("gl_tr")
        gl_ket = sem("gl_ket")
        gl_kv = sem("gl_kv")
        gl_state = sem("gl_state")
        gl_qk = sem("gl_qk")
        gl_at = sem("gl_at")
        gl_atc = sem("gl_atc")
        gl_o = sem("gl_o")
        gl_sq = sem("gl_sq")
        gl_ss = sem("gl_ss")
        gl_ms = sem("gl_ms")
        gl_rt = sem("gl_rt")
        gl_fin = sem("gl_fin")
        vblk_in = sem("vblk_in")
        v_out = sem("v_out")
        bias_in = [sem("bias_in0"), sem("bias_in1")]
        rope_in = sem("rope_in")
        rope_rot = sem("rope_rot")
        rope_done = sem("rope_done")
        at_s = sem("at_s")
        at_max = sem("at_max")
        at_p = sem("at_p")
        at_pt = sem("at_pt")
        at_ptc = [sem("at_ptc0"), sem("at_ptc1")]
        at_o = sem("at_o")
        at_sum = sem("at_sum")
        at_sink = sem("at_sink")
        at_on = sem("at_on")
        at_ot = sem("at_ot")
        at_y = sem("at_y")
        mg_unit = sem("mg_unit")
        mg_gate = sem("mg_gate")
        mg_prod = sem("mg_prod")
        mg_sum = sem("mg_sum")
        res_done = sem("res_done")
        out_dma = sem("out_dma")
        fin_sq = sem("fin_sq")

        tile_no = {key[1:]: n for n, key in enumerate(k for k in ORDER if k[0] == "proj")}

        def slot(key):
            return POS[key] % SLOTS

        def turns(key):
            return POS[key] // SLOTS + 1

        def wait_used(eng, key):
            if key[0] == "gate":
                eng.wait_ge(mg_unit, MG(key[1]) + 4 * key[2] + key[3] + 1)
            else:
                eng.wait_ge(tile_ready, tile_no[key[1:]] + 1)

        def next_split(key, ahead=2):
            n = SPLIT_NO[key] + ahead
            return n if n < len(SPLITS) else None

        def value_no(L, what, i):
            return 9 * L + {"vg": 0, "va": 4, "vb": 8}[what] + i

        mod_places = [p for p in ("start",) + MIXERS if p in MOD_AT]

        def width(L, needed):
            return T if L < DEPTH - 1 or needed else SEQ

        def pair(t):
            return (t % 2) * 1024

        def wait_tile(eng, L, name, i):
            t = tile_no[L, name, i]
            eng.wait_ge(drained[t % 2], t // 2 + 1)

        phase_list = [(L, name) for L in range(DEPTH) for name in ("filter", "D", "Dc", "C", "A", "B", "merge")
                      if name != "Dc" or L < DEPTH - 1]

        def PH(L, name):
            return phase_list.index((L, name)) + 1

        def barrier(eng, n):
            eng.drain().then_inc(phase_done, 1)
            eng.wait_ge(phase_done, 4 * n)

        def units(mixer, L):
            nq = 4 + (2 if L < DEPTH - 1 else 0)
            return [(q, i, p) for q in range(nq) for i in range(4) for p in range(2)]

        def head(mixer, i, p):
            return 2 * i + p if mixer == "A" else i + 4 * p

        def key_blocks(mixer, q):
            if q >= 4:
                return [4, 5]
            if mixer == "A":
                return [-1, -1, 4, 5]
            return [n for n in (q - 1, q, q + 1) if 0 <= n < 4] + [4, 5]

        unit0, u = {}, 0
        qt0, qn = {}, 0
        for L in range(DEPTH):
            for b in ("A", "B"):
                unit0[L, b] = u
                qt0[L, b] = qn
                u += len(units(b, L))
                qn += len(units(b, L)) // 8

        hy_runs = [(0, False), (0, True), (1, False)]
        HYN = {False: dict(nt=4, t0=0, n=SEQ), True: dict(nt=2, t0=4, n=CTX)}
        HYT = [HYN[is_c]["nt"] for _, is_c in hy_runs]

        def FD(run):
            return sum(7 + 4 * nt for nt in HYT[:run])

        def FA(run):
            return sum(3 + 2 * nt for nt in HYT[:run])

        def FP(run):
            return sum(4 + 6 * nt for nt in HYT[:run])

        def HZS(run):
            return sum(2 * nt for nt in HYT[:run])

        def HPR(run):
            return sum(HYT[:run])

        def FIN(run):
            return 48 * run

        def ZT(L):
            return 6 * L

        def QB(L):
            return 6 * L

        def MG(L):
            return 4 * KT * L

        def chunk_at(d, s):
            return 11 - s if d else (8 + s if s < 4 else s - 4)

        def state_slot(d, n):
            return 11 - n if d else (n + 4 if n < 8 else n - 8)

        block = ctx.enter_context(nc.Block())

        @block.sync
        def _(sp):
            sp.dma_start(at(FZE, 512)[0:33, :], zembT[:, 0:SEQ]).then_inc(first_in, 16)
            sp.dma_start(at(FW, 192)[0:64, :], filt_w[0]).then_inc(first_in, 16)
            sp.dma_start(par[:, :], params[0]).then_inc(par_first, 16)
            sp.dma_start(at(FWO, 1024)[0:64, :], filt_wout[0]).then_inc(first_in, 16)
            sp.dma_start(const_f[:, :], masks_f).then_inc(const_in, 16)
            for s in range(SLOTS):
                sp.dma_start(ring[:, s, :], wstream[s]).then_inc(ring_full[s], 16)
            with sp.Fori(1, len(ORDER) // SLOTS) as turn:
                for s in range(SLOTS):
                    sp.wait_ge(ring_read[s], turn)
                    sp.dma_start(ring[:, s, :], wstream[turn * SLOTS + s]).then_inc(ring_full[s], 16)
            for n in range(len(ORDER) - len(ORDER) % SLOTS, len(ORDER)):
                sp.wait_ge(ring_read[n % SLOTS], n // SLOTS)
                sp.dma_start(ring[:, n % SLOTS, :], wstream[n]).then_inc(ring_full[n % SLOTS], 16)

        @block.gpsimd
        def _(pool):
            def filter_inputs(L):
                if L:
                    pool.dma_start(par[:, :], params[L]).then_inc(par_in, 16)
                    pool.dma_start(at(FZE, 512)[0:33, :], zembT[:, 0:SEQ]).then_inc(filt_in, 16)
                    pool.dma_start(at(FW, 192)[0:64, :], filt_w[L]).then_inc(filt_in, 16)
                    pool.dma_start(at(FWO, 1024)[0:64, :], filt_wout[L]).then_inc(filt_in, 16)
                pool.dma_start(at(FDEC, 4, 512), decay[:, 0:4, :]).then_inc(dec_in, 16)
                pool.dma_start(at(FWD, 4, 1024), dft).then_inc(fwd_in, 16)
                pool.dma_start(aw[:, :], alpha_w[L]).then_inc(aw_in, 16)

            filter_inputs(0)
            pool.dma_start(at(X_AT, KT, T), xT).then_inc(x_in, 16)
            for dst, src in ((rotm[:, :], rot), (ident_b[:, :], masks_b[:, 0:128]),
                             (bmask[:, :, :], masks_b[:, 128:384].rearrange("p (a b) -> p a b", a=2)),
                             (cmask[:, :, :], masks_b[:, 384:384 + 2 * T].rearrange("p (a b) -> p a b", a=2)),
                             (umask[:, :, :], masks_u.rearrange("p (a b) -> p a b", a=2))):
                pool.dma_start(dst, src).then_inc(mask_in, 16)
            pool.dma_start(at(FWD_C, 2, 512), dft_c).then_inc(dftc_in, 16)
            pool.dma_start(at(INV_C, 4, 256), idft_c).then_inc(dftc_in, 16)
            for L in range(DEPTH):
                last = L == DEPTH - 1
                if L:
                    pool.dma_start(x_mid[:, :, 0:SEQ], at(X_AT, KT, T)[:, :, 0:SEQ]).then_inc(x_saved, 16)
                barrier(pool, PH(L, "filter"))
                pool.wait_ge(hy_spec, HZS(2 * L) + 8)
                pool.dma_start(at(INV, 8, 512), idft).then_inc(dft_in, 16)
                barrier(pool, PH(L, "D"))
                if not last:
                    pool.dma_start(at(FZE, 512)[0:33, 0:CTX], zembT[:, SEQ:T]).then_inc(filt_in, 16)
                    pool.dma_start(at(FW, 192)[0:64, :], filt_w[L]).then_inc(filt_in, 16)
                    pool.dma_start(at(FWO, 1024)[0:64, :], filt_wout[L]).then_inc(filt_in, 16)
                    pool.dma_start(at(FDEC, 4, 512)[:, 0:2, :], decay[:, 4:6, :]).then_inc(dec_in, 16)
                    barrier(pool, PH(L, "Dc"))
                barrier(pool, PH(L, "C"))
                for j in range(2):
                    pool.dma_start(at(ABIAS + 2048 * j, 8, 256), bias[L, j]).then_inc(bias_in[j], 16)
                pool.wait_ge(v_done, value_no(L, "va", 3) + 1)
                pool.dma_start(v_mid[L].rearrange("(t p) c -> p t c", p=128), at(AV, 6, 512)[:, 0:4, :]).then_inc(v_out, 16)
                pool.wait_ge(v_out, 16 * (L + 1))
                rows = v_mid[L].rearrange("(r c) f -> r c f", c=GRID_W)
                for j, c0 in enumerate(NATTEN_COL0):
                    for k in range(2):
                        for r in range(4):
                            pool.dma_start(at(AVB[j], 2, 512)[32 * r:32 * r + 32, k, :],
                                           rows[4 * k + r, c0:c0 + 32, :]).then_inc(vblk_in, 16)
                for j in range(2, 4):
                    pool.wait_ge(at_max, unit0[L, "A"] + 8 * (j - 1))
                    pool.dma_start(at(ABIAS + 2048 * (j % 2), 8, 256), bias[L, j]).then_inc(bias_in[j % 2], 16)
                barrier(pool, PH(L, "A"))
                pool.dma_start(at(BROPE, 2, 512), rope).then_inc(rope_in, 16)
                barrier(pool, PH(L, "B"))
                w = width(L, False)
                pool.dma_start(at(X_AT, KT, T)[:, :, 0:w], (x_mid if L else xT)[:, :, 0:w]).then_inc(x_in, 16)
                if not last:
                    pool.wait_ge(h_ready, 2 * KT * (L + 1))
                    filter_inputs(L + 1)
                barrier(pool, PH(L, "merge"))
            for k in range(KT):
                pool.wait_ge(res_done, k + 1)
                pool.dma_start(out[128 * k:128 * k + 128, :], at(MACC, KT, T)[:, k, 0:SEQ]).then_inc(out_dma, 16)
            pool.wait_ge(out_dma, 16 * KT)

        @block.tensor
        def _(pe):
            def mod_tile(L, m, place):
                key = ("mod", L, m)
                j = MOD_AT[place].index((L, m))
                if j == 0 and place != "start":
                    pe.wait_ge(mod_done, mod_places.index(place))
                pe.wait_ge(ring_full[slot(key)], 16 * turns(key))
                for k in range(KT):
                    mm = pe.matmul(pf[:, MOD_COL + 2 * j:MOD_COL + 2 * j + 2], slot_tile[:, slot(key), k, :], csil[:, k, :],
                                   start=(k == 0), stop=(k == KT - 1))
                mm.then_inc(ring_read[slot(key)], 1)

            def split_product(out, w, src, k, first, last):
                pe.matmul(out, w_hi[:, w, k, :], h_hi[:, k, src], start=first, stop=False)
                pe.matmul(out, w_hi[:, w, k, :], h_lo[:, k, src], start=False, stop=False)
                return pe.matmul(out, w_lo[:, w, k, :], h_hi[:, k, src], start=False, stop=last)

            def transpose_values(L, mixer, what, i):
                n = value_no(L, what, i)
                wait_tile(pe, L, what, i)
                if n:
                    pe.wait_ge(v_done, n)
                v = at(VT_AT[mixer] + T * (n % 2), T)
                for tt in range(6):
                    mm = pe.transpose(pf[:, 2048 + 128 * tt:2048 + 128 * tt + 128], v[:, 128 * tt:128 * tt + 128], ident[:, :])
                mm.then_inc(v_tr, 1)

            def project(L, mixer):
                extra = MOD_AT.get(mixer, []) if L == 0 else []
                turned = None
                for n, (what, i, _, need) in enumerate(TILES[mixer]):
                    key = ("proj", L, what, i)
                    t = tile_no[L, what, i]
                    pe.wait_ge(ring_read[slot(key)], turns(key))
                    if t >= 2:
                        pe.wait_ge(drained[t % 2], t // 2)
                    for c0, c1 in ((0, SEQ), (SEQ, width(L, need))):
                        if c1 == c0:
                            continue
                        for k in range(KT):
                            if n == 0 and mixer == "D" and c0 == 0:
                                pe.wait_ge(h_ready, 2 * KT * L + k + 1)
                            mm = split_product(pf[:, pair(t) + c0:pair(t) + c1], SPLIT_NO[key] % 2, slice(c0, c1), k,
                                               k == 0, k == KT - 1)
                    mm.then_inc(tile_ready, 1)
                    if turned:
                        transpose_values(L, mixer, *turned)
                    turned = (what, i) if what in VALUES else None
                    if n < len(extra):
                        mod_tile(*extra[n], mixer)
                if extra:
                    pe.wait_ge(mod_done, mod_places.index(mixer) + 1)

            def filter_net(c, run):
                nt, n = c["nt"], c["n"]
                base_d, base_a = FD(run), FA(run)
                pe.wait_ge(*((filt_in, FIN(run)) if run else (first_in, 48)))
                riders = MOD_AT["start"] if run == 0 else []

                def ride(a, b):
                    for lm in riders[a:b]:
                        mod_tile(*lm, "start")

                ze, w123 = at(FZE, 512), at(FW, 3, 64)
                for k in range(3):
                    src = (ze[0:33, 0:n], at(FH0, 512)[0:64, 0:n], at(FH1, 512)[0:64, 0:n])[k]
                    w = w123[0:33, 0, :] if k == 0 else w123[0:64, k, :]
                    if k:
                        ride(k - 1, k)
                        pe.wait_ge(filt_act, base_a + k)
                    pe.matmul(pf[0:64, 0:n], w, src, start=True, stop=True).then_inc(filt_pe, 1)
                ride(2, 3)
                pe.wait_ge(filt_act, base_a + 3)
                h3, wo = at(FH0, 512)[0:64, :], at(FWO, 1024)[0:64, :]
                for j in range(2 * nt):
                    if j >= 2:
                        pe.wait_ge(filt_dve, base_d + 3 + j - 1)
                    pe.matmul(pf[:, 512 * (1 + j % 2):512 * (2 + j % 2)], h3[:, 128 * (j // 2):128 * (j // 2) + 128],
                              wo[:, 512 * (j % 2):512 * (j % 2) + 512], start=True, stop=True).then_inc(filt_pe, 1)
                ride(3, 6)
                for j in range(2 * nt):
                    pe.wait_ge(filt_act, base_a + 3 + j + 1)
                    mm = pe.matmul(pf[:, 1536:2048], ones[:, :], at(FABS + 512 * (j % 2), 512),
                                   start=(j == 0), stop=(j == 2 * nt - 1), skip_group_check=True)
                    mm.then_inc(filt_pe, 1)
                pe.wait_ge(filt_dve, base_d + 3 + 2 * nt + 2)
                if nt == 4:
                    pe.wait_ge(fwd_in, 16 * (hy_runs[run][0] + 1))
                else:
                    pe.wait_ge(dftc_in, 32)
                fwd = at(FWD, 4, 1024) if nt == 4 else at(FWD_C, 2, 512)
                hs, hd = at(FDEC, 4, 512), at(FHB, 4, 512)
                for j in range(2 * nt):
                    if j >= 2:
                        pe.wait_ge(filt_dve, base_d + 3 + 2 * nt + 3 + j - 1)
                    src = hs if j < nt else hd
                    for t in range(nt):
                        mm = pe.matmul(pf[:, 512 * (4 + j % 2):512 * (5 + j % 2)], fwd[:, t, 128 * j:128 * j + 128],
                                       src[:, t, :], start=(t == 0), stop=(t == nt - 1))
                    mm.then_inc(filt_pe, 1)
                for t in range(nt):
                    mm = pe.matmul(pf[0:1, 0:512], alt[:, :], hs[:, t, :], start=(t == 0), stop=(t == nt - 1))
                mm.then_inc(filt_pe, 1)

            def norm(L):
                sq = at(NSQ, KT, T)
                for k in range(KT):
                    pe.wait_ge(norm_sq, KT * L + k + 1)
                    pe.matmul(pf[:, 0:SEQ], ones[:, :], sq[:, k, 0:SEQ], start=(k == 0), stop=(k == KT - 1))
                    mm = pe.matmul(pf[:, SEQ:T], ones[:, :], sq[:, k, SEQ:T], start=(k == 0), stop=(k == KT - 1))
                mm.then_inc(norm_ps, 1)

            def hyena(run):
                L, is_c = hy_runs[run]
                c = HYN[is_c]
                nt, n, t0 = c["nt"], c["n"], c["t0"]
                z, zt = at(HZ, 4, T), at(HV, 6, 512)
                zs = at(ZSPEC, 8, 512)
                fwd = at(FWD, 4, 1024) if nt == 4 else at(FWD_C, 2, 512)
                inv = at(INV, 8, 512) if nt == 4 else at(INV_C, 4, 256)
                if not is_c:
                    for j in range(6 if L < DEPTH - 1 else 4):
                        pe.wait_ge(hy_z, 4 * L + 4)
                        if j >= 2:
                            pe.wait_ge(hy_ztok, ZT(L) + j - 1)
                        for cc in range(4):
                            mm = pe.transpose(pf[:, 512 * (4 + j % 2) + 128 * cc:512 * (4 + j % 2) + 128 * cc + 128],
                                              z[:, cc, 128 * j:128 * j + 128], ident[:, :])
                        mm.then_inc(hy_tr, 1)
                    pe.wait_ge(hy_ztok, ZT(L) + (6 if L < DEPTH - 1 else 4))
                for j in range(2 * nt):
                    if j >= 2:
                        pe.wait_ge(hy_zs, HZS(run) + j - 1)
                    for t in range(nt):
                        mm = pe.matmul(pf[:, 512 * (6 + j % 2):512 * (7 + j % 2)], fwd[:, t, 128 * j:128 * j + 128],
                                       zt[:, t0 + t, :], start=(t == 0), stop=(t == nt - 1))
                    mm.then_inc(hy_spec, 1)
                pe.wait_ge(hy_prod, HPR(run) + nt)
                if not is_c:
                    pe.wait_ge(dft_in, 16 * (L + 1))
                for cc in range(4):
                    if cc >= 2:
                        pe.wait_ge(hy_out, 4 * run + cc - 1)
                    for j in range(2 * nt):
                        mm = pe.matmul(pf[:, 512 * (4 + cc % 2):512 * (4 + cc % 2) + n], zs[:, j, 128 * cc:128 * cc + 128],
                                       inv[:, j, :], start=(j == 0), stop=(j == 2 * nt - 1))
                    mm.then_inc(hy_inv, 1)

            def gla(L):
                oc = width(L, False)
                nto = oc // 128
                q, k, v = at(GQ, 2, T), at(GK, 2, T), at(GV, 6, 512)
                lr = at(LR, T)
                E = at(GE, 2, 3, T)
                S = at(GS, 2, 12, 128)
                A = at(GAT, 2, 2, T)
                wait_tile(pe, L, "gg", 3)
                wait_tile(pe, L, "gg", 2)
                pe.wait_ge(v_done, value_no(L, "vg", 3) + 1)
                pe.wait_ge(aw_in, 16 * (L + 1))
                for hp in range(2):
                    N = 2 * L + hp
                    if N:
                        pe.wait_ge(gl_fin, 2 * N)
                    for d in range(2):
                        c0 = 128 * (2 * d + hp)
                        pe.matmul(pf[:, 1024 * d:1024 * d + SEQ], aw[:, c0:c0 + 128], lr[0:32, 0:SEQ], start=True, stop=True)
                        pe.matmul(pf[:, 1024 * d + SEQ:1024 * d + T], aw[:, c0:c0 + 128], lr[0:32, SEQ:T],
                                  start=True, stop=True).then_inc(gl_alpha, 1)
                    for d in range(2):
                        pe.wait_ge(gl_ke, 2 * N + d + 1)
                        for tt in range(6):
                            mm = pe.transpose(pf[:, 1024 * d + 128 * tt:1024 * d + 128 * tt + 128],
                                              E[:, d, 2, 128 * tt:128 * tt + 128], ident[:, :])
                        mm.then_inc(gl_tr, 1)
                    pe.wait_ge(gl_ket, 2 * N + 2)
                    for d in range(2):
                        ket = E[:, d, 2, :].rearrange("p (t f) -> p t f", t=6)
                        base = 2048 if d == 0 else 0
                        for p in range(2):
                            for tt in range(6):
                                for e in range(2):
                                    rows = slice(64 * p, 64 * p + 64)
                                    mm = pe.matmul(pf[64 * e:64 * e + 64, base + 1024 * p + 128 * tt:base + 1024 * p + 128 * tt + 128],
                                                   ket[rows, tt, 64 * e:64 * e + 64],
                                                   v[rows, tt, 128 * (2 * hp + e):128 * (2 * hp + e) + 128],
                                                   start=True, stop=True)
                        mm.then_inc(gl_kv, 1)
                    for e in range(2):
                        rows = slice(64 * e, 64 * e + 64)
                        for d in range(2):
                            pe.wait_ge(gl_state, 2 * N + e + 1)
                            pe.wait_ge(gl_qk, 2 * N + d + 1)
                            base = (2048 if e == 0 else 0) + 1024 * d
                            for tt in range(nto):
                                mm = pe.matmul(pf[:, base + 128 * tt:base + 128 * tt + 128],
                                               E[rows, d, 1, 128 * tt:128 * tt + 128], E[rows, d, 0, 128 * tt:128 * tt + 128],
                                               start=True, stop=True)
                            mm.then_inc(gl_at, 1)
                    for e in range(2):
                        rows = slice(64 * e, 64 * e + 64)
                        base = 2048 if e == 0 else 0
                        vc = slice(128 * (2 * hp + e), 128 * (2 * hp + e) + 128)
                        pe.wait_ge(gl_atc, 4 * N + 2 * e + 2)
                        pe.wait_ge(gl_state, 2 * N + 2)
                        for tt in range(nto):
                            o = pf[:, base + 128 * tt:base + 128 * tt + 128]
                            pe.matmul(o, v[:, tt, vc], A[:, e, 0, 128 * tt:128 * tt + 128], start=True, stop=False)
                            pe.matmul(o, v[:, tt, vc], A[:, e, 1, 128 * tt:128 * tt + 128], start=False, stop=False)
                            for p in range(2):
                                for d in range(2):
                                    mm = pe.matmul(o[:, 64 * p:64 * p + 64], S[rows, d, state_slot(d, 2 * tt + p), :],
                                                   E[rows, d, 0, 128 * tt + 64 * p:128 * tt + 64 * p + 64],
                                                   start=False, stop=(p == 1 and d == 1))
                        mm.then_inc(gl_o, 1)
                    for e in range(2):
                        base = (2048 if e == 0 else 0) + 1024
                        pe.wait_ge(gl_sq, 2 * N + e + 1)
                        sq = at(GL, 2, T)[:, e, :]
                        for c0, c1 in ((0, SEQ), (SEQ, oc)):
                            if c1 > c0:
                                mm = pe.matmul(pf[:, base + c0:base + c1], ones[:, :], sq[:, c0:c1], start=True, stop=True)
                        mm.then_inc(gl_ss, 1)

            def rotary(L):
                for i in range(5):
                    wait_tile(pe, L, *(("qb", i) if i < 4 else ("kb", 0)))
                    if i >= 2:
                        pe.wait_ge(rope_done, 5 * L + i - 1)
                    src = at(BQ, 4, T)[:, i, 0:SEQ] if i < 4 else at(BK, T)[:, 0:SEQ]
                    pe.matmul(pf[:, 512 * (4 + i % 2):512 * (5 + i % 2)], rotm[:, :], src, start=True, stop=True)\
                        .then_inc(rope_rot, 1)

            def attention(L, mixer):
                A = mixer == "A"
                q_, k_ = (at(AQ, 4, T), at(AK, 4, T)) if A else (at(BQ, 4, T), at(BK, 1, T))
                v_ = at(AV, 6, 512) if A else at(BV, 6, 128)
                pt_at = APT if A else BTMP + 1280
                us = units(mixer, L)
                u0 = unit0[L, mixer]
                wait_tile(pe, L, "ga" if A else "gb", 3)
                wait_tile(pe, L, "ga" if A else "gb", 2)
                pe.wait_ge(v_done, value_no(L, "va" if A else "vb", 3 if A else 0) + 1)
                if not A:
                    pe.wait_ge(rope_done, 5 * (L + 1))

                def scores(n):
                    q, i, p = us[n]
                    rows = slice(64 * p, 64 * p + 64)
                    base = 1024 * p
                    if n >= 2:
                        pe.wait_ge(at_p, u0 + n - 1)
                    lhs = q_[rows, i, 128 * q:128 * q + 128]
                    ki = i if A else 0
                    blocks = key_blocks(mixer, q)
                    if A and q < 4:
                        c0 = NATTEN_COL0[q]
                        pe.matmul(pf[:, base:base + 256].rearrange("p (r c) -> p r c", c=2 * NKC), lhs,
                                  k_[rows, ki, 0:SEQ].rearrange("p (r c) -> p r c", c=GRID_W)[:, :, c0:c0 + 32],
                                  start=True, stop=True)
                        mm = pe.matmul(pf[:, base + 256:base + 512], lhs, k_[rows, ki, SEQ:T], start=True, stop=True)
                    elif q >= 4:
                        mm = pe.matmul(pf[:, base:base + 256], lhs, k_[rows, ki, SEQ:T], start=True, stop=True)
                    else:
                        for c, b in enumerate(blocks):
                            edge = b < 4 and b != q
                            mm = pe.matmul(pf[:, base + 128 * c:base + 128 * c + 128], lhs,
                                           k_[rows, ki, 128 * b:128 * b + 128], start=True, stop=not edge)
                            if edge:
                                mm = pe.matmul(pf[:, base + 128 * c:base + 128 * c + 128], ident_b[:, :],
                                               bmask[:, 0 if b < q else 1, :], start=False, stop=True)
                    mm.then_inc(at_s, 1)

                def transposes(n):
                    q, i, p = us[n]
                    P = at((AP_ if A else BTMP) + 640 * p, 640)
                    pe.wait_ge(at_p, u0 + n + 1)
                    if n >= 2:
                        pe.wait_ge(at_ptc[p], (u0 + n) // 2)
                    nb = len(key_blocks(mixer, q))
                    for c in range(min(nb, 4)):
                        mm = pe.transpose(pf[:, 2048 + 512 * p + 128 * c:2048 + 512 * p + 128 * c + 128],
                                          P[:, 128 * c:128 * c + 128], ident[:, :])
                    if nb == 5:
                        pe.wait_ge(at_ptc[1 - p], (u0 + n + 1) // 2)
                        mm = pe.transpose(pf[:, 3072:3200], P[:, 512:640], ident[:, :])
                    mm.then_inc(at_pt, 1)

                def values(n):
                    q, i, p = us[n]
                    hh = head(mixer, i, p)
                    PT = at(pt_at + 640 * p, 5, 128)
                    pe.wait_ge(at_ptc[p], (u0 + n) // 2 + 1)
                    if n == 0 and A:
                        pe.wait_ge(vblk_in, 16 * 32 * (L + 1))
                    if i == 0 and p == 0 and (n or (L, mixer) != (0, "A")):
                        pe.wait_ge(at_on, qt0[L, mixer] + q)
                    blocks = key_blocks(mixer, q)
                    for c, b in enumerate(blocks):
                        if A:
                            rhs = at(AVB[q % 4], 2, 512)[:, c % 2, 64 * hh:64 * hh + 64] if b < 0 else v_[:, b, 64 * hh:64 * hh + 64]
                        else:
                            rhs = v_[:, b, 64 * p:64 * p + 64]
                        mm = pe.matmul(pf[:, 3584 + 64 * hh:3584 + 64 * hh + 64], PT[:, c, :], rhs,
                                       start=(c == 0), stop=(c == len(blocks) - 1))
                    mm.then_inc(at_o, 1)

                def turn(q):
                    pe.wait_ge(at_on, qt0[L, mixer] + q + 1)
                    o = at(AO if A else BTMP + 2560, 512)
                    for f in range(4):
                        mm = pe.transpose(pf[:, 3072 + 128 * f:3072 + 128 * f + 128], o[:, 128 * f:128 * f + 128], ident[:, :])
                    mm.then_inc(at_ot, 1)

                scores(0)
                scores(1)
                for n in range(0, len(us), 2):
                    q = us[n][0]
                    transposes(n)
                    if n + 2 < len(us):
                        scores(n + 2)
                    transposes(n + 1)
                    if n + 3 < len(us):
                        scores(n + 3)
                    values(n)
                    values(n + 1)
                    if n % 8 == 6:
                        turn(q)
                        pe.wait_ge(at_y, qt0[L, mixer] + q + 1)

            def merge(L):
                g0, s0 = POS["gate", L, 0, 0], SPLIT_NO["gate", L, 0, 0]
                last = L == DEPTH - 1
                with pe.Fori(0, KT // 2) as it:
                    for v in range(8):
                        bi = v % 4
                        n = g0 + gate_place(v)
                        nb = g0 + BRANCH_TILES * (v // 4) + (2, 5)[bi // 2]
                        if bi % 2 == 0:
                            pe.wait_ge(ring_full[nb % SLOTS], 32 * it + 16 * (nb // SLOTS + 1))
                        pe.wait_ge(mg_prod, 8 * it + (MG(L) + v + 1))
                        src = y["ABCD"[bi]]
                        for c0, c1 in ((0, SEQ), (SEQ, T)):
                            if last and c0:
                                continue
                            for k in range(4):
                                mm = pe.matmul(pf[:, 2048 * (v % 2) + 1024 + c0:2048 * (v % 2) + 1024 + c1],
                                               slot_br[:, nb % SLOTS, bi % 2, k, :], src[:, k, c0:c1],
                                               start=(k == 0), stop=(k == 3))
                        if bi % 2 == 1:
                            mm.then_inc(ring_read[nb % SLOTS], 1)
                        pe.wait_ge(ring_read[n % SLOTS], 2 * it + (n // SLOTS + 1))
                        for c0, c1 in ((0, SEQ), (SEQ, T)):
                            if last and c0:
                                continue
                            for k in range(KT):
                                mm = split_product(pf[:, 2048 * (v % 2) + c0:2048 * (v % 2) + c1], (s0 + v) % 2,
                                                   slice(c0, c1), k, k == 0, k == KT - 1)
                        mm.then_inc(mg_unit, 1)
                for m in range(KT):
                    key = ("proj", L, "out", m)
                    t = tile_no[L, "out", m]
                    pe.wait_ge(ring_read[slot(key)], turns(key))
                    if m >= 2:
                        pe.wait_ge(drained[t % 2], t // 2)
                    for c0, c1 in ((0, SEQ), (SEQ, T)):
                        if last and c0:
                            continue
                        for k in range(KT):
                            if m == 0 and c0 == 0:
                                pe.wait_ge(h_ready, KT * (2 * L + 1) + k + 1)
                            mm = split_product(pf[:, pair(t) + c0:pair(t) + c1], SPLIT_NO[key] % 2, slice(c0, c1), k,
                                               k == 0, k == KT - 1)
                    mm.then_inc(tile_ready, 1)

            pe.wait_ge(csil_ready, 1)
            pe.wait_ge(const_in, 16)
            for L in range(DEPTH):
                filter_net(HYN[False], 2 * L)
                barrier(pe, PH(L, "filter"))
                norm(L)
                if L == 0:
                    for lm in MOD_AT["start"][6:]:
                        mod_tile(*lm, "start")
                    pe.wait_ge(mask_in, 16 * 5)
                project(L, "D")
                hyena(2 * L)
                barrier(pe, PH(L, "D"))
                if L < DEPTH - 1:
                    filter_net(HYN[True], 2 * L + 1)
                    hyena(2 * L + 1)
                    barrier(pe, PH(L, "Dc"))
                project(L, "C")
                gla(L)
                barrier(pe, PH(L, "C"))
                project(L, "A")
                attention(L, "A")
                barrier(pe, PH(L, "A"))
                project(L, "B")
                rotary(L)
                attention(L, "B")
                barrier(pe, PH(L, "B"))
                merge(L)
                barrier(pe, PH(L, "merge"))
            for k in range(KT):
                pe.wait_ge(fin_sq, k + 1)
                mm = pe.matmul(pf[:, 0:SEQ], ones[:, :], at(NSQ, KT, T)[:, k, 0:SEQ], start=(k == 0), stop=(k == KT - 1))
            mm.then_inc(norm_ps, 1)

        @block.scalar
        def _(act):
            def high_part(n):
                key = SPLITS[n]
                act.wait_ge(ring_full[slot(key)], 16 * turns(key))
                act.activation(w_hi[:, n % 2], slot_tile[:, slot(key)], ACT.Copy).then_inc(split_hi, 1)

            def drain_tile(L, name, i, need, dst, func, scale=1.0, rows=128):
                t = tile_no[L, name, i]
                w = width(L, need)
                act.wait_ge(tile_ready, t + 1)
                src = pf[0:rows, pair(t):pair(t) + w]
                act.activation(dst, src, func, scale=scale).then_inc(drained[t % 2], 1)

            def drain(L, mixer):
                for what, i, _, need in TILES[mixer]:
                    key = ("proj", L, what, i)
                    wait_used(act, key)
                    high_part(next_split(key))
                    w = width(L, need)
                    if what == "u":
                        t = tile_no[L, what, i]
                        dst = (at(HX0, 4, T), at(HZ, 4, T), at(HV, 4, T))[i // 4][:, i % 4, 0:w]
                        act.wait_ge(tile_ready, t + 1)
                        act.activation(dst, pf[:, pair(t):pair(t) + w], ACT.Identity,
                                       scale=par[:, P_CW + 12 + i:P_CW + 13 + i],
                                       bias=par[:, P_CB + i:P_CB + i + 1]).then_inc(conv_ready, 1)
                    elif what in ("gd", "gg", "ga", "gb"):
                        drain_tile(L, what, i, need, y[mixer][:, i, 0:w], ACT.Silu)
                    elif what == "lr":
                        drain_tile(L, what, i, need, at(LR, T)[0:32, 0:w], ACT.Copy, rows=32)
                    elif what in VALUES:
                        drain_tile(L, what, i, need, at(VT_AT[mixer] + T * (value_no(L, what, i) % 2), T), ACT.Copy)
                    elif what == "qa":
                        t = tile_no[L, what, i]
                        q = at(AQ + T * i, T)
                        act.wait_ge(tile_ready, t + 1)
                        ins = act.activation(q[:, 0:SEQ].rearrange("p (j r c) -> p r j c", r=8, c=NKC),
                                             pf[:, pair(t):pair(t) + SEQ].rearrange("p (r j c) -> p r j c", r=8, c=NKC),
                                             ACT.Copy, scale=HD ** -0.5)
                        if w > SEQ:
                            ins = act.activation(q[:, SEQ:T], pf[:, pair(t) + SEQ:pair(t) + T], ACT.Copy, scale=HD ** -0.5)
                        ins.then_inc(drained[t % 2], 1)
                    else:
                        off = {"ka": AK, "qb": BQ, "kb": BK, "qg": GQ, "kg": GK}[what]
                        drain_tile(L, what, i, need, at(off + T * i, T)[:, 0:w], ACT.Copy,
                                   scale=HD ** -0.5 if what[0] == "q" else 1.0)

            def filter_net(c, run):
                nt, n = c["nt"], c["n"]
                bd = FD(run)
                for k in range(3):
                    act.wait_ge(filt_dve, bd + k + 1)
                    dst = at((FH0, FH1, FH0)[k], 512)[0:64, 0:n]
                    act.activation(dst, at(FT, 512)[0:64, 0:n], ACT.Sin).then_inc(filt_act, 1)
                for j in range(2 * nt):
                    act.wait_ge(filt_dve, bd + 3 + 2 * nt)
                    if j >= 2:
                        act.wait_ge(filt_pe, FP(run) + 3 + 2 * nt + j - 1)
                    src = at(FHF if j % 2 == 0 else FHB, 4, 512)[:, j // 2, :]
                    act.activation(at(FABS + 512 * (j % 2), 512), src, ACT.Abs).then_inc(filt_act, 1)

            def norm(L, x):
                for k in range(KT):
                    act.activation(at(NSQ, KT, T)[:, k, :], x[:, k, :], ACT.Square).then_inc(norm_sq, 1)
                act.wait_ge(norm_ms, L + 1)
                act.activation(at(NRS, T), at(NRS, T), ACT.Sqrt).then_inc(norm_rt, 1)
                for k in range(KT):
                    act.wait_ge(norm_t, KT * L + k + 1)
                    for c, (c0, c1) in enumerate(((0, SEQ), (SEQ, T))):
                        ins = act.activation(h_hi[:, k, c0:c1], x[:, k, c0:c1], ACT.Identity, bias=mod[:, L, k, c:c + 1])
                    ins.then_inc(h_high, 1)

            def hyena(run):
                L, is_c = hy_runs[run]
                c = HYN[is_c]
                if not is_c:
                    for j in range(6 if L < DEPTH - 1 else 4):
                        act.wait_ge(hy_tr, ZT(L) + j + 1)
                        act.activation(at(HV, 6, 512)[:, j, :], pf[:, 512 * (4 + j % 2):512 * (5 + j % 2)], ACT.Copy)\
                            .then_inc(hy_ztok, 1)
                if is_c:
                    act.wait_ge(filt_dve, FD(run + 1))
                for j in range(2 * c["nt"]):
                    act.wait_ge(hy_spec, HZS(run) + j + 1)
                    act.activation(at(ZSPEC, 8, 512)[:, j, :], pf[:, 512 * (6 + j % 2):512 * (7 + j % 2)], ACT.Copy)\
                        .then_inc(hy_zs, 1)

            def gla(L):
                oc = width(L, False)
                E = at(GE, 2, 3, T)
                for hp in range(2):
                    N = 2 * L + hp
                    for d in range(2):
                        zb, lb = at(GL + 1536 * d, T), at(GL + 1536 * d + T, T)
                        act.wait_ge(gl_z, 2 * N + d + 1)
                        act.activation(lb, zb, ACT.Abs).then_inc(gl_ln, 1)
                        act.wait_ge(gl_ln, 6 * N + 3 * d + 1)
                        act.activation(lb, lb, ACT.Exp, scale=-1.0).then_inc(gl_ln, 1)
                        act.wait_ge(gl_ln, 6 * N + 3 * d + 2)
                        act.activation(lb, lb, ACT.Ln, bias=1.0).then_inc(gl_ln, 1)
                    for d in range(2):
                        zb, lb = at(GL + 1536 * d, T), at(GL + 1536 * d + T, T)
                        act.wait_ge(gl_cum, 2 * N + d + 1)
                        act.activation(E[:, d, 0, :], lb, ACT.Exp, scale=1.0 / 16)
                        act.activation(E[:, d, 1, :], lb, ACT.Exp, scale=-1.0 / 16)
                        act.wait_ge(gl_rest, 2 * N + d + 1)
                        act.activation(E[:, d, 2, :], zb, ACT.Exp, scale=1.0 / 16).then_inc(gl_exp, 1)
                    for d in range(2):
                        act.wait_ge(gl_tr, 2 * N + d + 1)
                        act.activation(E[:, d, 2, :], pf[:, 1024 * d:1024 * d + T], ACT.Copy).then_inc(gl_ket, 1)
                    for e in range(2):
                        base = 2048 if e == 0 else 0
                        act.wait_ge(gl_o, 2 * N + e + 1)
                        act.activation(at(GO[e], T)[:, 0:oc], pf[:, base:base + oc], ACT.Copy)
                        act.activation(at(GL, 2, T)[:, e, 0:oc], pf[:, base:base + oc], ACT.Square).then_inc(gl_sq, 1)
                    for e in range(2):
                        act.wait_ge(gl_ms, 2 * N + e + 1)
                        r = at(GR, T)[:, 0:oc]
                        act.activation(r, r, ACT.Sqrt).then_inc(gl_rt, 1)

            def attention(L, mixer):
                A = mixer == "A"
                us = units(mixer, L)
                u0 = unit0[L, mixer]
                p_at = AP_ if A else BTMP
                pt_at = APT if A else BTMP + 1280

                def exps(n):
                    q, i, p = us[n]
                    w = 128 * len(key_blocks(mixer, q))
                    hh = head(mixer, i, p)
                    act.wait_ge(at_max, u0 + n + 1)
                    if n >= 2:
                        act.wait_ge(at_pt, u0 + n - 1)
                    if hh == 0 and q >= 2:
                        act.wait_ge(at_on, qt0[L, mixer] + q - 1)
                    act.activation(at(p_at + 640 * p, 640)[:, 0:w], pf[:, 1024 * p:1024 * p + w], ACT.Exp,
                                   bias=stat[:, q % 2, 0, hh:hh + 1],
                                   accum_out=stat[:, q % 2, 1, hh:hh + 1]).then_inc(at_p, 1)

                def copies(n):
                    q, i, p = us[n]
                    nb = len(key_blocks(mixer, q))
                    act.wait_ge(at_pt, u0 + n + 1)
                    if n >= 2:
                        act.wait_ge(at_o, u0 + n - 1)
                    PT = at(pt_at + 640 * p, 640)
                    w = 128 * min(nb, 4)
                    ins = act.activation(PT[:, 0:w], pf[:, 2048 + 512 * p:2048 + 512 * p + w], ACT.Copy)
                    if nb == 5:
                        ins = act.activation(PT[:, 512:640], pf[:, 3072:3200], ACT.Copy)
                    ins.then_inc(at_ptc[1], 1)

                exps(0)
                exps(1)
                for n in range(0, len(us), 2):
                    if n + 2 < len(us):
                        exps(n + 2)
                    copies(n + 1)
                    if n + 3 < len(us):
                        exps(n + 3)
                    if mixer == "B" and n % 8 == 6:
                        q = us[n][0]
                        act.wait_ge(at_sum, QB(L) + q + 1)
                        act.activation(stat[:, q % 2, 3, :], stat[:, q % 2, 3, :], ACT.Exp).then_inc(at_sink, 1)

            def merge(L):
                w = width(L, False)
                g0, s0 = POS["gate", L, 0, 0], SPLIT_NO["gate", L, 0, 0]
                with act.Fori(0, KT // 2) as it:
                    for v in range(8):
                        act.wait_ge(mg_unit, 8 * it + (MG(L) + v + 1))
                        act.wait_ge(mg_prod, 8 * it + (MG(L) + v + 1))
                        act.activation(at(MGATE + T * (v % 2), T)[:, 0:w], pf[:, 2048 * (v % 2):2048 * (v % 2) + w],
                                       ACT.Sigmoid).then_inc(mg_gate, 1)
                        n = g0 + gate_place(v + 2)
                        act.wait_ge(ring_full[n % SLOTS], 32 * it + 16 * (n // SLOTS + 1))
                        act.activation(w_hi[:, (s0 + v) % 2], slot_tile[:, n % SLOTS], ACT.Copy).then_inc(split_hi, 1)
                act.wait_ge(mg_sum, 3 * KT * (L + 1))
                for k in range(KT):
                    act.activation(h_hi[:, k, 0:w], at(MACC, KT, T)[:, k, 0:w], ACT.Copy).then_inc(h_high, 1)
                for m in range(KT):
                    key = ("proj", L, "out", m)
                    if next_split(key) is not None:
                        wait_used(act, key)
                        high_part(next_split(key))

            act.wait_ge(par_first, 16)
            act.activation(csil[:, :, :], par[:, P_C:P_C + 16].rearrange("p (k c) -> p k c", c=2), ACT.Silu)\
                .then_inc(csil_ready, 1)
            for L in range(DEPTH):
                filter_net(HYN[False], 2 * L)
                barrier(act, PH(L, "filter"))
                if L == 0:
                    act.wait_ge(x_in, 16)
                norm(L, at(X_AT, KT, T))
                if L == 0:
                    high_part(0)
                    high_part(1)
                drain(L, "D")
                hyena(2 * L)
                barrier(act, PH(L, "D"))
                if L < DEPTH - 1:
                    filter_net(HYN[True], 2 * L + 1)
                    hyena(2 * L + 1)
                    barrier(act, PH(L, "Dc"))
                drain(L, "C")
                gla(L)
                barrier(act, PH(L, "C"))
                drain(L, "A")
                attention(L, "A")
                barrier(act, PH(L, "A"))
                drain(L, "B")
                attention(L, "B")
                barrier(act, PH(L, "B"))
                merge(L)
                barrier(act, PH(L, "merge"))
            for k in range(KT):
                act.activation(at(NSQ, KT, T)[:, k, 0:SEQ], at(X_AT, KT, T)[:, k, 0:SEQ], ACT.Square).then_inc(fin_sq, 1)
            act.wait_ge(norm_ms, DEPTH + 1)
            act.activation(at(MGATE, SEQ), at(MGATE, SEQ), ACT.Sqrt).then_inc(norm_rt, 1)

        @block.vector
        def _(dve):
            chain = [0]

            def link(ins):
                chain[0] += 1
                ins.then_inc(dve_chain, 1)
                dve.wait_ge(dve_chain, chain[0])

            def filter_net(c, run):
                nt, n = c["nt"], c["n"]
                ba, bp = FA(run), FP(run)
                t, r = at(FT, 512)[0:64, 0:n], at(FABS, 512)[0:64, 0:n]
                for k in range(3):
                    dve.wait_ge(filt_pe, bp + k + 1)
                    if k:
                        dve.wait_ge(filt_act, ba + k)
                    link(dve.tensor_scalar(t, pf[0:64, 0:n], par[0:64, P_B1 + k:P_B1 + k + 1], par[0:64, P_FREQ:P_FREQ + 1],
                                           ALU.add, ALU.mult))
                    link(dve.tensor_scalar(r, t, 1.0 / (2.0 * math.pi), ROUND, ALU.mult, ALU.add))
                    link(dve.tensor_scalar(r, r, ROUND, None, ALU.subtract))
                    link(dve.scalar_tensor_tensor(t, r, -TWO_PI_HI, t, ALU.mult, ALU.add))
                    link(dve.scalar_tensor_tensor(t, r, -TWO_PI_LO, t, ALU.mult, ALU.add))
                    dve.tensor_scalar(t, t, PI_IN, -PI_IN, ALU.min, ALU.max).then_inc(filt_dve, 1)
                dec = at(FDEC, 4, 512)
                hf, hb = at(FHF, 4, 512), at(FHB, 4, 512)
                dve.wait_ge(dec_in, 16 * (run + 1))
                for j in range(2 * nt):
                    dve.wait_ge(filt_pe, bp + 3 + j + 1)
                    dst = (hf, hb)[j % 2][:, j // 2, :]
                    ins = dve.tensor_tensor(dst, pf[:, 512 * (1 + j % 2):512 * (2 + j % 2)], dec[:, j // 2, :], ALU.mult)
                    if j == 1:
                        link(ins)
                        ins = dve.memset(hb[0:1, 0, :], 0.0)
                    ins.then_inc(filt_dve, 1)
                dve.wait_ge(filt_act, ba + 3 + 2 * nt)
                dve.wait_ge(filt_dve, FD(run) + 3 + 2 * nt)
                dve.tensor_tensor(dec[:, 0:nt, :], hf[:, 0:nt, :], hb[:, 0:nt, :], ALU.add).then_inc(filt_dve, 1)
                dve.wait_ge(filt_dve, FD(run) + 3 + 2 * nt + 1)
                dve.tensor_tensor(hb[:, 0:nt, :], hf[:, 0:nt, :], hb[:, 0:nt, :], ALU.subtract).then_inc(filt_dve, 1)
                dve.wait_ge(filt_pe, bp + 3 + 4 * nt)
                rl = at(FHF, 512)
                dve.wait_ge(filt_dve, FD(run) + 3 + 2 * nt + 2)
                dve.reciprocal(rl, pf[:, 1536:2048]).then_inc(filt_dve, 1)
                dve.wait_ge(filt_dve, FD(run) + 3 + 2 * nt + 3)
                ks = at(KSPEC, 8, 512)
                for j in range(2 * nt):
                    dve.wait_ge(filt_pe, bp + 3 + 4 * nt + j + 1)
                    dve.tensor_tensor(ks[:, j, :], pf[:, 512 * (4 + j % 2):512 * (5 + j % 2)], rl, ALU.mult)\
                        .then_inc(filt_dve, 1)
                dve.wait_ge(filt_pe, bp + 3 + 6 * nt + 1)
                dve.wait_ge(filt_dve, FD(run) + 3 + 4 * nt + 3)
                dve.tensor_tensor(ks[0:1, nt, :], pf[0:1, 0:512], rl[0:1, :], ALU.mult).then_inc(filt_dve, 1)

            def low_part(n):
                key = SPLITS[n]
                dve.wait_ge(split_hi, n + 1)
                dve.tensor_tensor(w_lo[:, n % 2], slot_tile[:, slot(key)], w_hi[:, n % 2].bitcast(F32), ALU.subtract)\
                    .then_inc(ring_read[slot(key)], 1)

            def modulation(place):
                key = ("mod",) + MOD_AT[place][-1]
                dve.wait_ge(ring_read[slot(key)], turns(key))
                for L in range(DEPTH):
                    ms = [m for l, m in MOD_AT[place] if l == L]
                    if ms:
                        c0 = MOD_COL + 2 * MOD_AT[place].index((L, ms[0]))
                        ins = dve.tensor_copy(mod[:, L, ms[0]:ms[-1] + 1, :],
                                              pf[:, c0:c0 + 2 * len(ms)].rearrange("p (m c) -> p m c", c=2))
                ins.then_inc(mod_done, 1)
                dve.wait_ge(mod_done, mod_places.index(place) + 1)

            def add_bias(L, m0, m1):
                for c in range(2):
                    link(dve.tensor_tensor(mod[:, L, m0:m1, c], mod[:, L, m0:m1, c], par[:, P_BMOD + m0:P_BMOD + m1], ALU.add))

            def norm(L, x):
                rstd = at(NRS, T)
                dve.wait_ge(norm_ps, L + 1)
                link(dve.tensor_scalar(rstd, pf[:, 0:T], 1.0 / D_MODEL, EPS, ALU.mult, ALU.add))
                dve.reciprocal(rstd, rstd).then_inc(norm_ms, 1)
                if L == 0:
                    modulation("start")
                add_bias(L, 0, 2 * KT if L == 0 else MOD_TILES)
                for c in range(2):
                    link(dve.scalar_tensor_tensor(nscale[:, :, c], mod[:, L, KT:2 * KT, c], 1.0, par[:, P_NORM:P_NORM + KT],
                                                  ALU.add, ALU.mult))
                dve.wait_ge(norm_rt, L + 1)
                if L:
                    dve.wait_ge(x_saved, 16 * L)
                for k in range(KT):
                    for c, (c0, c1) in enumerate(((0, SEQ), (SEQ, T))):
                        ins = dve.scalar_tensor_tensor(x[:, k, c0:c1], x[:, k, c0:c1], nscale[:, k, c:c + 1], rstd[:, c0:c1],
                                                       ALU.mult, ALU.mult)
                    ins.then_inc(norm_t, 1)
                for k in range(KT):
                    dve.wait_ge(h_high, 2 * KT * L + k + 1)
                    for c, (c0, c1) in enumerate(((0, SEQ), (SEQ, T))):
                        ins = dve.scalar_tensor_tensor(h_lo[:, k, c0:c1], x[:, k, c0:c1], mod[:, L, k, c:c + 1],
                                                       h_hi[:, k, c0:c1].bitcast(F32), ALU.add, ALU.subtract)
                    ins.then_inc(h_ready, 1)
                if L == 0:
                    low_part(0)
                    low_part(1)

            def conv(L, i):
                segs = ((0, SEQ), (SEQ, T))[:2 if L < DEPTH - 1 else 1]
                t = tile_no[L, "u", i]
                dst = (at(HX0, 4, T), at(HZ, 4, T), at(HV, 4, T))[i // 4][:, i % 4, :]
                src = pf[:, pair(t):pair(t) + T]
                dve.wait_ge(conv_ready, 12 * L + i + 1)
                for c0, c1 in segs:
                    ins = dve.scalar_tensor_tensor(dst[:, c0 + 1:c1], src[:, c0:c1 - 1], par[:, P_CW + i:P_CW + i + 1],
                                                   dst[:, c0 + 1:c1], ALU.mult, ALU.add)
                link(ins)
                for c0, c1 in segs:
                    ins = dve.scalar_tensor_tensor(dst[:, c0:c1 - 1], src[:, c0 + 1:c1], par[:, P_CW + 24 + i:P_CW + 25 + i],
                                                   dst[:, c0:c1 - 1], ALU.mult, ALU.add)
                ins.then_inc(drained[t % 2], 1)

            def project(L, mixer):
                tiles = TILES[mixer]
                w = width(L, False)

                def values(what, i):
                    n = value_no(L, what, i)
                    dst = {"vg": at(GV, 6, 512), "va": at(AV, 6, 512), "vb": at(BV, 6, 128)}[what]
                    dve.wait_ge(v_tr, n + 1)
                    dve.tensor_copy(dst[:, :, 128 * i:128 * i + 128], pf[:, 2048:2048 + T].rearrange("p (t f) -> p t f", f=128))\
                        .then_inc(v_done, 1)

                for j, (what, i, _, _) in enumerate(tiles):
                    low_part(next_split(("proj", L, what, i)))
                    if what == "u":
                        conv(L, i)
                    if what == "gd":
                        if i == 0:
                            for last in (10, 11):
                                t = tile_no[L, "u", last]
                                dve.wait_ge(drained[t % 2], t // 2 + 1)
                        z = at(HZ, 4, T)[:, i, 0:w]
                        dve.tensor_tensor(z, z, at(HV, 4, T)[:, i, 0:w], ALU.mult).then_inc(hy_z, 1)
                    if j >= 2 and tiles[j - 2][0] in VALUES:
                        values(*tiles[j - 2][:2])
                if L == 0 and mixer in MOD_AT:
                    modulation(mixer)
                    if mixer == "D":
                        add_bias(0, 2 * KT, MOD_TILES)

            def hyena(run):
                L, is_c = hy_runs[run]
                c = HYN[is_c]
                nt, n, c0 = c["nt"], c["n"], 128 * c["t0"]
                ks, zs = at(KSPEC, 8, 512), at(ZSPEC, 8, 512)
                t1, t2 = at(HTMP, 512), at(HTMP + 512, 512)
                for j in range(nt):
                    zc, zn, kc, kn = zs[:, j, :], zs[:, nt + j, :], ks[:, j, :], ks[:, nt + j, :]
                    dve.wait_ge(hy_zs, HZS(run) + nt + j + 1)
                    dve.tensor_tensor(t1, zn, kn, ALU.mult)
                    link(dve.tensor_tensor(t2, zn, kc, ALU.mult))
                    link(dve.tensor_tensor(zn, zc, kn, ALU.mult))
                    dve.tensor_tensor(zn, zn, t2, ALU.add)
                    link(dve.tensor_tensor(zc, zc, kc, ALU.mult))
                    if j == 0:
                        link(dve.tensor_copy(zn[0:1, :], t1[0:1, :]))
                        link(dve.memset(t1[0:1, :], 0.0))
                    dve.tensor_tensor(zc, zc, t1, ALU.subtract).then_inc(hy_prod, 1)
                    dve.wait_ge(hy_prod, HPR(run) + j + 1)
                if not is_c:
                    wait_tile(dve, L, "gd", 3)
                    wait_tile(dve, L, "gd", 2)
                x0, z = at(HX0, 4, T), at(HZ, 4, T)
                for cc in range(4):
                    dve.wait_ge(hy_inv, 4 * run + cc + 1)
                    zz, xx, yy = z[:, cc, c0:c0 + n], x0[:, cc, c0:c0 + n], y["D"][:, cc, c0:c0 + n]
                    dve.scalar_tensor_tensor(zz, zz, par[:, P_FB + cc:P_FB + cc + 1],
                                             pf[:, 512 * (4 + cc % 2):512 * (4 + cc % 2) + n], ALU.mult, ALU.add)\
                        .then_inc(hy_out, 1)
                    dve.wait_ge(hy_out, 4 * run + cc + 1)
                    link(dve.tensor_tensor(yy, yy, xx, ALU.mult))
                    link(dve.tensor_tensor(yy, yy, zz, ALU.mult))

            def gla(L):
                oc = width(L, False)
                q, k = at(GQ, 2, T), at(GK, 2, T)
                E = at(GE, 2, 3, T)
                S = at(GS, 2, 12, 128)
                A = at(GAT, 2, 2, T)
                link(dve.memset(A, 0.0))
                link(dve.memset(S[:, :, 0, :], 0.0))
                wait_tile(dve, L, "gg", 3)
                wait_tile(dve, L, "gg", 2)
                for hp in range(2):
                    N = 2 * L + hp
                    for d in range(2):
                        zb, lb = at(GL + 1536 * d, T), at(GL + 1536 * d + T, T)
                        dve.wait_ge(gl_alpha, 2 * N + d + 1)
                        dve.tensor_scalar(zb, pf[:, 1024 * d:1024 * d + T], par[:, P_BA + 2 * d + hp:P_BA + 2 * d + hp + 1], None,
                                          ALU.add).then_inc(gl_z, 1)
                    for d in range(2):
                        zb, lb = at(GL + 1536 * d, T), at(GL + 1536 * d + T, T)
                        dve.wait_ge(gl_ln, 6 * N + 3 * d + 3)
                        link(dve.scalar_tensor_tensor(zb, zb, 0.0, lb, ALU.min, ALU.subtract))
                        if d == 0:
                            dve.tensor_tensor_scan(lb, cmask[:, 0, :], zb, 0.0, ALU.mult, ALU.add).then_inc(gl_cum, 1)
                        else:
                            dve.tensor_tensor_scan(lb[:, ::-1], cmask[:, 1, ::-1], zb[:, ::-1], 0.0, ALU.mult, ALU.add)\
                                .then_inc(gl_cum, 1)
                        dve.wait_ge(gl_cum, 2 * N + d + 1)
                        l3 = lb.rearrange("p (n c) -> p n c", c=64)
                        end = l3[:, :, 63:64] if d == 0 else l3[:, :, 0:1]
                        dve.tensor_tensor(zb.rearrange("p (n c) -> p n c", c=64), end.to_broadcast([128, 12, 64]), l3,
                                          ALU.subtract).then_inc(gl_rest, 1)
                    for d in range(2):
                        dve.wait_ge(gl_exp, 2 * N + d + 1)
                        e3 = E[:, d, 0, :].rearrange("p (n c) -> p n c", c=64)
                        dve.tensor_tensor(E[:, d, 2, :], E[:, d, 2, :], k[:, hp, :], ALU.mult).then_inc(gl_ke, 1)
                        dve.tensor_tensor(E[:, d, 1, :], E[:, d, 1, :], k[:, hp, :], ALU.mult)
                        link(dve.tensor_copy(gend[:, d, :], e3[:, :, 63 if d == 0 else 0]))
                        dve.tensor_tensor(E[:, d, 0, 0:oc], E[:, d, 0, 0:oc], q[:, hp, 0:oc], ALU.mult).then_inc(gl_qk, 1)
                    for d in range(2):
                        dve.wait_ge(gl_kv, 2 * N + d + 1)
                        base = 2048 if d == 0 else 0
                        for s in range(11):
                            n = chunk_at(d, s)
                            kv = pf[:, base + 1024 * (n % 2) + 128 * (n // 2):base + 1024 * (n % 2) + 128 * (n // 2) + 128]
                            ins = dve.scalar_tensor_tensor(S[:, d, s + 1, :], S[:, d, s, :], gend[:, d, n:n + 1], kv,
                                                           ALU.mult, ALU.add)
                            if s < 10:
                                link(ins)
                        ins.then_inc(gl_state, 1)
                    for e in range(2):
                        for d in range(2):
                            dve.wait_ge(gl_at, 4 * N + 2 * e + d + 1)
                            base = (2048 if e == 0 else 0) + 1024 * d
                            dve.copy_predicated(A[:, e, d, 0:oc].rearrange("p (t i) -> p t i", i=128),
                                                umask[:, d:d + 1, :].to_broadcast([128, oc // 128, 128]),
                                                pf[:, base:base + oc].rearrange("p (t i) -> p t i", i=128)).then_inc(gl_atc, 1)
                    for e in range(2):
                        base = (2048 if e == 0 else 0) + 1024
                        r = at(GR, T)[:, 0:oc]
                        o = at(GO[e], T)[:, 0:oc]
                        yy = y["C"][:, 2 * hp + e, 0:oc]
                        dve.wait_ge(gl_ss, 2 * N + e + 1)
                        link(dve.tensor_scalar(r, pf[:, base:base + oc], 1.0 / 128, EPS, ALU.mult, ALU.add))
                        dve.reciprocal(r, r).then_inc(gl_ms, 1)
                        dve.wait_ge(gl_rt, 2 * N + e + 1)
                        link(dve.scalar_tensor_tensor(o, o, par[:, P_GN:P_GN + 1], r, ALU.mult, ALU.mult))
                        dve.tensor_tensor(yy, yy, o, ALU.mult).then_inc(gl_fin, 1)
                        dve.wait_ge(gl_fin, 2 * N + e + 1)

            def rotary(L):
                cs = at(BROPE, 2, 512)
                t = at(BTMP, 512)
                dve.wait_ge(rope_in, 16 * (L + 1))
                for i in range(5):
                    x = at(BQ, 4, T)[:, i, 0:SEQ] if i < 4 else at(BK, T)[:, 0:SEQ]
                    dve.wait_ge(rope_rot, 5 * L + i + 1)
                    dve.tensor_tensor(t, pf[:, 512 * (4 + i % 2):512 * (5 + i % 2)], cs[:, 1, :], ALU.mult)
                    link(dve.tensor_tensor(x, x, cs[:, 0, :], ALU.mult))
                    dve.tensor_tensor(x, x, t, ALU.add).then_inc(rope_done, 1)
                    dve.wait_ge(rope_done, 5 * L + i + 1)

            def attention(L, mixer):
                A = mixer == "A"
                us = units(mixer, L)
                u0 = unit0[L, mixer]
                pt_at = APT if A else BTMP + 1280
                o_at = AO if A else BTMP + 2560

                def maxima(n):
                    q, i, p = us[n]
                    hh = head(mixer, i, p)
                    w = 128 * len(key_blocks(mixer, q))
                    s = pf[:, 1024 * p:1024 * p + w]
                    dve.wait_ge(at_s, u0 + n + 1)
                    if A and q < 4:
                        if i == 0 and p == 0:
                            dve.wait_ge(bias_in[q % 2], 16 * (2 * L + q // 2 + 1))
                        dve.tensor_reduce(rmx[:, 0:1], s[:, 256:512], AX, ALU.max)
                        link(dve.tensor_tensor_reduce(s[:, 0:256], s[:, 0:256], at(ABIAS + 2048 * (q % 2), 8, 256)[:, hh, :],
                                                      1.0, -3e38, ALU.add, ALU.max, rmx[:, 1:2]))
                        m1 = rmx[:, 1:2]
                    else:
                        link(dve.tensor_reduce(rmx[:, 0:1], s, AX, ALU.max))
                        m1 = par[:, P_SINK + hh:P_SINK + hh + 1] if not A else rmx[:, 0:1]
                    dve.tensor_scalar(stat[:, q % 2, 0, hh:hh + 1], rmx[:, 0:1], m1, -1.0, ALU.max, ALU.mult).then_inc(at_max, 1)
                    dve.wait_ge(at_max, u0 + n + 1)

                def copies(n):
                    q, i, p = us[n]
                    nb = len(key_blocks(mixer, q))
                    dve.wait_ge(at_pt, u0 + n + 1)
                    if n >= 2:
                        dve.wait_ge(at_o, u0 + n - 1)
                    PT = at(pt_at + 640 * p, 640)
                    w = 128 * min(nb, 4)
                    ins = dve.tensor_copy(PT[:, 0:w], pf[:, 2048 + 512 * p:2048 + 512 * p + w])
                    if nb == 5:
                        ins = dve.tensor_copy(PT[:, 512:640], pf[:, 3072:3200])
                    ins.then_inc(at_ptc[0], 1)

                def finish(q, n):
                    st = stat[:, q % 2, :, :]
                    if not A:
                        dve.tensor_tensor(st[:, 3, :], par[:, P_SINK:P_SINK + 8], st[:, 0, :], ALU.add).then_inc(at_sum, 1)
                        dve.wait_ge(at_sink, QB(L) + q + 1)
                        dve.wait_ge(at_p, u0 + n + 2)
                        link(dve.tensor_tensor(st[:, 1, :], st[:, 1, :], st[:, 3, :], ALU.add))
                    dve.wait_ge(at_p, u0 + n + 2)
                    link(dve.reciprocal(st[:, 2, :], st[:, 1, :]))
                    dve.wait_ge(at_o, u0 + n + 2)
                    o = at(o_at, 8, 64)
                    dve.tensor_tensor(o, pf[:, 3584:4096].rearrange("p (h d) -> p h d", d=64),
                                      st[:, 2, :].unsqueeze(2).to_broadcast([128, 8, 64]), ALU.mult).then_inc(at_on, 1)

                def gate(q):
                    dve.wait_ge(at_ot, qt0[L, mixer] + q + 1)
                    turned = pf[:, 3072:3584].rearrange("p (f t) -> p f t", f=4)
                    if A and q < 4:
                        yy = y[mixer][:, :, 0:SEQ].rearrange("p f (r c) -> p f r c", c=GRID_W)[:, :, :, NKC * q:NKC * q + NKC]
                        turned = turned.rearrange("p f (r c) -> p f r c", c=NKC)
                        for f in range(4):
                            ins = dve.tensor_tensor(yy[:, f], yy[:, f], turned[:, f], ALU.mult)
                    else:
                        yy = y[mixer][:, :, 128 * q:128 * q + 128]
                        ins = dve.tensor_tensor(yy, yy, turned, ALU.mult)
                    ins.then_inc(at_y, 1)

                maxima(0)
                maxima(1)
                for n in range(0, len(us), 2):
                    q = us[n][0]
                    copies(n)
                    if n + 2 < len(us):
                        maxima(n + 2)
                        maxima(n + 3)
                    if n % 8 == 6:
                        finish(q, n)
                        gate(q)

            def merge(L):
                w = width(L, False)
                last = L == DEPTH - 1
                acc = at(MACC, KT, T)
                g0, s0 = POS["gate", L, 0, 0], SPLIT_NO["gate", L, 0, 0]
                with dve.Fori(0, KT // 2) as it:
                    for v in range(8):
                        prod = at(MPROD[v % 2], T)[:, 0:w]
                        dst = ar[:, bass.ds(it * (2 * T) + (MACC + T * (v // 4)), w)]
                        dve.wait_ge(mg_gate, 8 * it + (MG(L) + v + 1))
                        src = pf[:, 2048 * (v % 2) + 1024:2048 * (v % 2) + 1024 + w]
                        gate = at(MGATE + T * (v % 2), T)[:, 0:w]
                        if v % 4 == 0:
                            dve.tensor_tensor(dst, gate, src, ALU.mult).then_inc(mg_prod, 1)
                        else:
                            dve.tensor_tensor(prod, gate, src, ALU.mult).then_inc(mg_prod, 1)
                            dve.wait_ge(mg_prod, 8 * it + (MG(L) + v + 3))
                            dve.tensor_tensor(dst, dst, prod, ALU.add).then_inc(mg_sum, 1)
                            dve.wait_ge(mg_sum, 6 * it + (3 * KT * L + v - v // 4))
                        n = g0 + gate_place(v + 2)
                        dve.wait_ge(split_hi, 8 * it + (s0 + v + 3))
                        dve.tensor_tensor(w_lo[:, (s0 + v) % 2], slot_tile[:, n % SLOTS], w_hi[:, (s0 + v) % 2].bitcast(F32),
                                          ALU.subtract).then_inc(ring_read[n % SLOTS], 1)
                for k in range(KT):
                    dve.wait_ge(h_high, KT * (2 * L + 1) + k + 1)
                    dve.tensor_tensor(h_lo[:, k, 0:w], acc[:, k, 0:w], h_hi[:, k, 0:w].bitcast(F32), ALU.subtract)\
                        .then_inc(h_ready, 1)
                x = at(X_AT, KT, T)
                dve.wait_ge(x_in, 16 * (L + 2))
                for m in range(KT):
                    t = tile_no[L, "out", m]
                    if next_split(("proj", L, "out", m)) is not None:
                        low_part(next_split(("proj", L, "out", m)))
                    dve.wait_ge(tile_ready, t + 1)
                    for c, (c0, c1) in enumerate(((0, SEQ), (SEQ, w))):
                        if c1 > c0:
                            ins = dve.scalar_tensor_tensor(x[:, m, c0:c1], pf[:, pair(t) + c0:pair(t) + c1],
                                                           mod[:, L, 2 * KT + m, c:c + 1], x[:, m, c0:c1], ALU.mult, ALU.add)
                    ins.then_inc(drained[t % 2], 1)

            for i in range(2):
                dve.memset(rmx[:, 2 + i:3 + i], 0.0).then_inc(mg_prod, 1)
            for L in range(DEPTH):
                dve.wait_ge(*((par_in, 16 * L) if L else (par_first, 16)))
                filter_net(HYN[False], 2 * L)
                barrier(dve, PH(L, "filter"))
                norm(L, at(X_AT, KT, T))
                if L == 0:
                    dve.wait_ge(mask_in, 16 * 5)
                project(L, "D")
                hyena(2 * L)
                barrier(dve, PH(L, "D"))
                if L < DEPTH - 1:
                    filter_net(HYN[True], 2 * L + 1)
                    hyena(2 * L + 1)
                    barrier(dve, PH(L, "Dc"))
                project(L, "C")
                gla(L)
                barrier(dve, PH(L, "C"))
                project(L, "A")
                attention(L, "A")
                barrier(dve, PH(L, "A"))
                project(L, "B")
                rotary(L)
                attention(L, "B")
                barrier(dve, PH(L, "B"))
                merge(L)
                barrier(dve, PH(L, "merge"))
            r = at(MGATE, SEQ)
            dve.wait_ge(norm_ps, DEPTH + 1)
            link(dve.tensor_scalar(r, pf[:, 0:SEQ], 1.0 / D_MODEL, EPS, ALU.mult, ALU.add))
            dve.reciprocal(r, r).then_inc(norm_ms, 1)
            dve.wait_ge(norm_rt, DEPTH + 1)
            for k in range(KT):
                dve.scalar_tensor_tensor(at(MACC, KT, T)[:, k, 0:SEQ], at(X_AT, KT, T)[:, k, 0:SEQ], par[:, P_FIN + k:P_FIN + k + 1], r,
                                         ALU.mult, ALU.mult).then_inc(res_done, 1)


def weight_stream(w_mod, w_in, w_branch, w_out):
    def tile(w, c0, n=128):
        t = np.zeros((128, KT, 128), np.float32)
        t[:, :, :n] = w[:, c0:c0 + n].reshape(KT, 128, n).transpose(1, 0, 2)
        return t

    start = {(ti[0], ti[1]): ti[2] for b in MIXERS for ti in TILES[b]}

    def weights(kind, L, a, b=None):
        if kind == "mod":
            return tile(w_mod[L], 128 * a)
        if kind == "gate":
            return tile(w_in[L], GM + D_MODEL * b + 128 * a)
        if kind == "branch":
            br = w_branch[L][2 * b:2 * b + 2, :, 128 * a:128 * a + 128].reshape(2, 4, 128, 128)
            return br.transpose(2, 0, 1, 3)
        if a == "out":
            return tile(w_out[L], 128 * b)
        c0 = start[a, b]
        if a == "lr":
            return tile(w_in[L], c0, 32)
        if a == "qb":
            t = tile(w_in[L], c0 + HD * b)
            t[:, :, HD:] = tile(w_in[L], c0 + HD * (b + 4))[:, :, :HD]
            return t
        return tile(w_in[L], c0)

    return np.stack([weights(*key).reshape(128, WTILE) for key in ORDER])


def columns(v):
    return np.asarray(v).reshape(-1, 128).T


def parameter_table(L, a):
    t = np.zeros((128, P_W), np.float32)
    t[:, P_NORM:P_NORM + 8] = columns(a["norm_w"][L])
    t[:, P_BMOD:P_BMOD + 24] = columns(a["b_mod"][L])
    t[:, P_CW:P_CW + 36] = columns(a["conv_w"][L])
    t[:, P_CB:P_CB + 12] = columns(a["conv_b"][L])
    t[:, P_FB:P_FB + 4] = columns(a["filt_bias"][L])
    t[:, P_BA:P_BA + 4] = columns(a["b_alpha"][L])
    t[:, P_GN] = a["gla_norm_w"][L]
    for col, name in ((P_FREQ, "filt_freq"), (P_B1, "filt_b1"), (P_B2, "filt_b2"), (P_B3, "filt_b3")):
        t[:64, col] = a[name][L]
    t[:, P_SINK:P_SINK + 8] = a["sink"][L]
    t[:, P_FIN:P_FIN + 8] = columns(a["final_norm_w"])
    t[:, P_C:P_C + 16:2] = columns(a["c"])
    t[:, P_C + 1:P_C + 16:2] = columns(a["c_ctx"])
    return t


def natten_bias(rpb):
    r, c, rk, ck = np.ogrid[0:8, 0:NKC, 0:8, 0:2 * NKC]
    out = np.empty((4, 128, HEADS, 256), np.float32)
    for j, c0 in enumerate(NATTEN_COL0):
        col, kcol = NKC * j + c, c0 + ck
        first = np.clip(col - NKC // 2, 0, GRID_W - NKC)
        seen = np.broadcast_to((kcol >= first) & (kcol < first + NKC), (8, NKC, 8, 2 * NKC))
        dr = np.broadcast_to(rk - r + NKR - 1, seen.shape)
        dc = np.broadcast_to(np.clip(kcol - col + NKC - 1, 0, 2 * NKC - 2), seen.shape)
        v = np.where(seen, rpb[:, dr, dc], np.float32(NEG))
        out[j] = v.reshape(HEADS, 128, 256).transpose(1, 0, 2)
    return out


def filter_constants(n):
    f32 = np.float32
    t = np.linspace(0.0, 1.0, n, dtype=f32)
    ang = (f32(2.0 * math.pi) * np.arange(n, dtype=f32) / f32(n)).astype(f32)
    f = np.linspace(1e-4, 15, 16, dtype=f32)
    fa = (f[:, None] * ang[None, :]).astype(f32).astype(np.float64)
    z = np.concatenate([t[None, :], np.cos(fa), -np.sin(fa)], 0).astype(f32)
    deltas = np.abs(np.linspace(math.log(1e-2) / 1.5, math.log(1e-2) / 0.3, 512, dtype=f32))
    decay = np.exp((-t[:, None] * deltas[None, :]).astype(np.float64)).astype(f32)
    return z, decay


def transforms(n):
    w, t = np.arange(n)[:, None], np.arange(n)[None, :]
    ang = 2.0 * np.pi * ((w * t) % (2 * n)) / (2 * n)
    c, s = np.cos(ang), np.sin(ang)
    s[0] = (-1.0) ** np.arange(n)
    back = np.concatenate([c, s], 0) / n
    back[0] /= 2
    back[n] /= 2
    def rows(m):
        return m.reshape(-1, 128, m.shape[1]).transpose(1, 0, 2).astype(np.float32)
    return rows(np.concatenate([c, s], 0).T), rows(back)


def kernel(**inputs):
    import concourse.bacc as bacc
    import ml_dtypes
    from concourse.bass_utils import run_bass_kernel_spmd

    a = {k: np.asarray(v) for k, v in inputs.items()}
    z_l, dec_l = filter_constants(SEQ)
    z_c, dec_c = filter_constants(CTX)
    dft, idft = transforms(SEQ)
    dft_c, idft_c = transforms(CTX)
    eye = np.eye(128, dtype=np.float32)
    sign = ((-1.0) ** np.arange(128)).astype(np.float32)
    i = np.arange(128)
    left = np.where(i[None, :] >= i[:, None], 0.0, NEG)
    right = np.where(i[None, :] <= i[:, None], 0.0, NEG)
    tt = np.arange(T)
    starts = np.broadcast_to((tt % 64 != 0).astype(np.float32), (128, T))
    ends = np.broadcast_to((tt % 64 != 63).astype(np.float32), (128, T))
    same = i[:, None] // 64 == i[None, :] // 64
    pos = np.arange(SEQ)
    inv = (np.float32(10000.0) ** (-np.arange(16, dtype=np.float32) / 16)).astype(np.float32)
    ang = np.concatenate([(pos // GRID_W)[:, None] * inv, (pos % GRID_W)[:, None] * inv], 1).astype(np.float32)
    ang = np.tile(ang.T.astype(np.float64), (4, 1))
    rot = np.zeros((128, 128), np.float32)
    for b in (0, 64):
        for d in range(32):
            rot[b + 32 + d, b + d] = -1.0
            rot[b + d, b + 32 + d] = 1.0
    fw = np.zeros((DEPTH, 64, 192), np.float32)
    fw[:, :33, 0:64], fw[:, :, 64:128], fw[:, :, 128:192] = a["filt_w1"], a["filt_w2"], a["filt_w3"]
    alpha = np.zeros((DEPTH, 32, 512), np.float32)
    alpha[:, 0:16, 0:256], alpha[:, 16:32, 256:512] = a["w_alpha_up"][:, 0], a["w_alpha_up"][:, 1]
    xT = np.concatenate([a["x"][0], a["ctx"][0]], 0).T.reshape(KT, 128, T).transpose(1, 0, 2)
    arrays = {
        "wstream": weight_stream(a["w_mod"], a["w_in"], a["w_branch"], a["w_out"]),
        "xT": xT,
        "params": np.stack([parameter_table(L, a) for L in range(DEPTH)]),
        "zembT": np.concatenate([z_l, z_c], 1),
        "filt_w": fw,
        "filt_wout": a["filt_wout"],
        "decay": np.concatenate([dec_l, dec_c], 0).reshape(6, 128, 512).transpose(1, 0, 2),
        "dft": dft, "dft_c": dft_c, "idft": idft, "idft_c": idft_c,
        "bias": np.stack([natten_bias(a["rpb"][L]) for L in range(DEPTH)]),
        "rope": np.stack([np.cos(ang), np.sin(ang)], 1).astype(np.float32),
        "rot": rot,
        "alpha_w": alpha,
        "masks_f": np.concatenate([np.ones((128, 128), np.float32), eye, sign[:, None]], 1),
        "masks_b": np.concatenate([eye, left, right, starts, ends], 1).astype(ml_dtypes.bfloat16),
        "masks_u": np.concatenate([same & (i[:, None] <= i[None, :]), same & (i[:, None] >= i[None, :])], 1).astype(np.int32),
    }
    nc = bacc.Bacc("TRN2", target_bir_lowering=False, num_devices=1)
    sent, args = {}, []
    for name, v in arrays.items():
        v = np.ascontiguousarray(v)
        sent[f"in_{name}"] = v
        args.append(nc.dram_tensor(f"in_{name}", v.shape, mybir.dt.from_np(v.dtype), kind="ExternalInput").ap())
    args.append(nc.dram_tensor("x_mid", [128, KT, T], F32, kind="Internal").ap())
    args.append(nc.dram_tensor("v_mid", [DEPTH, SEQ, 512], F32, kind="Internal").ap())
    args.append(nc.dram_tensor("outT", [D_MODEL, SEQ], F32, kind="ExternalOutput").ap())
    build(nc, *args)
    r = run_bass_kernel_spmd(nc, [sent], core_ids=[0])
    return np.ascontiguousarray(r.results[0]["outT"].T)[None]
```

```python
import math
from contextlib import ExitStack

import numpy as np

import concourse.bass as bass
from concourse import mybir

F32 = mybir.dt.float32
F32R = mybir.dt.float32r
BF16 = mybir.dt.bfloat16
I32 = mybir.dt.int32
ALU = mybir.AluOpType
ACT = mybir.ActivationFunctionType
AX = mybir.AxisListType.X

D_MODEL, SEQ, CTX, DEPTH = 1024, 512, 256, 2
T = SEQ + CTX
KT = D_MODEL // 128
HD = 64
HEADS = 8
GRID_W, NKR, NKC = 64, 8, 16
EPS = 1e-6
NEG = -1e30
SLOTS = 6
WTILE = KT * 128
ROUND = 1.5 * 2.0 ** 23
TWO_PI_HI = 6.28125
TWO_PI_LO = 2.0 * math.pi - TWO_PI_HI
PI_IN = 3.1415925

WIDTHS = (512, 512, 512, 512, 512, 128, 128, 512, 256, 256, 512, 16, 16, 512, 1536, 512, 4096)
STARTS = np.concatenate([[0], np.cumsum(WIDTHS)]).astype(int)
(QA, KA, VA, GA, QB, KB, VB, GB, QG, KG, VG, LRF, LRB, GG, UH, GH, GM) = STARTS[:-1]

TILES = {
    "D": [("u", i, UH + 128 * i, False) for i in range(12)] + [("gd", i, GH + 128 * i, False) for i in range(4)],
    "C": [("lr", 0, LRF, True)] + [("kg", i, KG + 128 * i, True) for i in range(2)]
         + [("qg", i, QG + 128 * i, False) for i in range(2)] + [("vg", i, VG + 128 * i, True) for i in range(4)]
         + [("gg", i, GG + 128 * i, False) for i in range(4)],
    "A": [("ka", i, KA + 128 * i, True) for i in range(4)] + [("va", i, VA + 128 * i, True) for i in range(4)]
         + [("qa", i, QA + 128 * i, False) for i in range(4)] + [("ga", i, GA + 128 * i, False) for i in range(4)],
    "B": [("kb", 0, KB, True), ("vb", 0, VB, True)] + [("qb", i, QB, False) for i in range(4)]
         + [("gb", i, GB + 128 * i, False) for i in range(4)],
}
MIXERS = ("D", "C", "A", "B")
MOD_TILES = 3 * KT
BRANCH_TILES = 6
MOD_AT = {"start": [(0, m) for m in range(2 * KT)],
          "norm0": [(0, m) for m in range(2 * KT, 2 * KT + 5)],
          "Dc": [(0, m) for m in range(2 * KT + 5, MOD_TILES)] + [(1, m) for m in range(20)],
          "norm1": [(1, m) for m in range(20, MOD_TILES)]}
HYENA_MODS = (MOD_AT["Dc"][:6], MOD_AT["Dc"][15:], [])
FILTER_MODS = MOD_AT["Dc"][6:15]
MOD_PLACES = ("start", "norm0", "Dc", "norm1")
MOD_NO = {lm: n for n, lm in enumerate(lm for p in MOD_PLACES for lm in MOD_AT[p])}


def mods(place):
    return [("mod",) + lm for lm in MOD_AT[place]]


def tile_order():
    order = mods("start")
    for L in range(DEPTH):
        order += mods(f"norm{L}")
        for b in MIXERS:
            for i, ti in enumerate(TILES[b]):
                order.append(("proj", L) + ti[:2])
                if (L, b, i) == (0, "C", 1):
                    order += mods("Dc")
        for m in range(KT):
            order += [("gate", L, m, 0), ("gate", L, m, 1), ("branch", L, m, 0),
                      ("gate", L, m, 2), ("gate", L, m, 3), ("branch", L, m, 1)]
        order += [("proj", L, "out", m) for m in range(KT)]
    return order


ORDER = tile_order()
POS = {key: n for n, key in enumerate(ORDER)}
SPLITS = [key for key in ORDER if key[0] in ("proj", "gate")]
SPLIT_NO = {key: n for n, key in enumerate(SPLITS)}
NATTEN_COL0 = [min(max(j * NKC - NKC // 2, 0), GRID_W - 2 * NKC) for j in range(GRID_W // NKC)]

ARENA = 27904
Y_AT = {"D": 0, "C": 3072, "A": 6144, "B": 9216}
KSPEC, FWD, INV, FWD_C, INV_C = 3072, 7168, 9216, 11264, 12288
X_AT = 13312
HX0, HZ, HV = 13312, 16384, 19456
ZSPEC, HTMP = 22528, 26624
LR, GQ, GK, GV, GE, GS, GL, GAT = 6144, 6912, 8448, 9984, 13056, 17664, 20736, 23808
GSQ, GO = (LR, GQ), (GK, 26880)
AQ, AK, AV, AVB, ABIAS, AP_, APT, AO = 9216, 12288, 15360, (15360, 16384, 18432, 19456), 20480, 24576, 25856, 27136
BQ, BK, BV, BROPE, BTMP = 12288, 15360, 16128, 16896, 17920
VT_AT = {"C": GAT, "A": AP_, "B": BTMP + 3072}
NSQ_AT = ((FWD_C, FWD_C + T, 26624), (19456, 20224, 20992), (19456, 20224, 20992))
NRS = 25600
MACC, MGATE, MPROD = 19456, 25600, (12288, 27136)
FZE, FH0, FH1, FT, FABS = KSPEC, KSPEC + 512, KSPEC + 1024, KSPEC + 1536, KSPEC + 2048
FHF, FHB, FDEC = ZSPEC, ZSPEC + 2048, HV
FW, FWO = KSPEC + 3072, HTMP
FZE_C, FW_C = 12992, 12800

P_NORM, P_BMOD, P_CW, P_CB, P_FB, P_BA, P_GN, P_FREQ, P_B1, P_B2, P_B3, P_SINK, P_FIN, P_C, P_W = (
    0, 8, 32, 68, 80, 84, 88, 89, 90, 91, 92, 93, 101, 109, 125)


MOD_COL = {"start": 3 * 512, "norm0": 2 * 512, "Dc": T, "norm1": 6 * 512}
NORM_COL = 4 * 512
VALUES = ("va", "vb", "vg")
ALPHA_AT = {2: (0, 0), 3: (0, 1), 10: (1, 0), 11: (1, 1)}


def gate_place(v):
    return BRANCH_TILES * (v // 4) + (0, 1, 3, 4)[v % 4]


def build(nc, wstream, xT, params, zembT, filt_w, filt_wout, decay, dft, dft_c, idft, idft_c,
          bias, rope, rot, alpha_w, masks_f, masks_b, masks_u, x_mid, v_mid, out):
    with ExitStack() as ctx:
        def sb(name, shape, dt=F32):
            return ctx.enter_context(nc.sbuf_tensor(name, shape, dt))

        def sem(name):
            return ctx.enter_context(nc.semaphore(name))

        ar = sb("arena", [128, ARENA])
        h_hi = sb("h_hi", [128, KT, T], F32R)
        h_lo = sb("h_lo", [128, KT, T], F32R)
        ring = sb("ring", [128, SLOTS, WTILE])
        w_hi = sb("w_hi", [128, 2, KT, 128], F32R)
        w_lo = sb("w_lo", [128, 2, KT, 128], F32R)
        const_f = sb("const_f", [128, 257])
        ones, ident = const_f[:, 0:128], const_f[:, 128:256]
        ident_b = sb("ident_b", [128, 128], BF16)
        bmask = sb("bmask", [128, 2, 128], BF16)
        cmask = sb("cmask", [128, 2, T], BF16)
        umask = sb("umask", [128, 2, 128], I32)
        alt = const_f[:, 256:257]
        rotm = sb("rotm", [128, 128])
        aw = sb("aw", [32, 512])
        par = sb("par", [128, P_W])
        csil = sb("csil", [128, 8, 2])
        mod = sb("mod", [128, DEPTH, MOD_TILES, 2])
        mod_row = sb("mod_row", [2, 128])
        nscale = sb("nscale", [128, 8, 2])
        stat = sb("stat", [128, 2, 4, 8])
        rmx = sb("rmx", [128, 4])
        gend = sb("gend", [128, 2, 12])
        pf = ctx.enter_context(nc.psum_tensor("psum", [128, 8 * 512], F32))

        def at(off, *shape):
            n = int(np.prod(shape))
            v = ar[:, off:off + n]
            if len(shape) == 1:
                return v
            names = "abcd"[:len(shape)]
            return v.rearrange(f"p ({' '.join(names)}) -> p {' '.join(names)}",
                               **{k: s for k, s in zip(names, shape)})

        y = {b: at(Y_AT[b], 4, T) for b in MIXERS}
        slot_tile = ring[:, :, :].rearrange("p s (k m) -> p s k m", k=KT)
        slot_br = ring[:, :, :].rearrange("p s (b k m) -> p s b k m", b=2, k=4)

        ring_full = [sem(f"ring_full{s}") for s in range(SLOTS)]
        ring_read = [sem(f"ring_read{s}") for s in range(SLOTS)]
        split_hi = sem("split_hi")
        const_in = sem("const_in")
        mask_in = sem("mask_in")
        first_in = sem("first_in")
        par_first = sem("par_first")
        par_in = sem("par_in")
        csil_ready = sem("csil_ready")
        row_done = sem("row_done")
        mod_tr = sem("mod_tr")
        mod_done = sem("mod_done")
        norm_t = sem("norm_t")
        h_high = sem("h_high")
        h_ready = sem("h_ready")
        v_tr = sem("v_tr")
        v_done = sem("v_done")
        dec_in = sem("dec_in")
        fwd_in = sem("fwd_in")
        dftc_in = sem("dftc_in")
        aw_in = sem("aw_in")
        x_in = sem("x_in")
        x_saved = sem("x_saved")
        tile_ready = sem("tile_ready")
        drained = [sem("drained0"), sem("drained1")]
        conv_ready = sem("conv_ready")
        dve_chain = sem("dve_chain")
        phase_done = sem("phase_done")
        filt_in = sem("filt_in")
        ctx_in = sem("ctx_in")
        filt_pe = sem("filt_pe")
        filt_dve = sem("filt_dve")
        filt_act = sem("filt_act")
        norm_sq = sem("norm_sq")
        norm_sum = sem("norm_sum")
        norm_ps = sem("norm_ps")
        norm_ms = sem("norm_ms")
        norm_rt = sem("norm_rt")
        dft_in = sem("dft_in")
        hy_z = sem("hy_z")
        hy_tr = sem("hy_tr")
        hy_ztok = sem("hy_ztok")
        hy_spec = sem("hy_spec")
        hy_zs = sem("hy_zs")
        hy_comb = sem("hy_comb")
        hy_pool = sem("hy_pool")
        hy_prod = sem("hy_prod")
        hy_inv = sem("hy_inv")
        hy_out = sem("hy_out")
        gl_alpha = sem("gl_alpha")
        gl_z = sem("gl_z")
        gl_ln = sem("gl_ln")
        gl_cum = sem("gl_cum")
        gl_rest = sem("gl_rest")
        gl_exp = sem("gl_exp")
        gl_exp2 = sem("gl_exp2")
        gl_ke = sem("gl_ke")
        gl_tr = sem("gl_tr")
        gl_ket = sem("gl_ket")
        gl_kv = sem("gl_kv")
        gl_state = sem("gl_state")
        gl_qk = sem("gl_qk")
        gl_at = sem("gl_at")
        gl_atc = sem("gl_atc")
        gl_o = sem("gl_o")
        gl_sq = sem("gl_sq")
        gl_ss = sem("gl_ss")
        gl_rd = sem("gl_rd")
        gl_ms = sem("gl_ms")
        gl_rt = sem("gl_rt")
        gl_fin = sem("gl_fin")
        vblk_in = sem("vblk_in")
        v_out = sem("v_out")
        bias_in = [sem("bias_in0"), sem("bias_in1")]
        rope_in = sem("rope_in")
        rope_rot = sem("rope_rot")
        rope_done = sem("rope_done")
        at_s = sem("at_s")
        at_max = sem("at_max")
        at_p = sem("at_p")
        at_pt = sem("at_pt")
        at_ptc = [sem("at_ptc0"), sem("at_ptc1")]
        at_o = sem("at_o")
        at_sum = sem("at_sum")
        at_sink = sem("at_sink")
        at_on = sem("at_on")
        at_ot = sem("at_ot")
        at_y = sem("at_y")
        mg_unit = sem("mg_unit")
        mg_gate = sem("mg_gate")
        mg_prod = sem("mg_prod")
        mg_sum = sem("mg_sum")
        res_done = sem("res_done")
        out_dma = sem("out_dma")

        tile_no = {key[1:]: n for n, key in enumerate(k for k in ORDER if k[0] == "proj")}

        def slot(key):
            return POS[key] % SLOTS

        def turns(key):
            return POS[key] // SLOTS + 1

        def wait_used(eng, key):
            if key[0] == "gate":
                eng.wait_ge(mg_unit, MG(key[1]) + 4 * key[2] + key[3] + 1)
            else:
                eng.wait_ge(tile_ready, tile_no[key[1:]] + 1)

        def next_split(key, ahead=2):
            n = SPLIT_NO[key] + ahead
            return n if n < len(SPLITS) else None

        def value_no(L, what, i):
            return 9 * L + {"vg": 0, "va": 4, "vb": 8}[what] + i

        def width(L, needed):
            return T if L < DEPTH - 1 or needed else SEQ

        behind_scores = {tile_no[L, what, 3] for L in range(DEPTH) for what in ("ga", "gb")}

        def pair(t):
            return 3072 if t in behind_scores else (t % 2) * 1024

        def wait_tile(eng, L, name, i):
            t = tile_no[L, name, i]
            eng.wait_ge(drained[t % 2], t // 2 + 1)

        phase_list = [(0, "filter"), (0, "D")]

        def PH(L, name):
            return phase_list.index((L, name)) + 1

        def arrive(eng):
            eng.drain().then_inc(phase_done, 1)

        def barrier(eng, n):
            arrive(eng)
            eng.wait_ge(phase_done, 4 * n)

        def filter_steps(nt):
            return 4 + 3 * nt

        def dec_at(run):
            return at(FWD_C if run == 2 else FDEC, 4, 512)

        def spectrum_pair(nt, i):
            first = i if 2 * i < nt else nt // 2 + i
            return first, first + nt // 2

        def early_parts(eng, L, part):
            for what, i, _, _ in TILES["C"][:2]:
                wait_used(eng, ("proj", L, what, i))
                part(next_split(("proj", L, what, i)))

        def last_at_y(L, mixer):
            return qt0[L, mixer] + len(units(mixer, L)) // 8

        def units(mixer, L):
            nq = 4 + (2 if L < DEPTH - 1 else 0)
            return [(q, i, p) for q in range(nq) for i in range(4) for p in range(2)]

        def head(mixer, i, p):
            return 2 * i + p if mixer == "A" else i + 4 * p

        def key_blocks(mixer, q):
            if q >= 4:
                return [4, 5]
            if mixer == "A":
                return [-1, -1, 4, 5]
            return [n for n in (q - 1, q, q + 1) if 0 <= n < 4] + [4, 5]

        unit0, u = {}, 0
        qt0, qn = {}, 0
        for L in range(DEPTH):
            for b in ("A", "B"):
                unit0[L, b] = u
                qt0[L, b] = qn
                u += len(units(b, L))
                qn += len(units(b, L)) // 8

        hy_runs = [(0, False), (0, True), (1, False)]
        HYN = {False: dict(nt=4, t0=0, n=SEQ), True: dict(nt=2, t0=4, n=CTX)}
        HYT = [HYN[is_c]["nt"] for _, is_c in hy_runs]

        def FD(run):
            return sum(7 + 4 * nt for nt in HYT[:run])

        def FA(run):
            return sum(3 + 2 * nt for nt in HYT[:run])

        def FP(run):
            return sum(4 + 6 * nt for nt in HYT[:run])

        def HPR(run):
            return sum(HYT[:run])

        def FIN(run):
            return (0, 16, 64)[run]

        def ZT(L):
            return 6 * L

        def QB(L):
            return 6 * L

        def MG(L):
            return 4 * KT * L

        def chunk_at(d, s):
            return 11 - s if d else (8 + s if s < 4 else s - 4)

        def state_slot(d, n):
            return 11 - n if d else (n + 4 if n < 8 else n - 8)

        block = ctx.enter_context(nc.Block())

        @block.sync
        def _(sp):
            sp.dma_start(at(FZE, 512)[0:33, :], zembT[:, 0:SEQ]).then_inc(first_in, 16)
            sp.dma_start(at(FW, 192)[0:64, :], filt_w[0]).then_inc(first_in, 16)
            sp.dma_start(par[:, :], params[0]).then_inc(par_first, 16)
            sp.dma_start(at(FWO, 1024)[0:64, :], filt_wout[0]).then_inc(first_in, 16)
            sp.dma_start(const_f[:, :], masks_f).then_inc(const_in, 16)
            for s in range(SLOTS):
                sp.dma_start(ring[:, s, :], wstream[s]).then_inc(ring_full[s], 16)
            with sp.Fori(1, len(ORDER) // SLOTS) as turn:
                for s in range(SLOTS):
                    sp.wait_ge(ring_read[s], turn)
                    sp.dma_start(ring[:, s, :], wstream[turn * SLOTS + s]).then_inc(ring_full[s], 16)
            for n in range(len(ORDER) - len(ORDER) % SLOTS, len(ORDER)):
                sp.wait_ge(ring_read[n % SLOTS], n // SLOTS)
                sp.dma_start(ring[:, n % SLOTS, :], wstream[n]).then_inc(ring_full[n % SLOTS], 16)

        @block.gpsimd
        def _(pool):
            def filter_inputs(L):
                if L:
                    pool.dma_start(par[:, :], params[L]).then_inc(par_in, 16)
                    pool.dma_start(at(FZE, 512)[0:33, :], zembT[:, 0:SEQ]).then_inc(filt_in, 16)
                    pool.dma_start(at(FW, 192)[0:64, :], filt_w[L]).then_inc(filt_in, 16)
                    pool.dma_start(at(FWO, 1024)[0:64, :], filt_wout[L]).then_inc(filt_in, 16)
                pool.dma_start(dec_at(2 * L), decay[:, 0:4, :]).then_inc(dec_in, 16)
                pool.dma_start(at(FWD, 4, 512), dft).then_inc(fwd_in, 16)
                pool.dma_start(at(INV, 8, 256), idft).then_inc(dft_in, 16)
                pool.dma_start(aw[:, :], alpha_w[L]).then_inc(aw_in, 16)

            def spectrum_products(L):
                ks, zs = at(KSPEC, 8, 512), at(ZSPEC, 8, 512)
                t1, t2 = at(HV + 1024, 512), at(HV + 1536, 512)
                pool.wait_ge(hy_comb, HPR(2 * L) + 4)
                done = 12 * L
                for j in (1, 3):
                    zc, zn, kc, kn = zs[:, j, :], zs[:, 4 + j, :], ks[:, j, :], ks[:, 4 + j, :]
                    for out, a, b, op in ((t1, zn, kn, ALU.mult), (t2, zn, kc, ALU.mult), (zn, zc, kn, ALU.mult),
                                          (zn, zn, t2, ALU.add), (zc, zc, kc, ALU.mult), (zc, zc, t1, ALU.subtract)):
                        pool.tensor_tensor(out, a, b, op).then_inc(hy_pool, 1)
                        done += 1
                        pool.wait_ge(hy_pool, done)

            filter_inputs(0)
            pool.dma_start(at(FZE_C, CTX)[0:33, :], zembT[:, SEQ:T]).then_inc(ctx_in, 16)
            pool.dma_start(at(FW_C, 192)[0:64, :], filt_w[0]).then_inc(ctx_in, 16)
            pool.dma_start(at(X_AT, KT, T), xT).then_inc(x_in, 16)
            for dst, src in ((rotm[:, :], rot), (ident_b[:, :], masks_b[:, 0:128]),
                             (bmask[:, :, :], masks_b[:, 128:384].rearrange("p (a b) -> p a b", a=2)),
                             (cmask[:, :, :], masks_b[:, 384:384 + 2 * T].rearrange("p (a b) -> p a b", a=2)),
                             (umask[:, :, :], masks_u.rearrange("p (a b) -> p a b", a=2))):
                pool.dma_start(dst, src).then_inc(mask_in, 16)
            for L in range(DEPTH):
                last = L == DEPTH - 1
                if L == 0:
                    barrier(pool, PH(L, "filter"))
                    pool.wait_ge(norm_ps, 1)
                    pool.dma_start(at(FWD_C, 2, 256), dft_c).then_inc(dftc_in, 16)
                    pool.dma_start(at(INV_C, 4, 128), idft_c).then_inc(dftc_in, 16)
                spectrum_products(L)
                if L == 0:
                    barrier(pool, PH(L, "D"))
                if not last:
                    pool.dma_start(at(FWO, 1024)[0:64, :], filt_wout[L]).then_inc(filt_in, 16)
                    pool.dma_start(at(FDEC, 4, 512)[:, 0:2, :], decay[:, 4:6, :]).then_inc(dec_in, 16)
                pool.wait_ge(gl_fin, 4 * (L + 1))
                for j in range(2):
                    pool.dma_start(at(ABIAS + 2048 * j, 8, 256), bias[L, j]).then_inc(bias_in[j], 16)
                pool.wait_ge(v_done, value_no(L, "va", 3) + 1)
                pool.dma_start(v_mid[L].rearrange("(t p) c -> p t c", p=128), at(AV, 6, 512)[:, 0:4, :]).then_inc(v_out, 16)
                pool.wait_ge(v_out, 16 * (L + 1))
                rows = v_mid[L].rearrange("(r c) f -> r c f", c=GRID_W)
                for j, c0 in enumerate(NATTEN_COL0):
                    for k in range(2):
                        for r in range(4):
                            pool.dma_start(at(AVB[j], 2, 512)[32 * r:32 * r + 32, k, :],
                                           rows[4 * k + r, c0:c0 + 32, :]).then_inc(vblk_in, 16)
                for j in range(2, 4):
                    pool.wait_ge(at_max, unit0[L, "A"] + 8 * (j - 1))
                    pool.dma_start(at(ABIAS + 2048 * (j % 2), 8, 256), bias[L, j]).then_inc(bias_in[j % 2], 16)
                pool.wait_ge(at_o, unit0[L, "A"] + len(units("A", L)))
                pool.dma_start(at(BROPE, 2, 512), rope).then_inc(rope_in, 16)
                pool.wait_ge(at_y, last_at_y(L, "B"))
                w = width(L, False)
                pool.dma_start(at(X_AT, KT, T)[:, :, 0:w], (x_mid if L else xT)[:, :, 0:w]).then_inc(x_in, 16)
                if not last:
                    pool.wait_ge(h_ready, 2 * KT * (L + 1))
                    filter_inputs(L + 1)
                    for m in range(KT):
                        wait_tile(pool, L, "out", m)
                        pool.dma_start(x_mid[:, m, 0:SEQ], at(X_AT, KT, T)[:, m, 0:SEQ]).then_inc(x_saved, 16)
            for k in range(KT):
                pool.wait_ge(res_done, k + 1)
                pool.dma_start(out[128 * k:128 * k + 128, :], at(MACC, KT, T)[:, k, 0:SEQ]).then_inc(out_dma, 16)
            pool.wait_ge(out_dma, 16 * KT)

        @block.tensor
        def _(pe):
            def mod_tile(L, m, place):
                key = ("mod", L, m)
                j = MOD_AT[place].index((L, m))
                if j == 0 and MOD_PLACES.index(place) >= 2:
                    pe.wait_ge(mod_done, MOD_PLACES.index(place))
                if j:
                    mod_column(place, j - 1)
                pe.wait_ge(ring_full[slot(key)], 16 * turns(key))
                col = MOD_COL[place]
                for k in range(KT):
                    mm = pe.matmul(pf[0:2, col:col + 128], csil[:, k, :], slot_tile[:, slot(key), k, :],
                                   start=(k == 0), stop=(k == KT - 1))
                mm.then_inc(ring_read[slot(key)], 1)
                if j == len(MOD_AT[place]) - 1:
                    mod_column(place, j)

            def mod_column(place, j):
                pe.wait_ge(row_done, MOD_NO[MOD_AT[place][j]] + 1)
                col = MOD_COL[place] + 128 + 2 * j
                pe.matmul(pf[:, col:col + 2], mod_row[:, :], ident[0:2, 0:2], start=True, stop=True).then_inc(mod_tr, 1)

            def multiply(w, out, cols, wait_k=None):
                parts = [(0, SEQ)] + ([(SEQ, T)] if cols > SEQ else [])
                for k in range(KT):
                    if wait_k:
                        pe.wait_ge(h_ready, wait_k + k)
                    for c0, c1 in parts:
                        pe.matmul(pf[:, out + c0:out + c1], w_hi[:, w, k, :], h_hi[:, k, c0:c1], start=(k == 0), stop=False)
                        pe.matmul(pf[:, out + c0:out + c1], w_hi[:, w, k, :], h_lo[:, k, c0:c1], start=False, stop=False)
                    for c0, c1 in parts:
                        mm = pe.matmul(pf[:, out + c0:out + c1], w_lo[:, w, k, :], h_hi[:, k, c0:c1], start=False, stop=(k == KT - 1))
                return mm

            def transpose_values(L, mixer, what, i):
                n = value_no(L, what, i)
                wait_tile(pe, L, what, i)
                if n:
                    pe.wait_ge(v_done, n)
                v = at(VT_AT[mixer] + T * (n % 2), T)
                for tt in range(6):
                    mm = pe.transpose(pf[:, 2048 + 128 * tt:2048 + 128 * tt + 128], v[:, 128 * tt:128 * tt + 128], ident[:, :])
                mm.then_inc(v_tr, 1)

            def project(L, mixer, tiles):
                turned = None
                for n in tiles:
                    what, i, _, need = TILES[mixer][n]
                    key = ("proj", L, what, i)
                    t = tile_no[L, what, i]
                    pe.wait_ge(ring_read[slot(key)], turns(key))
                    if t >= 2:
                        pe.wait_ge(drained[t % 2], t // 2)
                    multiply(SPLIT_NO[key] % 2, pair(t), width(L, need),
                             2 * KT * L + 1 if (mixer, n) == ("D", 0) else None).then_inc(tile_ready, 1)
                    if mixer == "A" and n == 0:
                        gla_squares(L, 1)
                    if mixer == "A" and n == 1:
                        pe.wait_ge(gl_rd, 4 * (L + 1))
                    if turned:
                        transpose_values(L, mixer, *turned)
                    turned = (what, i) if what in VALUES else None
                    if mixer == "B" and 4 <= n < 9:
                        rotary(L, n - 4)
                    if mixer == "C" and n in ALPHA_AT:
                        gla_alpha(L, *ALPHA_AT[n])
                    if (mixer, n) == ("D", 0):
                        pe.wait_ge(mod_done, MOD_PLACES.index(f"norm{L}") + 1)
                    if (L, mixer) == (1, "D"):
                        filter_step(HYN[False], 2, n)

            def filter_step(c, run, step):
                nt, n = c["nt"], c["n"]
                base_d, base_a = FD(run), FA(run)
                h3, wo = at(FH0, 512)[0:64, :], at(FWO, 1024)[0:64, :]
                if step < 3:
                    k = step
                    ze, w123 = at(FZE_C if run == 1 else FZE, 512 if run != 1 else CTX), at(FW_C if run == 1 else FW, 3, 64)
                    src = (ze[0:33, 0:n], at(FH0, 512)[0:64, 0:n], at(FH1, 512)[0:64, 0:n])[k]
                    w = w123[0:33, 0, :] if k == 0 else w123[0:64, k, :]
                    if k == 0:
                        pe.wait_ge(*((first_in, 48), (ctx_in, 32), (filt_in, FIN(2)))[run])
                        if run == 1:
                            pe.wait_ge(hy_out, 4)
                    else:
                        pe.wait_ge(filt_act, base_a + k)
                    pe.matmul(pf[0:64, 2048:2048 + n], w, src, start=True, stop=True).then_inc(filt_pe, 1)
                elif step < 3 + nt:
                    t = step - 3
                    if run == 1:
                        pe.wait_ge(filt_in, FIN(1))
                    pe.wait_ge(filt_act, base_a + 3)
                    for p in range(2):
                        if t:
                            pe.wait_ge(filt_dve, base_d + 3 + 2 * t + p - 1)
                        pe.matmul(pf[:, 512 * (5 + p):512 * (6 + p)], h3[:, 128 * t:128 * t + 128],
                                  wo[:, 512 * p:512 * p + 512], start=True, stop=True).then_inc(filt_pe, 1)
                elif step == 3 + nt:
                    for j in range(2 * nt):
                        pe.wait_ge(filt_act, base_a + 3 + j + 1)
                        pe.matmul(pf[:, 3584:4096], ones[:, :], at(FABS + 512 * (j % 2), 512),
                                  start=(j == 0), stop=(j == 2 * nt - 1), skip_group_check=True).then_inc(filt_pe, 1)
                else:
                    i, p = divmod(step - 4 - nt, 2)
                    if (i, p) == (0, 0):
                        pe.wait_ge(filt_dve, base_d + 3 + 2 * nt + 2)
                        pe.wait_ge(*((fwd_in, 16 * (hy_runs[run][0] + 1)) if nt == 4 else (dftc_in, 32)))
                    if i:
                        pe.wait_ge(filt_dve, base_d + 3 + 2 * nt + 3 + 2 * i + p - 1)
                    fwd = at(FWD, 4, 512) if nt == 4 else at(FWD_C, 2, 256)
                    hs, hd = dec_at(run), at(FHB, 4, 512)
                    src = hs if 2 * i < nt else hd
                    if (2 * i, p) == (nt, 0):
                        for t in range(nt // 2):
                            mm = pe.matmul(pf[0:1, 2048:2560], alt[:, :], hs[:, t, :], start=(t == 0), stop=(t == nt // 2 - 1))
                        mm.then_inc(filt_pe, 1)
                    for t in range(nt // 2):
                        mm = pe.matmul(pf[:, 512 * (5 + p):512 * (6 + p)], fwd[:, p * nt // 2 + t, 128 * i:128 * i + 128],
                                       src[:, p * nt // 2 + t, :], start=(t == 0), stop=(t == nt // 2 - 1))
                    mm.then_inc(filt_pe, 1)

            def norm(L):
                total = at(NSQ_AT[L][0], T)
                pe.wait_ge(norm_sum, (KT - 1) * (L + 1))
                pe.matmul(pf[:, NORM_COL:NORM_COL + SEQ], ones[:, :], total[:, 0:SEQ], start=True, stop=True)
                mm = pe.matmul(pf[:, NORM_COL + SEQ:NORM_COL + T], ones[:, :], total[:, SEQ:T], start=True, stop=True)
                mm.then_inc(norm_ps, 1)

            def hyena(run):
                L, is_c = hy_runs[run]
                c = HYN[is_c]
                nt, n, t0 = c["nt"], c["n"], c["t0"]
                z, zt = at(HZ, 4, T), at(HV, 6, 512)
                zs = at(ZSPEC, 8, 512)
                fwd = at(FWD, 4, 512) if nt == 4 else at(FWD_C, 2, 256)
                inv = at(INV, 8, 256) if nt == 4 else at(INV_C, 4, 128)
                lt = nt // 2
                pe.wait_ge(filt_dve, FD(run + 1))
                if not is_c:
                    for j in range(6 if L < DEPTH - 1 else 4):
                        pe.wait_ge(hy_z, 4 * L + 4)
                        if j >= 2:
                            pe.wait_ge(hy_ztok, ZT(L) + j - 1)
                        t1 = (256 * (j % 2) + j // 2) if j < 4 else SEQ + j - 4
                        for cc in range(4):
                            mm = pe.transpose(pf[:, 512 * (4 + j % 2) + 128 * cc:512 * (4 + j % 2) + 128 * cc + 128],
                                              z[:, cc, t1:t1 + 255:2], ident[:, :])
                        mm.then_inc(hy_tr, 1)
                    pe.wait_ge(hy_ztok, ZT(L) + (6 if L < DEPTH - 1 else 4))
                for j in range(2 * nt):
                    i, p = divmod(j, 2)
                    if i:
                        pe.wait_ge((hy_zs, hy_comb)[p], HPR(run) + i)
                    for t in range(lt):
                        mm = pe.matmul(pf[:, 512 * (6 + p):512 * (7 + p)], fwd[:, p * lt + t, 128 * i:128 * i + 128],
                                       zt[:, t0 + p * lt + t, :], start=(t == 0), stop=(t == lt - 1))
                    mm.then_inc(hy_spec, 1)
                if not is_c:
                    project(L, "C", range(2))
                for lm in HYENA_MODS[run]:
                    mod_tile(*lm, "Dc")
                pe.wait_ge(hy_prod, HPR(run) + nt)
                if not is_c:
                    pe.wait_ge(dft_in, 16 * (L + 1))
                for cc in range(4):
                    if cc >= 2:
                        pe.wait_ge(hy_out, 4 * run + cc - 1)
                    f = slice(128 * cc, 128 * cc + 128)
                    col = 512 * (4 + cc % 2)
                    for p in range(2):
                        for j in range(nt):
                            src = at(KSPEC, 8, 512)[:, j if j < lt else nt + j - lt, f] if p == 0 else \
                                zs[:, lt + j if j < lt else nt + j, f]
                            mm = pe.matmul(pf[:, col + p * n // 2:col + (p + 1) * n // 2], src, inv[:, p * nt + j, :],
                                           start=(j == 0), stop=(j == nt - 1))
                    mm.then_inc(hy_inv, 1)

            def gla_alpha(L, hp, d):
                N = 2 * L + hp
                lr = at(LR, T)
                if (hp, d) == (0, 0):
                    wait_tile(pe, L, "lr", 0)
                    pe.wait_ge(aw_in, 16 * (L + 1))
                    pe.wait_ge(hy_out, 4 * len([r for r in hy_runs if r[0] <= L]))
                elif d == 0:
                    pe.wait_ge(v_done, value_no(L, "vg", 3) + 1)
                else:
                    pe.wait_ge(gl_z, 2 * N + 1)
                c0 = 128 * (2 * d + hp)
                pe.matmul(pf[:, 2048:2048 + SEQ], aw[:, c0:c0 + 128], lr[0:32, 0:SEQ], start=True, stop=True)
                pe.matmul(pf[:, 2048 + SEQ:2048 + T], aw[:, c0:c0 + 128], lr[0:32, SEQ:T],
                          start=True, stop=True).then_inc(gl_alpha, 1)

            def gla_turn(L, hp):
                N = 2 * L + hp
                for d in range(2):
                    pe.wait_ge(gl_ke, 2 * N + d + 1)
                    for tt in range(6):
                        mm = pe.transpose(pf[:, 1024 * d + 128 * tt:1024 * d + 128 * tt + 128],
                                          at(GE, 2, 3, T)[:, d, 2, 128 * tt:128 * tt + 128], ident[:, :])
                    mm.then_inc(gl_tr, 1)

            def gla_squares(L, hp):
                N, oc = 2 * L + hp, width(L, False)
                for e in range(2):
                    base = 2048 + 1024 * e
                    pe.wait_ge(gl_sq, 2 * N + e + 1)
                    for c0, c1 in ((0, SEQ), (SEQ, oc)):
                        if c1 > c0:
                            mm = pe.matmul(pf[:, base + c0:base + c1], ones[:, :], at(GSQ[e], T)[:, c0:c1], start=True, stop=True)
                    mm.then_inc(gl_ss, 1)

            def gla(L):
                oc = width(L, False)
                nto = oc // 128
                v = at(GV, 6, 512)
                E = at(GE, 2, 3, T)
                S = at(GS, 2, 12, 128)
                A = at(GAT, 2, 2, T)
                wait_tile(pe, L, "gg", 3)
                wait_tile(pe, L, "gg", 2)
                pe.wait_ge(gl_z, 4 * L + 4)
                gla_turn(L, 0)
                for hp in range(2):
                    N = 2 * L + hp
                    if hp:
                        pe.wait_ge(gl_rd, 2 * N)
                    pe.wait_ge(gl_ket, 2 * N + 2)
                    for d in range(2):
                        ket = E[:, d, 2, :].rearrange("p (t f) -> p t f", t=6)
                        base = 2048 if d == 0 else 0
                        for p in range(2):
                            for tt in range(6):
                                for e in range(2):
                                    rows = slice(64 * p, 64 * p + 64)
                                    mm = pe.matmul(pf[64 * e:64 * e + 64, base + 1024 * p + 128 * tt:base + 1024 * p + 128 * tt + 128],
                                                   ket[rows, tt, 64 * e:64 * e + 64],
                                                   v[rows, tt, 128 * (2 * hp + e):128 * (2 * hp + e) + 128],
                                                   start=True, stop=True)
                        mm.then_inc(gl_kv, 1)
                    for e in range(2):
                        rows = slice(64 * e, 64 * e + 64)
                        for d in range(2):
                            pe.wait_ge(gl_state, 2 * N + e + 1)
                            pe.wait_ge(gl_qk, 2 * N + d + 1)
                            base = (2048 if e == 0 else 0) + 1024 * d
                            for tt in range(nto):
                                mm = pe.matmul(pf[:, base + 128 * tt:base + 128 * tt + 128],
                                               E[rows, d, 1, 128 * tt:128 * tt + 128], E[rows, d, 0, 128 * tt:128 * tt + 128],
                                               start=True, stop=True)
                            mm.then_inc(gl_at, 1)
                    for e in range(2):
                        rows = slice(64 * e, 64 * e + 64)
                        base = 2048 + 1024 * e
                        vc = slice(128 * (2 * hp + e), 128 * (2 * hp + e) + 128)
                        pe.wait_ge(gl_atc, 4 * N + 2 * e + 2)
                        pe.wait_ge(gl_state, 2 * N + 2)
                        for tt in range(nto):
                            o = pf[:, base + 128 * tt:base + 128 * tt + 128]
                            pe.matmul(o, v[:, tt, vc], A[:, e, 0, 128 * tt:128 * tt + 128], start=True, stop=False)
                            pe.matmul(o, v[:, tt, vc], A[:, e, 1, 128 * tt:128 * tt + 128], start=False, stop=False)
                            for p in range(2):
                                for d in range(2):
                                    mm = pe.matmul(o[:, 64 * p:64 * p + 64], S[rows, d, state_slot(d, 2 * tt + p), :],
                                                   E[rows, d, 0, 128 * tt + 64 * p:128 * tt + 64 * p + 64],
                                                   start=False, stop=(p == 1 and d == 1))
                        mm.then_inc(gl_o, 1)
                    if hp == 0:
                        gla_squares(L, 0)
                        gla_turn(L, 1)

            def rotary(L, i):
                wait_tile(pe, L, *(("qb", i - 1) if i else ("kb", 0)))
                if i == 0:
                    pe.wait_ge(v_done, value_no(L, "vb", 0) + 1)
                if i >= 2:
                    pe.wait_ge(rope_done, 5 * L + i - 1)
                src = at(BQ, 4, T)[:, i - 1, 0:SEQ] if i else at(BK, T)[:, 0:SEQ]
                pe.matmul(pf[:, 512 * (4 + i % 2):512 * (5 + i % 2)], rotm[:, :], src, start=True, stop=True).then_inc(rope_rot, 1)

            def attention(L, mixer):
                A = mixer == "A"
                q_, k_ = (at(AQ, 4, T), at(AK, 4, T)) if A else (at(BQ, 4, T), at(BK, 1, T))
                v_ = at(AV, 6, 512) if A else at(BV, 6, 128)
                pt_at = APT if A else BTMP + 1280
                us = units(mixer, L)
                u0 = unit0[L, mixer]
                gates = "ga" if A else "gb"

                def scores(n):
                    q, i, p = us[n]
                    rows = slice(64 * p, 64 * p + 64)
                    base = 1024 * p
                    if n >= 2:
                        pe.wait_ge(at_p, u0 + n - 1)
                    lhs = q_[rows, i, 128 * q:128 * q + 128]
                    ki = i if A else 0
                    blocks = key_blocks(mixer, q)
                    if A and q < 4:
                        c0 = NATTEN_COL0[q]
                        pe.matmul(pf[:, base:base + 256].rearrange("p (r c) -> p r c", c=2 * NKC), lhs,
                                  k_[rows, ki, 0:SEQ].rearrange("p (r c) -> p r c", c=GRID_W)[:, :, c0:c0 + 32],
                                  start=True, stop=True)
                        mm = pe.matmul(pf[:, base + 256:base + 512], lhs, k_[rows, ki, SEQ:T], start=True, stop=True)
                    elif q >= 4:
                        mm = pe.matmul(pf[:, base:base + 256], lhs, k_[rows, ki, SEQ:T], start=True, stop=True)
                    else:
                        for c, b in enumerate(blocks):
                            edge = b < 4 and b != q
                            mm = pe.matmul(pf[:, base + 128 * c:base + 128 * c + 128], lhs,
                                           k_[rows, ki, 128 * b:128 * b + 128], start=True, stop=not edge)
                            if edge:
                                mm = pe.matmul(pf[:, base + 128 * c:base + 128 * c + 128], ident_b[:, :],
                                               bmask[:, 0 if b < q else 1, :], start=False, stop=True)
                    mm.then_inc(at_s, 1)

                def transposes(n):
                    q, i, p = us[n]
                    P = at((AP_ if A else BTMP) + 640 * p, 640)
                    pe.wait_ge(at_p, u0 + n + 1)
                    if n >= 2:
                        pe.wait_ge(at_ptc[p], (u0 + n) // 2)
                    nb = len(key_blocks(mixer, q))
                    for c in range(min(nb, 4)):
                        mm = pe.transpose(pf[:, 2048 + 512 * p + 128 * c:2048 + 512 * p + 128 * c + 128],
                                          P[:, 128 * c:128 * c + 128], ident[:, :])
                    if nb == 5:
                        pe.wait_ge(at_y, qt0[L, mixer] + turned[0])
                        pe.wait_ge(at_ptc[1 - p], (u0 + n + 1) // 2)
                        mm = pe.transpose(pf[:, 3072:3200], P[:, 512:640], ident[:, :])
                    mm.then_inc(at_pt, 1)

                def values(n):
                    q, i, p = us[n]
                    hh = head(mixer, i, p)
                    PT = at(pt_at + 640 * p, 5, 128)
                    pe.wait_ge(at_ptc[p], (u0 + n) // 2 + 1)
                    if n == 0:
                        wait_tile(pe, L, gates, 3)
                    if n == 0 and A:
                        pe.wait_ge(vblk_in, 16 * 32 * (L + 1))
                    if i == 0 and p == 0 and (n or (L, mixer) != (0, "A")):
                        pe.wait_ge(at_on, qt0[L, mixer] + q)
                    blocks = key_blocks(mixer, q)
                    for c, b in enumerate(blocks):
                        if A:
                            rhs = at(AVB[q % 4], 2, 512)[:, c % 2, 64 * hh:64 * hh + 64] if b < 0 else v_[:, b, 64 * hh:64 * hh + 64]
                        else:
                            rhs = v_[:, b, 64 * p:64 * p + 64]
                        mm = pe.matmul(pf[:, 3584 + 64 * hh:3584 + 64 * hh + 64], PT[:, c, :], rhs,
                                       start=(c == 0), stop=(c == len(blocks) - 1))
                    mm.then_inc(at_o, 1)

                turned = [0]

                def turn(q, n=None):
                    if n is not None and len(key_blocks(mixer, us[n][0])) == 5:
                        for p in range(2):
                            pe.wait_ge(at_ptc[p], (u0 + n) // 2 + 1)
                    turned[0] = q + 1
                    if qt0[L, mixer] + q:
                        pe.wait_ge(at_y, qt0[L, mixer] + q)
                    pe.wait_ge(at_on, qt0[L, mixer] + q + 1)
                    o = at(AO if A else BTMP + 2560, 512)
                    for f in range(4):
                        mm = pe.transpose(pf[:, 3072 + 128 * f:3072 + 128 * f + 128], o[:, 128 * f:128 * f + 128], ident[:, :])
                    mm.then_inc(at_ot, 1)

                wait_tile(pe, L, gates, 1)
                wait_tile(pe, L, gates, 2)
                if not A:
                    pe.wait_ge(rope_done, 5 * L + 2)
                scores(0)
                scores(1)
                if not A:
                    pe.wait_ge(rope_done, 5 * (L + 1))
                    pe.wait_ge(at_y, last_at_y(L, "A"))
                project(L, mixer, [len(TILES[mixer]) - 1])
                pe.wait_ge(v_done, value_no(L, "va" if A else "vb", 3 if A else 0) + 1)
                for n in range(0, len(us), 2):
                    q = us[n][0]
                    transposes(n)
                    transposes(n + 1)
                    if n + 2 < len(us):
                        scores(n + 2)
                    if n + 3 < len(us):
                        scores(n + 3)
                    if n % 8 == 0 and q:
                        turn(q - 1, n)
                    values(n)
                    values(n + 1)
                turn(us[-1][0])

            def merge(L):
                g0, s0 = POS["gate", L, 0, 0], SPLIT_NO["gate", L, 0, 0]
                last = L == DEPTH - 1
                pe.wait_ge(at_y, last_at_y(L, "B"))
                with pe.Fori(0, KT // 2) as it:
                    for v in range(8):
                        bi = v % 4
                        n = g0 + gate_place(v)
                        nb = g0 + BRANCH_TILES * (v // 4) + (2, 5)[bi // 2]
                        if bi % 2 == 0:
                            pe.wait_ge(ring_full[nb % SLOTS], 32 * it + 16 * (nb // SLOTS + 1))
                        pe.wait_ge(mg_prod, 8 * it + (MG(L) + v + 1))
                        src = y["ABCD"[bi]]
                        for c0, c1 in ((0, SEQ), (SEQ, T)):
                            if last and c0:
                                continue
                            for k in range(4):
                                mm = pe.matmul(pf[:, 2048 * (v % 2) + 1024 + c0:2048 * (v % 2) + 1024 + c1],
                                               slot_br[:, nb % SLOTS, bi % 2, k, :], src[:, k, c0:c1],
                                               start=(k == 0), stop=(k == 3))
                        if bi % 2 == 1:
                            mm.then_inc(ring_read[nb % SLOTS], 1)
                        pe.wait_ge(ring_read[n % SLOTS], 2 * it + (n // SLOTS + 1))
                        multiply((s0 + v) % 2, 2048 * (v % 2), width(L, False)).then_inc(mg_unit, 1)
                for m in range(KT):
                    key = ("proj", L, "out", m)
                    t = tile_no[L, "out", m]
                    pe.wait_ge(ring_read[slot(key)], turns(key))
                    if m >= 2:
                        pe.wait_ge(drained[t % 2], t // 2)
                    multiply(SPLIT_NO[key] % 2, pair(t), width(L, False),
                             KT * (2 * L + 1) + 1 if m == 0 else None).then_inc(tile_ready, 1)

            for step in range(filter_steps(4)):
                filter_step(HYN[False], 0, step)
                if step == 0:
                    pe.wait_ge(csil_ready, 1)
                    pe.wait_ge(const_in, 16)
                mod_tile(*MOD_AT["start"][step], "start")
            barrier(pe, PH(0, "filter"))
            for L in range(DEPTH):
                norm(L)
                for lm in MOD_AT[f"norm{L}"]:
                    mod_tile(*lm, f"norm{L}")
                if L == 0:
                    pe.wait_ge(mask_in, 16 * 5)
                project(L, "D", range(16))
                hyena(2 * L)
                if L == 0:
                    arrive(pe)
                if L < DEPTH - 1:
                    for step in range(filter_steps(2)):
                        filter_step(HYN[True], 1, step)
                        if step < len(FILTER_MODS):
                            mod_tile(*FILTER_MODS[step], "Dc")
                    hyena(2 * L + 1)
                project(L, "C", range(2, 13))
                gla(L)
                project(L, "A", range(15))
                attention(L, "A")
                project(L, "B", range(9))
                attention(L, "B")
                merge(L)
            pe.wait_ge(norm_sum, (KT - 1) * (DEPTH + 1))
            mm = pe.matmul(pf[:, NORM_COL:NORM_COL + SEQ], ones[:, :], at(NSQ_AT[DEPTH][0], T)[:, 0:SEQ], start=True, stop=True)
            mm.then_inc(norm_ps, 1)

        @block.scalar
        def _(act):
            def high_part(n):
                key = SPLITS[n]
                act.wait_ge(ring_full[slot(key)], 16 * turns(key))
                act.activation(w_hi[:, n % 2], slot_tile[:, slot(key)], ACT.Copy).then_inc(split_hi, 1)

            def drain_tile(L, name, i, need, dst, func, scale=1.0, rows=128):
                t = tile_no[L, name, i]
                w = width(L, need)
                act.wait_ge(tile_ready, t + 1)
                src = pf[0:rows, pair(t):pair(t) + w]
                act.activation(dst, src, func, scale=scale).then_inc(drained[t % 2], 1)

            def drain(L, mixer, numbers):
                for n in numbers:
                    what, i, _, need = TILES[mixer][n]
                    key = ("proj", L, what, i)
                    if mixer != "C" or n >= 2:
                        wait_used(act, key)
                        high_part(next_split(key))
                    w = width(L, need)
                    if what == "u":
                        t = tile_no[L, what, i]
                        dst = (at(HX0, 4, T), at(HZ, 4, T), at(HV, 4, T))[i // 4][:, i % 4, 0:w]
                        act.wait_ge(tile_ready, t + 1)
                        act.activation(dst, pf[:, pair(t):pair(t) + w], ACT.Identity,
                                       scale=par[:, P_CW + 12 + i:P_CW + 13 + i],
                                       bias=par[:, P_CB + i:P_CB + i + 1]).then_inc(conv_ready, 1)
                    elif what in ("gd", "gg", "ga", "gb"):
                        drain_tile(L, what, i, need, y[mixer][:, i, 0:w], ACT.Silu)
                    elif what == "lr":
                        drain_tile(L, what, i, need, at(LR, T)[0:32, 0:w], ACT.Copy, rows=32)
                    elif what in VALUES:
                        drain_tile(L, what, i, need, at(VT_AT[mixer] + T * (value_no(L, what, i) % 2), T), ACT.Copy)
                    elif what == "qa":
                        t = tile_no[L, what, i]
                        q = at(AQ + T * i, T)
                        act.wait_ge(tile_ready, t + 1)
                        ins = act.activation(q[:, 0:SEQ].rearrange("p (j r c) -> p r j c", r=8, c=NKC),
                                             pf[:, pair(t):pair(t) + SEQ].rearrange("p (r j c) -> p r j c", r=8, c=NKC),
                                             ACT.Copy, scale=HD ** -0.5)
                        if w > SEQ:
                            ins = act.activation(q[:, SEQ:T], pf[:, pair(t) + SEQ:pair(t) + T], ACT.Copy, scale=HD ** -0.5)
                        ins.then_inc(drained[t % 2], 1)
                    else:
                        off = {"ka": AK, "qb": BQ, "kb": BK, "qg": GQ, "kg": GK}[what]
                        drain_tile(L, what, i, need, at(off + T * i, T)[:, 0:w], ACT.Copy,
                                   scale=HD ** -0.5 if what[0] == "q" else 1.0)
                    if (L, mixer) == (1, "D"):
                        filter_step(HYN[False], 2, n)
                    if mixer == "C" and n == 4:
                        gla_log(L, 0)
                    if mixer == "C" and n in (6, 7):
                        gla_decay(L, 0, n - 6)
                        gla_decay_rest(L, 0, n - 6)
                    if mixer == "A" and n in (1, 2):
                        gla_root(L, 1, n - 1)

            def filter_step(c, run, step):
                nt, n = c["nt"], c["n"]
                bd = FD(run)
                if step < 3:
                    act.wait_ge(filt_dve, bd + step + 1)
                    dst = at((FH0, FH1, FH0)[step], 512)[0:64, 0:n]
                    act.activation(dst, at(FT, 512)[0:64, 0:n], ACT.Sin).then_inc(filt_act, 1)
                elif step == 3 + nt:
                    act.wait_ge(filt_dve, bd + 3 + 2 * nt)
                    for j in range(2 * nt):
                        if j >= 2:
                            act.wait_ge(filt_pe, FP(run) + 3 + 2 * nt + j - 1)
                        src = at(FHF if j % 2 == 0 else FHB, 4, 512)[:, j // 2, :]
                        act.activation(at(FABS + 512 * (j % 2), 512), src, ACT.Abs).then_inc(filt_act, 1)

            def square(n, k):
                w = T if n < DEPTH else SEQ
                if k >= 3:
                    act.wait_ge(norm_sum, (KT - 1) * n + k - 2)
                act.activation(at(NSQ_AT[n][0 if k == 0 else 1 + k % 2], T)[:, 0:w], at(X_AT, KT, T)[:, k, 0:w], ACT.Square)\
                    .then_inc(norm_sq, 1)

            def norm(L, x):
                act.wait_ge(norm_ms, L + 1)
                act.activation(at(NRS, T), at(NRS, T), ACT.Sqrt).then_inc(norm_rt, 1)
                for k in range(KT):
                    act.wait_ge(norm_t, KT * L + k + 1)
                    for c, (c0, c1) in enumerate(((0, SEQ), (SEQ, T))):
                        ins = act.activation(h_hi[:, k, c0:c1], x[:, k, c0:c1], ACT.Identity, bias=mod[:, L, k, c:c + 1])
                    ins.then_inc(h_high, 1)

            def hyena(run):
                L, is_c = hy_runs[run]
                c = HYN[is_c]
                if not is_c:
                    for j in range(6 if L < DEPTH - 1 else 4):
                        act.wait_ge(hy_tr, ZT(L) + j + 1)
                        act.activation(at(HV, 6, 512)[:, j, :], pf[:, 512 * (4 + j % 2):512 * (5 + j % 2)], ACT.Copy)\
                            .then_inc(hy_ztok, 1)
                act.wait_ge(filt_dve, FD(run + 1))
                nt = c["nt"]
                for i in range(nt):
                    act.wait_ge(hy_spec, 2 * HPR(run) + 2 * i + 1)
                    act.activation(at(ZSPEC, 8, 512)[:, spectrum_pair(nt, i)[1], :], pf[:, 3072:3584], ACT.Copy).then_inc(hy_zs, 1)

            def gla_log(L, hp):
                N = 2 * L + hp
                zb = [at(GL + 1536 * d, T) for d in range(2)]
                lb = [at(GL + 1536 * d + T, T) for d in range(2)]
                for d in range(2):
                    act.wait_ge(gl_z, 2 * N + d + 1)
                    act.activation(lb[d], zb[d], ACT.Abs).then_inc(gl_ln, 1)
                for d in range(2):
                    act.wait_ge(gl_ln, 6 * N + d + 1)
                    act.activation(lb[d], lb[d], ACT.Exp, scale=-1.0).then_inc(gl_ln, 1)
                for d in range(2):
                    act.wait_ge(gl_ln, 6 * N + d + 3)
                    act.activation(lb[d], lb[d], ACT.Ln, bias=1.0).then_inc(gl_ln, 1)

            def gla_decay(L, hp, d):
                E, lb = at(GE, 2, 3, T), at(GL + 1536 * d + T, T)
                act.wait_ge(gl_cum, 4 * L + 2 * hp + d + 1)
                act.activation(E[:, d, 0, :], lb, ACT.Exp, scale=1.0 / 16)
                act.activation(E[:, d, 1, :], lb, ACT.Exp, scale=-1.0 / 16).then_inc(gl_exp, 1)

            def gla_decay_rest(L, hp, d):
                act.wait_ge(gl_rest, 4 * L + 2 * hp + d + 1)
                act.activation(at(GE, 2, 3, T)[:, d, 2, :], at(GL + 1536 * d, T), ACT.Exp, scale=1.0 / 16).then_inc(gl_exp2, 1)

            def gla_root(L, hp, e):
                act.wait_ge(gl_ms, 4 * L + 2 * hp + e + 1)
                r = at(GSQ[e], T)[:, 0:width(L, False)]
                act.activation(r, r, ACT.Sqrt).then_inc(gl_rt, 1)

            def gla(L):
                oc = width(L, False)
                for hp in range(2):
                    N = 2 * L + hp
                    for d in range(2):
                        act.wait_ge(gl_tr, 2 * N + d + 1)
                        act.activation(at(GE, 2, 3, T)[:, d, 2, :], pf[:, 1024 * d:1024 * d + T], ACT.Copy).then_inc(gl_ket, 1)
                    if hp == 0:
                        gla_log(L, 1)
                    else:
                        gla_decay(L, 1, 0)
                        gla_decay(L, 1, 1)
                        gla_root(L, 0, 0)
                        gla_root(L, 0, 1)
                        act.wait_ge(gl_fin, 2 * N)
                    for e in range(2):
                        base = 2048 + 1024 * e
                        act.wait_ge(gl_o, 2 * N + e + 1)
                        act.activation(at(GO[e], T)[:, 0:oc], pf[:, base:base + oc], ACT.Copy)
                        act.activation(at(GSQ[e], T)[:, 0:oc], pf[:, base:base + oc], ACT.Square).then_inc(gl_sq, 1)
                        if (hp, e) == (0, 0):
                            gla_decay_rest(L, 1, 0)
                            gla_decay_rest(L, 1, 1)

            def attention(L, mixer):
                A = mixer == "A"
                us = units(mixer, L)
                u0 = unit0[L, mixer]
                p_at = AP_ if A else BTMP
                pt_at = APT if A else BTMP + 1280

                def exps(n):
                    q, i, p = us[n]
                    w = 128 * len(key_blocks(mixer, q))
                    hh = head(mixer, i, p)
                    act.wait_ge(at_max, u0 + n + 1)
                    if n >= 2:
                        act.wait_ge(at_pt, u0 + n - 1)
                    if hh == 0 and q >= 2:
                        act.wait_ge(at_on, qt0[L, mixer] + q - 1)
                    act.activation(at(p_at + 640 * p, 640)[:, 0:w], pf[:, 1024 * p:1024 * p + w], ACT.Exp,
                                   bias=stat[:, q % 2, 0, hh:hh + 1],
                                   accum_out=stat[:, q % 2, 1, hh:hh + 1]).then_inc(at_p, 1)

                def copies(n):
                    q, i, p = us[n]
                    nb = len(key_blocks(mixer, q))
                    act.wait_ge(at_pt, u0 + n + 1)
                    if n >= 2:
                        act.wait_ge(at_o, u0 + n - 1)
                    PT = at(pt_at + 640 * p, 640)
                    w = 128 * min(nb, 4)
                    ins = act.activation(PT[:, 0:w], pf[:, 2048 + 512 * p:2048 + 512 * p + w], ACT.Copy)
                    if nb == 5:
                        ins = act.activation(PT[:, 512:640], pf[:, 3072:3200], ACT.Copy)
                    ins.then_inc(at_ptc[1], 1)

                exps(0)
                exps(1)
                drain(L, mixer, [len(TILES[mixer]) - 1])
                for n in range(0, len(us), 2):
                    copies(n + 1)
                    if n + 2 < len(us):
                        exps(n + 2)
                    if n + 3 < len(us):
                        exps(n + 3)
                    if mixer == "B" and n % 8 == 6:
                        q = us[n][0]
                        act.wait_ge(at_sum, QB(L) + q + 1)
                        act.activation(stat[:, q % 2, 3, :], stat[:, q % 2, 3, :], ACT.Exp).then_inc(at_sink, 1)

            def merge(L):
                w = width(L, False)
                g0, s0 = POS["gate", L, 0, 0], SPLIT_NO["gate", L, 0, 0]
                with act.Fori(0, KT // 2) as it:
                    for v in range(8):
                        act.wait_ge(mg_unit, 8 * it + (MG(L) + v + 1))
                        act.wait_ge(mg_prod, 8 * it + (MG(L) + v + 1))
                        act.activation(at(MGATE + T * (v % 2), T)[:, 0:w], pf[:, 2048 * (v % 2):2048 * (v % 2) + w],
                                       ACT.Sigmoid).then_inc(mg_gate, 1)
                        n = g0 + gate_place(v + 2)
                        act.wait_ge(ring_full[n % SLOTS], 32 * it + 16 * (n // SLOTS + 1))
                        act.activation(w_hi[:, (s0 + v) % 2], slot_tile[:, n % SLOTS], ACT.Copy).then_inc(split_hi, 1)
                act.wait_ge(mg_sum, 3 * KT * (L + 1))
                for k in range(KT):
                    act.activation(h_hi[:, k, 0:w], at(MACC, KT, T)[:, k, 0:w], ACT.Copy).then_inc(h_high, 1)
                for m in range(KT):
                    key = ("proj", L, "out", m)
                    if next_split(key) is not None:
                        wait_used(act, key)
                        high_part(next_split(key))
                    wait_tile(act, L, "out", m)
                    square(L + 1, m)

            act.wait_ge(par_first, 16)
            act.activation(csil[:, :, :], par[:, P_C:P_C + 16].rearrange("p (k c) -> p k c", c=2), ACT.Silu)\
                .then_inc(csil_ready, 1)
            for step in range(filter_steps(4)):
                filter_step(HYN[False], 0, step)
                if step == 8:
                    act.wait_ge(x_in, 16)
                if step >= 8:
                    square(0, step - 8)
            barrier(act, PH(0, "filter"))
            for L in range(DEPTH):
                norm(L, at(X_AT, KT, T))
                if L == 0:
                    high_part(0)
                    high_part(1)
                drain(L, "D", range(16))
                hyena(2 * L)
                if L == DEPTH - 1:
                    early_parts(act, L, high_part)
                else:
                    barrier(act, PH(L, "D"))
                if L < DEPTH - 1:
                    for step in range(filter_steps(2)):
                        filter_step(HYN[True], 1, step)
                    hyena(2 * L + 1)
                    early_parts(act, L, high_part)
                act.wait_ge(hy_inv, 4 * len([r for r in hy_runs if r[0] <= L]))
                if L == 0:
                    act.wait_ge(mod_done, MOD_PLACES.index("Dc") + 1)
                drain(L, "C", range(13))
                gla(L)
                drain(L, "A", range(15))
                attention(L, "A")
                drain(L, "B", range(9))
                attention(L, "B")
                merge(L)
            act.wait_ge(norm_ms, DEPTH + 1)
            act.activation(at(MGATE, SEQ), at(MGATE, SEQ), ACT.Sqrt).then_inc(norm_rt, 1)

        @block.vector
        def _(dve):
            chain = [0]

            def link(ins):
                chain[0] += 1
                ins.then_inc(dve_chain, 1)
                dve.wait_ge(dve_chain, chain[0])

            def filter_step(c, run, step):
                nt, n = c["nt"], c["n"]
                ba, bp = FA(run), FP(run)
                hf, hb, dec = at(FHF, 4, 512), at(FHB, 4, 512), dec_at(run)
                rl = at(FHF, 512)
                if step < 3:
                    k = step
                    t, r = at(FT, 512)[0:64, 0:n], at(FABS, 512)[0:64, 0:n]
                    dve.wait_ge(filt_pe, bp + k + 1)
                    if k:
                        dve.wait_ge(filt_act, ba + k)
                    link(dve.tensor_scalar(t, pf[0:64, 2048:2048 + n], par[0:64, P_B1 + k:P_B1 + k + 1],
                                           par[0:64, P_FREQ:P_FREQ + 1], ALU.add, ALU.mult))
                    link(dve.tensor_scalar(r, t, 1.0 / (2.0 * math.pi), ROUND, ALU.mult, ALU.add))
                    link(dve.tensor_scalar(r, r, ROUND, None, ALU.subtract))
                    link(dve.scalar_tensor_tensor(t, r, -TWO_PI_HI, t, ALU.mult, ALU.add))
                    link(dve.scalar_tensor_tensor(t, r, -TWO_PI_LO, t, ALU.mult, ALU.add))
                    dve.tensor_scalar(t, t, PI_IN, -PI_IN, ALU.min, ALU.max).then_inc(filt_dve, 1)
                elif step < 3 + nt:
                    if step == 3:
                        dve.wait_ge(dec_in, 16 * (run + 1))
                    for j in (2 * (step - 3), 2 * (step - 3) + 1):
                        dve.wait_ge(filt_pe, bp + 3 + j + 1)
                        dst = (hf, hb)[j % 2][:, j // 2, :]
                        ins = dve.tensor_tensor(dst, pf[:, 512 * (5 + j % 2):512 * (6 + j % 2)], dec[:, j // 2, :], ALU.mult)
                        if j == 1:
                            link(ins)
                            ins = dve.memset(hb[0:1, 0, :], 0.0)
                        ins.then_inc(filt_dve, 1)
                elif step == 3 + nt:
                    dve.wait_ge(filt_act, ba + 3 + 2 * nt)
                    dve.wait_ge(filt_dve, FD(run) + 3 + 2 * nt)
                    dve.tensor_tensor(dec[:, 0:nt, :], hf[:, 0:nt, :], hb[:, 0:nt, :], ALU.add).then_inc(filt_dve, 1)
                    dve.wait_ge(filt_dve, FD(run) + 3 + 2 * nt + 1)
                    dve.tensor_tensor(hb[:, 0:nt, :], hf[:, 0:nt, :], hb[:, 0:nt, :], ALU.subtract).then_inc(filt_dve, 1)
                else:
                    i, p = divmod(step - 4 - nt, 2)
                    sines = 2 * i >= nt
                    ks, tmp = at(KSPEC, 8, 512), at(FHF + 512, 512)
                    done = FD(run) + 3 + 2 * nt + 3 + 2 * i + p
                    if (i, p) == (0, 0):
                        dve.wait_ge(filt_pe, bp + 3 + 4 * nt)
                        dve.wait_ge(filt_dve, FD(run) + 3 + 2 * nt + 2)
                        dve.reciprocal(rl, pf[:, 3584:4096]).then_inc(filt_dve, 1)
                        dve.wait_ge(filt_dve, FD(run) + 3 + 2 * nt + 3)
                    low, high = spectrum_pair(nt, i)
                    dve.wait_ge(filt_pe, bp + 3 + 4 * nt + 2 * i + p + (2 if sines else 1))
                    if p == 0:
                        dve.tensor_tensor(ks[:, high, :], pf[:, 2560:3072], rl, ALU.mult).then_inc(filt_dve, 1)
                        dve.wait_ge(filt_dve, done + 1)
                        if 2 * i == nt:
                            link(dve.tensor_tensor(ks[0:1, high, :], pf[0:1, 2048:2560], rl[0:1, :], ALU.mult))
                    else:
                        dve.tensor_tensor(tmp, pf[:, 3072:3584], rl, ALU.mult).then_inc(filt_dve, 1)
                        dve.wait_ge(filt_dve, done + 1)
                        link(dve.tensor_tensor(ks[:, low, :], tmp, ks[:, high, :], ALU.add))
                        if sines:
                            ins = dve.tensor_tensor(ks[:, high, :], tmp, ks[:, high, :], ALU.subtract)
                            if i < nt - 1:
                                link(ins)
                            else:
                                ins.then_inc(filt_dve, 1)
                                dve.wait_ge(filt_dve, FD(run + 1))
                        else:
                            link(dve.tensor_tensor(ks[:, high, :], ks[:, high, :], tmp, ALU.subtract))

            def low_part(n):
                key = SPLITS[n]
                dve.wait_ge(split_hi, n + 1)
                dve.tensor_tensor(w_lo[:, n % 2], slot_tile[:, slot(key)], w_hi[:, n % 2].bitcast(F32), ALU.subtract)\
                    .then_inc(ring_read[slot(key)], 1)

            def mod_products(L, m):
                key, n = ("mod", L, m), MOD_NO[L, m]
                place = [p for p in MOD_PLACES if (L, m) in MOD_AT[p]][0]
                j = MOD_AT[place].index((L, m))
                dve.wait_ge(ring_read[slot(key)], turns(key))
                if n:
                    dve.wait_ge(mod_tr, n)
                col = MOD_COL[place]
                dve.tensor_copy(mod_row[:, :], pf[0:2, col:col + 128]).then_inc(row_done, 1)

            def modulation(place):
                dve.wait_ge(mod_tr, MOD_NO[MOD_AT[place][-1]] + 1)
                for L in range(DEPTH):
                    ms = [m for l, m in MOD_AT[place] if l == L]
                    if ms:
                        c0 = MOD_COL[place] + 128 + 2 * MOD_AT[place].index((L, ms[0]))
                        ins = dve.tensor_copy(mod[:, L, ms[0]:ms[-1] + 1, :],
                                              pf[:, c0:c0 + 2 * len(ms)].rearrange("p (m c) -> p m c", c=2))
                ins.then_inc(mod_done, 1)
                dve.wait_ge(mod_done, MOD_PLACES.index(place) + 1)

            def add_bias(L, m0, m1):
                for c in range(2):
                    link(dve.tensor_tensor(mod[:, L, m0:m1, c], mod[:, L, m0:m1, c], par[:, P_BMOD + m0:P_BMOD + m1], ALU.add))

            def add_square(n, k):
                w = T if n < DEPTH else SEQ
                total = at(NSQ_AT[n][0], T)[:, 0:w]
                dve.wait_ge(norm_sq, KT * n + k + 1)
                if k > 1:
                    dve.wait_ge(norm_sum, (KT - 1) * n + k - 1)
                dve.tensor_tensor(total, total, at(NSQ_AT[n][1 + k % 2], T)[:, 0:w], ALU.add).then_inc(norm_sum, 1)

            def norm(L, x):
                rstd = at(NRS, T)
                if L == 0:
                    modulation("start")
                add_bias(L, 0, 2 * KT if L == 0 else 20)
                for c in range(2):
                    link(dve.scalar_tensor_tensor(nscale[:, :, c], mod[:, L, KT:2 * KT, c], 1.0, par[:, P_NORM:P_NORM + KT],
                                                  ALU.add, ALU.mult))
                dve.wait_ge(norm_ps, L + 1)
                link(dve.tensor_scalar(rstd, pf[:, NORM_COL:NORM_COL + T], 1.0 / D_MODEL, EPS, ALU.mult, ALU.add))
                dve.reciprocal(rstd, rstd).then_inc(norm_ms, 1)
                mod_products(*MOD_AT[f"norm{L}"][0])
                if L:
                    dve.wait_ge(x_saved, 16 * KT * L)
                dve.wait_ge(norm_rt, L + 1)

                def scaled(k):
                    for c, (c0, c1) in enumerate(((0, SEQ), (SEQ, T))):
                        ins = dve.scalar_tensor_tensor(x[:, k, c0:c1], x[:, k, c0:c1], nscale[:, k, c:c + 1], rstd[:, c0:c1],
                                                       ALU.mult, ALU.mult)
                    ins.then_inc(norm_t, 1)

                scaled(0)
                scaled(1)
                for k in range(KT):
                    dve.wait_ge(h_high, 2 * KT * L + k + 1)
                    for c, (c0, c1) in enumerate(((0, SEQ), (SEQ, T))):
                        ins = dve.scalar_tensor_tensor(h_lo[:, k, c0:c1], x[:, k, c0:c1], mod[:, L, k, c:c + 1],
                                                       h_hi[:, k, c0:c1].bitcast(F32), ALU.add, ALU.subtract)
                    ins.then_inc(h_ready, 1)
                    if k + 2 < KT:
                        scaled(k + 2)
                    if k % 2 == 0:
                        for lm in MOD_AT[f"norm{L}"][k // 2 + 1:k // 2 + 2]:
                            mod_products(*lm)
                if L == 0:
                    low_part(0)
                    low_part(1)
                modulation(f"norm{L}")
                if L:
                    add_bias(L, 20, MOD_TILES)

            def conv(L, i):
                segs = ((0, SEQ), (SEQ, T))[:2 if L < DEPTH - 1 else 1]
                t = tile_no[L, "u", i]
                dst = (at(HX0, 4, T), at(HZ, 4, T), at(HV, 4, T))[i // 4][:, i % 4, :]
                src = pf[:, pair(t):pair(t) + T]
                dve.wait_ge(conv_ready, 12 * L + i + 1)
                for c0, c1 in segs:
                    ins = dve.scalar_tensor_tensor(dst[:, c0 + 1:c1], src[:, c0:c1 - 1], par[:, P_CW + i:P_CW + i + 1],
                                                   dst[:, c0 + 1:c1], ALU.mult, ALU.add)
                link(ins)
                for c0, c1 in segs:
                    ins = dve.scalar_tensor_tensor(dst[:, c0:c1 - 1], src[:, c0 + 1:c1], par[:, P_CW + 24 + i:P_CW + 25 + i],
                                                   dst[:, c0:c1 - 1], ALU.mult, ALU.add)
                ins.then_inc(drained[t % 2], 1)

            def project(L, mixer, numbers):
                tiles = TILES[mixer]
                w = width(L, False)

                def values(what, i):
                    n = value_no(L, what, i)
                    dst = {"vg": at(GV, 6, 512), "va": at(AV, 6, 512), "vb": at(BV, 6, 128)}[what]
                    dve.wait_ge(v_tr, n + 1)
                    dve.tensor_copy(dst[:, :, 128 * i:128 * i + 128], pf[:, 2048:2048 + T].rearrange("p (t f) -> p t f", f=128))\
                        .then_inc(v_done, 1)

                for j in numbers:
                    what, i, _, _ = tiles[j]
                    if mixer != "C" or j >= 2:
                        low_part(next_split(("proj", L, what, i)))
                    if what == "u":
                        conv(L, i)
                    if what == "gd":
                        if i == 0:
                            for last in (10, 11):
                                t = tile_no[L, "u", last]
                                dve.wait_ge(drained[t % 2], t // 2 + 1)
                        z = at(HZ, 4, T)[:, i, 0:w]
                        dve.tensor_tensor(z, z, at(HV, 4, T)[:, i, 0:w], ALU.mult).then_inc(hy_z, 1)
                    if j and tiles[j - 1][0] in VALUES:
                        values(*tiles[j - 1][:2])
                    if (L, mixer) == (1, "D"):
                        filter_step(HYN[False], 2, j)
                    if mixer == "C":
                        if j in ALPHA_AT:
                            gla_z(L, *ALPHA_AT[j])
                        if j in (4, 5):
                            gla_cum(L, 0, j - 4)
                        if j == 11:
                            dve.memset(at(GAT, 2, 2, T), 0.0)
                            link(dve.memset(at(GS, 2, 12, 128)[:, :, 0, :], 0.0))
                        if j in (8, 9):
                            gla_rest_keys(L, 0, j - 8)
                            gla_queries(L, 0, j - 8)
                    if mixer == "B" and 4 <= j < 9:
                        rotary(L, j - 4)
                    if mixer == "A" and j < 4:
                        if j == 0:
                            gla_mean(L, 1, 0)
                            gla_mean(L, 1, 1)
                        else:
                            (gla_inverse if j < 3 else gla_finish)(L, 1, (j - 1) % 2)
                            if j == 3:
                                gla_finish(L, 1, 1)

            def hyena(run):
                L, is_c = hy_runs[run]
                c = HYN[is_c]
                nt, n, c0 = c["nt"], c["n"], 128 * c["t0"]
                ks, zs = at(KSPEC, 8, 512), at(ZSPEC, 8, 512)
                t1, t2 = at(HTMP, 512), at(HTMP + 512, 512)
                lt = nt // 2

                def ride(n):
                    for lm in HYENA_MODS[run][n:n + 1]:
                        mod_products(*lm)

                for i in range(nt):
                    low, high = spectrum_pair(nt, i)
                    odd = pf[:, 3584:4096]
                    dve.wait_ge(hy_zs, HPR(run) + i + 1)
                    dve.wait_ge(hy_spec, 2 * HPR(run) + 2 * i + 2)
                    link(dve.tensor_tensor(zs[:, low, :], odd, zs[:, high, :], ALU.add))
                    if 2 * i < nt:
                        ins = dve.tensor_tensor(zs[:, high, :], zs[:, high, :], odd, ALU.subtract)
                    else:
                        ins = dve.tensor_tensor(zs[:, high, :], odd, zs[:, high, :], ALU.subtract)
                    ins.then_inc(hy_comb, 1)
                    dve.wait_ge(hy_comb, HPR(run) + i + 1)
                u, v, ku, kv = zs[0:1, nt, :], zs[0:1, nt + lt, :], ks[0:1, nt, :], ks[0:1, nt + lt, :]
                mid = [at(HV + 512 * p, 512)[0:1, :] for p in range(2)]
                a, b = t1[0:1, :], t2[0:1, :]
                dve.tensor_tensor(a, u, kv, ALU.mult)
                link(dve.tensor_tensor(b, v, ku, ALU.mult))
                link(dve.scalar_tensor_tensor(mid[0], a, -1.0, b, ALU.mult, ALU.subtract))
                if is_c:
                    ride(0)
                dve.tensor_tensor(a, u, ku, ALU.mult)
                link(dve.tensor_tensor(b, v, kv, ALU.mult))
                link(dve.tensor_tensor(mid[1], a, b, ALU.subtract))
                if is_c:
                    ride(1)
                for j in range(0, nt, lt):
                    zc, zn, kc, kn = zs[:, j, :], zs[:, nt + j, :], ks[:, j, :], ks[:, nt + j, :]
                    dve.tensor_tensor(t1, zn, kn, ALU.mult)
                    link(dve.tensor_tensor(t2, zn, kc, ALU.mult))
                    link(dve.tensor_tensor(zn, zc, kn, ALU.mult))
                    if is_c or j:
                        ride((2 * j + 2) if is_c else 0)
                    dve.tensor_tensor(zn, zn, t2, ALU.add)
                    link(dve.tensor_tensor(zc, zc, kc, ALU.mult))
                    link(dve.memset(t1[0:1, :], 0.0))
                    link(dve.tensor_tensor(zc, zc, t1, ALU.subtract))
                    if is_c or j:
                        ride((2 * j + 3) if is_c else 1)
                for count, i in enumerate((0, 2, 1, 3) if nt == 4 else (0, 1)):
                    low, high = spectrum_pair(nt, i)
                    if count == 2:
                        dve.wait_ge(hy_pool, 12 * (L + 1))
                    ops = (ALU.add, ALU.subtract) if 2 * i < nt else (ALU.subtract, ALU.add)
                    link(dve.tensor_tensor(ks[:, low, :], zs[:, low, :], zs[:, high, :], ops[0]))
                    ins = dve.tensor_tensor(zs[:, high, :], zs[:, low, :], zs[:, high, :], ops[1])
                    if 2 * i == nt:
                        link(ins)
                        link(dve.tensor_copy(ks[0:1, low, :], mid[0]))
                        ins = dve.tensor_copy(zs[0:1, high, :], mid[1])
                    ins.then_inc(hy_prod, 1)
                    ride((6 if is_c else 2) + count)
                if not is_c:
                    wait_tile(dve, L, "gd", 3)
                    wait_tile(dve, L, "gd", 2)
                x0, z = at(HX0, 4, T), at(HZ, 4, T)
                for cc in range(4):
                    dve.wait_ge(hy_inv, 4 * run + cc + 1)
                    zz, xx, yy = z[:, cc, c0:c0 + n], x0[:, cc, c0:c0 + n], y["D"][:, cc, c0:c0 + n]
                    by_parity = zz.rearrange("f (r p) -> f p r", p=2)
                    dve.scalar_tensor_tensor(by_parity, by_parity, par[:, P_FB + cc:P_FB + cc + 1],
                                             pf[:, 512 * (4 + cc % 2):512 * (4 + cc % 2) + n].rearrange("f (p r) -> f p r", p=2),
                                             ALU.mult, ALU.add)\
                        .then_inc(hy_out, 1)
                    dve.wait_ge(hy_out, 4 * run + cc + 1)
                    link(dve.tensor_tensor(yy, yy, xx, ALU.mult))
                    link(dve.tensor_tensor(yy, yy, zz, ALU.mult))

            def gla_z(L, hp, d):
                dve.wait_ge(gl_alpha, 4 * L + 2 * hp + d + 1)
                dve.tensor_scalar(at(GL + 1536 * d, T), pf[:, 2048:2048 + T],
                                  par[:, P_BA + 2 * d + hp:P_BA + 2 * d + hp + 1], None, ALU.add).then_inc(gl_z, 1)

            def gla_cum(L, hp, d):
                N = 2 * L + hp
                zb, lb = at(GL + 1536 * d, T), at(GL + 1536 * d + T, T)
                dve.wait_ge(gl_ln, 6 * N + d + 5)
                link(dve.scalar_tensor_tensor(zb, zb, 0.0, lb, ALU.min, ALU.subtract))
                if d == 0:
                    dve.tensor_tensor_scan(lb, cmask[:, 0, :], zb, 0.0, ALU.mult, ALU.add).then_inc(gl_cum, 1)
                else:
                    dve.tensor_tensor_scan(lb[:, ::-1], cmask[:, 1, ::-1], zb[:, ::-1], 0.0, ALU.mult, ALU.add)\
                        .then_inc(gl_cum, 1)
                dve.wait_ge(gl_cum, 2 * N + d + 1)
                l3 = lb.rearrange("p (n c) -> p n c", c=64)
                end = l3[:, :, 63:64] if d == 0 else l3[:, :, 0:1]
                dve.tensor_tensor(zb.rearrange("p (n c) -> p n c", c=64), end.to_broadcast([128, 12, 64]), l3,
                                  ALU.subtract).then_inc(gl_rest, 1)

            def gla_rest_keys(L, hp, d):
                e2 = at(GE, 2, 3, T)[:, d, 2, :]
                dve.wait_ge(gl_exp2, 4 * L + 2 * hp + d + 1)
                dve.tensor_tensor(e2, e2, at(GK, 2, T)[:, hp, :], ALU.mult).then_inc(gl_ke, 1)

            def gla_queries(L, hp, d):
                oc = width(L, False)
                E = at(GE, 2, 3, T)
                dve.wait_ge(gl_exp, 4 * L + 2 * hp + d + 1)
                e3 = E[:, d, 0, :].rearrange("p (n c) -> p n c", c=64)
                dve.tensor_tensor(E[:, d, 1, :], E[:, d, 1, :], at(GK, 2, T)[:, hp, :], ALU.mult)
                link(dve.tensor_copy(gend[:, d, :], e3[:, :, 63 if d == 0 else 0]))
                dve.tensor_tensor(E[:, d, 0, 0:oc], E[:, d, 0, 0:oc], at(GQ, 2, T)[:, hp, 0:oc], ALU.mult).then_inc(gl_qk, 1)

            def gla_mean(L, hp, e):
                oc, base = width(L, False), 2048 + 1024 * e
                dve.wait_ge(gl_ss, 4 * L + 2 * hp + e + 1)
                dve.tensor_scalar(at(GSQ[e], T)[:, 0:oc], pf[:, base:base + oc], 1.0 / 128, EPS, ALU.mult, ALU.add)\
                    .then_inc(gl_rd, 1)

            def gla_inverse(L, hp, e):
                r = at(GSQ[e], T)[:, 0:width(L, False)]
                dve.wait_ge(gl_rd, 4 * L + 2 * hp + e + 1)
                dve.reciprocal(r, r).then_inc(gl_ms, 1)

            def gla_finish(L, hp, e):
                oc, n = width(L, False), 4 * L + 2 * hp + e + 1
                r, o, yy = at(GSQ[e], T)[:, 0:oc], at(GO[e], T)[:, 0:oc], y["C"][:, 2 * hp + e, 0:oc]
                dve.wait_ge(gl_rt, n)
                link(dve.scalar_tensor_tensor(o, o, par[:, P_GN:P_GN + 1], r, ALU.mult, ALU.mult))
                dve.tensor_tensor(yy, yy, o, ALU.mult).then_inc(gl_fin, 1)

            def gla(L):
                oc = width(L, False)
                S = at(GS, 2, 12, 128)
                A = at(GAT, 2, 2, T)
                wait_tile(dve, L, "gg", 3)
                wait_tile(dve, L, "gg", 2)
                for hp in range(2):
                    N = 2 * L + hp
                    if hp:
                        gla_queries(L, 1, 0)
                        gla_queries(L, 1, 1)
                    for d in range(2):
                        dve.wait_ge(gl_kv, 2 * N + d + 1)
                        base = 2048 if d == 0 else 0
                        for s in range(11):
                            n = chunk_at(d, s)
                            kv = pf[:, base + 1024 * (n % 2) + 128 * (n // 2):base + 1024 * (n % 2) + 128 * (n // 2) + 128]
                            ins = dve.scalar_tensor_tensor(S[:, d, s + 1, :], S[:, d, s, :], gend[:, d, n:n + 1], kv,
                                                           ALU.mult, ALU.add)
                            if s < 10:
                                link(ins)
                        ins.then_inc(gl_state, 1)
                    for e in range(2):
                        for d in range(2):
                            dve.wait_ge(gl_at, 4 * N + 2 * e + d + 1)
                            base = (2048 if e == 0 else 0) + 1024 * d
                            dve.copy_predicated(A[:, e, d, 0:oc].rearrange("p (t i) -> p t i", i=128),
                                                umask[:, d:d + 1, :].to_broadcast([128, oc // 128, 128]),
                                                pf[:, base:base + oc].rearrange("p (t i) -> p t i", i=128)).then_inc(gl_atc, 1)
                    if hp == 0:
                        gla_cum(L, 1, 0)
                        gla_cum(L, 1, 1)
                        for d in range(2):
                            gla_rest_keys(L, 1, d)
                        for e in range(2):
                            gla_mean(L, 0, e)
                    else:
                        for e in range(2):
                            gla_inverse(L, 0, e)
                        for e in range(2):
                            gla_finish(L, 0, e)

            def rotary(L, i):
                cs = at(BROPE, 2, 512)
                t = at(BTMP, 512)
                if i == 0:
                    dve.wait_ge(rope_in, 16 * (L + 1))
                x = at(BQ, 4, T)[:, i - 1, 0:SEQ] if i else at(BK, T)[:, 0:SEQ]
                dve.wait_ge(rope_rot, 5 * L + i + 1)
                dve.tensor_tensor(t, pf[:, 512 * (4 + i % 2):512 * (5 + i % 2)], cs[:, 1, :], ALU.mult)
                link(dve.tensor_tensor(x, x, cs[:, 0, :], ALU.mult))
                dve.tensor_tensor(x, x, t, ALU.add).then_inc(rope_done, 1)
                dve.wait_ge(rope_done, 5 * L + i + 1)

            def attention(L, mixer):
                A = mixer == "A"
                us = units(mixer, L)
                u0 = unit0[L, mixer]
                pt_at = APT if A else BTMP + 1280
                o_at = AO if A else BTMP + 2560

                def maxima(n):
                    q, i, p = us[n]
                    hh = head(mixer, i, p)
                    w = 128 * len(key_blocks(mixer, q))
                    s = pf[:, 1024 * p:1024 * p + w]
                    dve.wait_ge(at_s, u0 + n + 1)
                    if A and q < 4:
                        if i == 0 and p == 0:
                            dve.wait_ge(bias_in[q % 2], 16 * (2 * L + q // 2 + 1))
                        dve.tensor_reduce(rmx[:, 0:1], s[:, 256:512], AX, ALU.max)
                        link(dve.tensor_tensor_reduce(s[:, 0:256], s[:, 0:256], at(ABIAS + 2048 * (q % 2), 8, 256)[:, hh, :],
                                                      1.0, -3e38, ALU.add, ALU.max, rmx[:, 1:2]))
                        m1 = rmx[:, 1:2]
                    else:
                        link(dve.tensor_reduce(rmx[:, 0:1], s, AX, ALU.max))
                        m1 = par[:, P_SINK + hh:P_SINK + hh + 1] if not A else rmx[:, 0:1]
                    dve.tensor_scalar(stat[:, q % 2, 0, hh:hh + 1], rmx[:, 0:1], m1, -1.0, ALU.max, ALU.mult).then_inc(at_max, 1)
                    dve.wait_ge(at_max, u0 + n + 1)

                def copies(n):
                    q, i, p = us[n]
                    nb = len(key_blocks(mixer, q))
                    dve.wait_ge(at_pt, u0 + n + 1)
                    if n >= 2:
                        dve.wait_ge(at_o, u0 + n - 1)
                    PT = at(pt_at + 640 * p, 640)
                    w = 128 * min(nb, 4)
                    ins = dve.tensor_copy(PT[:, 0:w], pf[:, 2048 + 512 * p:2048 + 512 * p + w])
                    if nb == 5:
                        ins = dve.tensor_copy(PT[:, 512:640], pf[:, 3072:3200])
                    ins.then_inc(at_ptc[0], 1)

                def finish(q, n):
                    st = stat[:, q % 2, :, :]
                    if not A:
                        dve.tensor_tensor(st[:, 3, :], par[:, P_SINK:P_SINK + 8], st[:, 0, :], ALU.add).then_inc(at_sum, 1)
                        dve.wait_ge(at_sink, QB(L) + q + 1)
                        dve.wait_ge(at_p, u0 + n + 2)
                        link(dve.tensor_tensor(st[:, 1, :], st[:, 1, :], st[:, 3, :], ALU.add))
                    dve.wait_ge(at_p, u0 + n + 2)
                    link(dve.reciprocal(st[:, 2, :], st[:, 1, :]))
                    dve.wait_ge(at_o, u0 + n + 2)
                    o = at(o_at, 8, 64)
                    dve.tensor_tensor(o, pf[:, 3584:4096].rearrange("p (h d) -> p h d", d=64),
                                      st[:, 2, :].unsqueeze(2).to_broadcast([128, 8, 64]), ALU.mult).then_inc(at_on, 1)

                def gate(q):
                    dve.wait_ge(at_ot, qt0[L, mixer] + q + 1)
                    turned = pf[:, 3072:3584].rearrange("p (f t) -> p f t", f=4)
                    if A and q < 4:
                        yy = y[mixer][:, :, 0:SEQ].rearrange("p f (r c) -> p f r c", c=GRID_W)[:, :, :, NKC * q:NKC * q + NKC]
                        turned = turned.rearrange("p f (r c) -> p f r c", c=NKC)
                        for f in range(4):
                            ins = dve.tensor_tensor(yy[:, f], yy[:, f], turned[:, f], ALU.mult)
                    else:
                        yy = y[mixer][:, :, 128 * q:128 * q + 128]
                        ins = dve.tensor_tensor(yy, yy, turned, ALU.mult)
                    ins.then_inc(at_y, 1)

                maxima(0)
                maxima(1)
                project(L, mixer, [len(TILES[mixer]) - 1])
                for n in range(0, len(us), 2):
                    q = us[n][0]
                    copies(n)
                    if n + 2 < len(us):
                        maxima(n + 2)
                        maxima(n + 3)
                    if n % 8 == 0 and q:
                        gate(q - 1)
                    if n % 8 == 6:
                        finish(q, n)
                gate(us[-1][0])

            def merge(L):
                w = width(L, False)
                last = L == DEPTH - 1
                acc = at(MACC, KT, T)
                g0, s0 = POS["gate", L, 0, 0], SPLIT_NO["gate", L, 0, 0]
                with dve.Fori(0, KT // 2) as it:
                    for v in range(8):
                        prod = at(MPROD[v % 2], T)[:, 0:w]
                        dst = ar[:, bass.ds(it * (2 * T) + (MACC + T * (v // 4)), w)]
                        dve.wait_ge(mg_gate, 8 * it + (MG(L) + v + 1))
                        src = pf[:, 2048 * (v % 2) + 1024:2048 * (v % 2) + 1024 + w]
                        gate = at(MGATE + T * (v % 2), T)[:, 0:w]
                        if v % 4 == 0:
                            dve.tensor_tensor(dst, gate, src, ALU.mult).then_inc(mg_prod, 1)
                        else:
                            dve.tensor_tensor(prod, gate, src, ALU.mult).then_inc(mg_prod, 1)
                            dve.wait_ge(mg_prod, 8 * it + (MG(L) + v + 3))
                            dve.tensor_tensor(dst, dst, prod, ALU.add).then_inc(mg_sum, 1)
                            dve.wait_ge(mg_sum, 6 * it + (3 * KT * L + v - v // 4))
                        n = g0 + gate_place(v + 2)
                        dve.wait_ge(split_hi, 8 * it + (s0 + v + 3))
                        dve.tensor_tensor(w_lo[:, (s0 + v) % 2], slot_tile[:, n % SLOTS], w_hi[:, (s0 + v) % 2].bitcast(F32),
                                          ALU.subtract).then_inc(ring_read[n % SLOTS], 1)
                for k in range(KT):
                    dve.wait_ge(h_high, KT * (2 * L + 1) + k + 1)
                    dve.tensor_tensor(h_lo[:, k, 0:w], acc[:, k, 0:w], h_hi[:, k, 0:w].bitcast(F32), ALU.subtract)\
                        .then_inc(h_ready, 1)
                x = at(X_AT, KT, T)
                dve.wait_ge(x_in, 16 * (L + 2))
                for m in range(KT):
                    t = tile_no[L, "out", m]
                    if next_split(("proj", L, "out", m)) is not None:
                        low_part(next_split(("proj", L, "out", m)))
                    dve.wait_ge(tile_ready, t + 1)
                    for c, (c0, c1) in enumerate(((0, SEQ), (SEQ, w))):
                        if c1 > c0:
                            ins = dve.scalar_tensor_tensor(x[:, m, c0:c1], pf[:, pair(t) + c0:pair(t) + c1],
                                                           mod[:, L, 2 * KT + m, c:c + 1], x[:, m, c0:c1], ALU.mult, ALU.add)
                    ins.then_inc(drained[t % 2], 1)
                    if m >= 2:
                        add_square(L + 1, m - 1)
                add_square(L + 1, KT - 1)

            for i in range(2):
                dve.memset(rmx[:, 2 + i:3 + i], 0.0).then_inc(mg_prod, 1)
            dve.wait_ge(par_first, 16)
            for step in range(filter_steps(4)):
                filter_step(HYN[False], 0, step)
                mod_products(*MOD_AT["start"][step])
                if step > 8:
                    add_square(0, step - 8)
            barrier(dve, PH(0, "filter"))
            for L in range(DEPTH):
                if L:
                    dve.wait_ge(par_in, 16 * L)
                norm(L, at(X_AT, KT, T))
                if L == 0:
                    dve.wait_ge(mask_in, 16 * 5)
                project(L, "D", range(16))
                hyena(2 * L)
                if L == DEPTH - 1:
                    early_parts(dve, L, low_part)
                else:
                    barrier(dve, PH(L, "D"))
                if L < DEPTH - 1:
                    for step in range(filter_steps(2)):
                        filter_step(HYN[True], 1, step)
                        if step < len(FILTER_MODS):
                            mod_products(*FILTER_MODS[step])
                    hyena(2 * L + 1)
                    modulation("Dc")
                    add_bias(0, 2 * KT, MOD_TILES)
                    early_parts(dve, L, low_part)
                project(L, "C", range(13))
                gla(L)
                project(L, "A", range(15))
                attention(L, "A")
                project(L, "B", range(9))
                attention(L, "B")
                merge(L)
            r = at(MGATE, SEQ)
            dve.wait_ge(norm_ps, DEPTH + 1)
            link(dve.tensor_scalar(r, pf[:, NORM_COL:NORM_COL + SEQ], 1.0 / D_MODEL, EPS, ALU.mult, ALU.add))
            dve.reciprocal(r, r).then_inc(norm_ms, 1)
            dve.wait_ge(norm_rt, DEPTH + 1)
            for k in range(KT):
                dve.scalar_tensor_tensor(at(MACC, KT, T)[:, k, 0:SEQ], at(X_AT, KT, T)[:, k, 0:SEQ], par[:, P_FIN + k:P_FIN + k + 1], r,
                                         ALU.mult, ALU.mult).then_inc(res_done, 1)


def weight_stream(w_mod, w_in, w_branch, w_out):
    def tile(w, c0, n=128):
        t = np.zeros((128, KT, 128), np.float32)
        t[:, :, :n] = w[:, c0:c0 + n].reshape(KT, 128, n).transpose(1, 0, 2)
        return t

    start = {(ti[0], ti[1]): ti[2] for b in MIXERS for ti in TILES[b]}

    def weights(kind, L, a, b=None):
        if kind == "mod":
            return tile(w_mod[L], 128 * a)
        if kind == "gate":
            return tile(w_in[L], GM + D_MODEL * b + 128 * a)
        if kind == "branch":
            br = w_branch[L][2 * b:2 * b + 2, :, 128 * a:128 * a + 128].reshape(2, 4, 128, 128)
            return br.transpose(2, 0, 1, 3)
        if a == "out":
            return tile(w_out[L], 128 * b)
        c0 = start[a, b]
        if a == "lr":
            return tile(w_in[L], c0, 32)
        if a == "qb":
            t = tile(w_in[L], c0 + HD * b)
            t[:, :, HD:] = tile(w_in[L], c0 + HD * (b + 4))[:, :, :HD]
            return t
        return tile(w_in[L], c0)

    return np.stack([weights(*key).reshape(128, WTILE) for key in ORDER])


def columns(v):
    return np.asarray(v).reshape(-1, 128).T


def parameter_table(L, a):
    t = np.zeros((128, P_W), np.float32)
    t[:, P_NORM:P_NORM + 8] = columns(a["norm_w"][L])
    t[:, P_BMOD:P_BMOD + 24] = columns(a["b_mod"][L])
    t[:, P_CW:P_CW + 36] = columns(a["conv_w"][L])
    t[:, P_CB:P_CB + 12] = columns(a["conv_b"][L])
    t[:, P_FB:P_FB + 4] = columns(a["filt_bias"][L])
    t[:, P_BA:P_BA + 4] = columns(a["b_alpha"][L])
    t[:, P_GN] = a["gla_norm_w"][L]
    for col, name in ((P_FREQ, "filt_freq"), (P_B1, "filt_b1"), (P_B2, "filt_b2"), (P_B3, "filt_b3")):
        t[:64, col] = a[name][L]
    t[:, P_SINK:P_SINK + 8] = a["sink"][L]
    t[:, P_FIN:P_FIN + 8] = columns(a["final_norm_w"])
    t[:, P_C:P_C + 16:2] = columns(a["c"])
    t[:, P_C + 1:P_C + 16:2] = columns(a["c_ctx"])
    return t


def natten_bias(rpb):
    r, c, rk, ck = np.ogrid[0:8, 0:NKC, 0:8, 0:2 * NKC]
    out = np.empty((4, 128, HEADS, 256), np.float32)
    for j, c0 in enumerate(NATTEN_COL0):
        col, kcol = NKC * j + c, c0 + ck
        first = np.clip(col - NKC // 2, 0, GRID_W - NKC)
        seen = np.broadcast_to((kcol >= first) & (kcol < first + NKC), (8, NKC, 8, 2 * NKC))
        dr = np.broadcast_to(rk - r + NKR - 1, seen.shape)
        dc = np.broadcast_to(np.clip(kcol - col + NKC - 1, 0, 2 * NKC - 2), seen.shape)
        v = np.where(seen, rpb[:, dr, dc], np.float32(NEG))
        out[j] = v.reshape(HEADS, 128, 256).transpose(1, 0, 2)
    return out


def filter_constants(n):
    f32 = np.float32
    t = np.linspace(0.0, 1.0, n, dtype=f32)
    ang = (f32(2.0 * math.pi) * np.arange(n, dtype=f32) / f32(n)).astype(f32)
    f = np.linspace(1e-4, 15, 16, dtype=f32)
    fa = (f[:, None] * ang[None, :]).astype(f32).astype(np.float64)
    z = np.concatenate([t[None, :], np.cos(fa), -np.sin(fa)], 0).astype(f32)
    deltas = np.abs(np.linspace(math.log(1e-2) / 1.5, math.log(1e-2) / 0.3, 512, dtype=f32))
    decay = np.exp((-t[:, None] * deltas[None, :]).astype(np.float64)).astype(f32)
    return z, decay


def transforms(n):
    w, t = np.arange(n // 2)[:, None], np.concatenate([np.arange(0, n, 2), np.arange(1, n, 2)])[None, :]
    ang = 2.0 * np.pi * ((w * t) % (2 * n)) / (2 * n)
    c, s = np.cos(ang), np.sin(ang)
    mid = 2.0 * np.pi * (t[0] % 4) / 4
    s[0] = np.where(t[0] % 2 == 0, np.cos(mid), np.sin(mid))
    fwd = np.concatenate([c, s], 0).T
    c, s = c / n, s / n
    c[0] /= 2
    s[0] /= 2
    back = np.concatenate([m[:, half] for half in (slice(0, n // 2), slice(n // 2, n)) for m in (c, s)], 0)

    def rows(m):
        return m.reshape(-1, 128, m.shape[1]).transpose(1, 0, 2).astype(np.float32)
    return rows(fwd), rows(back)


def parity_order(v, axis):
    return np.concatenate([v.take(range(p, v.shape[axis], 2), axis) for p in range(2)], axis)


def kernel(**inputs):
    import concourse.bacc as bacc
    import ml_dtypes
    from concourse.bass_utils import run_bass_kernel_spmd

    a = {k: np.asarray(v) for k, v in inputs.items()}
    z_l, dec_l = filter_constants(SEQ)
    z_c, dec_c = filter_constants(CTX)
    dft, idft = transforms(SEQ)
    dft_c, idft_c = transforms(CTX)
    eye = np.eye(128, dtype=np.float32)
    sign = ((-1.0) ** np.arange(128)).astype(np.float32)
    i = np.arange(128)
    left = np.where(i[None, :] >= i[:, None], 0.0, NEG)
    right = np.where(i[None, :] <= i[:, None], 0.0, NEG)
    tt = np.arange(T)
    starts = np.broadcast_to((tt % 64 != 0).astype(np.float32), (128, T))
    ends = np.broadcast_to((tt % 64 != 63).astype(np.float32), (128, T))
    same = i[:, None] // 64 == i[None, :] // 64
    pos = np.arange(SEQ)
    inv = (np.float32(10000.0) ** (-np.arange(16, dtype=np.float32) / 16)).astype(np.float32)
    ang = np.concatenate([(pos // GRID_W)[:, None] * inv, (pos % GRID_W)[:, None] * inv], 1).astype(np.float32)
    ang = np.tile(ang.T.astype(np.float64), (4, 1))
    rot = np.zeros((128, 128), np.float32)
    for b in (0, 64):
        for d in range(32):
            rot[b + 32 + d, b + d] = -1.0
            rot[b + d, b + 32 + d] = 1.0
    fw = np.zeros((DEPTH, 64, 192), np.float32)
    fw[:, :33, 0:64], fw[:, :, 64:128], fw[:, :, 128:192] = a["filt_w1"], a["filt_w2"], a["filt_w3"]
    alpha = np.zeros((DEPTH, 32, 512), np.float32)
    alpha[:, 0:16, 0:256], alpha[:, 16:32, 256:512] = a["w_alpha_up"][:, 0], a["w_alpha_up"][:, 1]
    xT = np.concatenate([a["x"][0], a["ctx"][0]], 0).T.reshape(KT, 128, T).transpose(1, 0, 2)
    arrays = {
        "wstream": weight_stream(a["w_mod"], a["w_in"], a["w_branch"], a["w_out"]),
        "xT": xT,
        "params": np.stack([parameter_table(L, a) for L in range(DEPTH)]),
        "zembT": np.concatenate([parity_order(z_l, 1), parity_order(z_c, 1)], 1),
        "filt_w": fw,
        "filt_wout": a["filt_wout"],
        "decay": np.concatenate([parity_order(dec_l, 0), parity_order(dec_c, 0)], 0).reshape(6, 128, 512).transpose(1, 0, 2),
        "dft": dft, "dft_c": dft_c, "idft": idft, "idft_c": idft_c,
        "bias": np.stack([natten_bias(a["rpb"][L]) for L in range(DEPTH)]),
        "rope": np.stack([np.cos(ang), np.sin(ang)], 1).astype(np.float32),
        "rot": rot,
        "alpha_w": alpha,
        "masks_f": np.concatenate([np.ones((128, 128), np.float32), eye, sign[:, None]], 1),
        "masks_b": np.concatenate([eye, left, right, starts, ends], 1).astype(ml_dtypes.bfloat16),
        "masks_u": np.concatenate([same & (i[:, None] <= i[None, :]), same & (i[:, None] >= i[None, :])], 1).astype(np.int32),
    }
    nc = bacc.Bacc("TRN2", target_bir_lowering=False, num_devices=1)
    sent, args = {}, []
    for name, v in arrays.items():
        v = np.ascontiguousarray(v)
        sent[f"in_{name}"] = v
        args.append(nc.dram_tensor(f"in_{name}", v.shape, mybir.dt.from_np(v.dtype), kind="ExternalInput").ap())
    args.append(nc.dram_tensor("x_mid", [128, KT, T], F32, kind="Internal").ap())
    args.append(nc.dram_tensor("v_mid", [DEPTH, SEQ, 512], F32, kind="Internal").ap())
    args.append(nc.dram_tensor("outT", [D_MODEL, SEQ], F32, kind="ExternalOutput").ap())
    build(nc, *args)
    r = run_bass_kernel_spmd(nc, [sent], core_ids=[0])
    return np.ascontiguousarray(r.results[0]["outT"].T)[None]
```
